# Optimizing a Trainium2 kernel written in Bass

```python
import jax, jax.numpy as jnp
from jax import lax
import numpy as np

D_MODEL = 1024
BATCH = 1
SEQ = 512
DEPTH = 1
DEC_BATCH = 8
DEC_SEQ = 1
PAST_LEN = 2048
PAGE_SIZE = 128

ATT_HEADS = 8
ATT_HEAD_DIM = 64
ATT_WIDTH = ATT_HEADS * ATT_HEAD_DIM
MOBA_BLOCK = 256
MOBA_TOPK = 3
ATT_QUERY_CHUNK = 64
M_HEADS = 4
M_WIDTH = D_MODEL
M_V_DIM = M_WIDTH // M_HEADS
M_QK_DIM = M_V_DIM // 2
M_QK_WIDTH = M_HEADS * M_QK_DIM
M_CONV = 4
M_CHUNK = 64
NORM_EPS = 1e-6
NEG_SCORE = -1e30
COLUMN_WIDTHS = (ATT_WIDTH, ATT_WIDTH, ATT_WIDTH, ATT_WIDTH, 2 * M_QK_WIDTH, M_WIDTH, M_WIDTH, M_WIDTH,
                 2 * M_HEADS, D_MODEL, D_MODEL)

kernel_name = "moba_mlstm_gated_parallel_decoder_step"

F32 = jnp.float32

def rms_norm(x, g):
    xf = x.astype(F32)
    y = xf * lax.rsqrt(jnp.mean(xf * xf, axis=-1, keepdims=True) + NORM_EPS)
    return (y * g.astype(F32)).astype(x.dtype)

def split_columns(z):
    parts, start = [], 0
    for w in COLUMN_WIDTHS:
        parts.append(z[..., start:start + w])
        start += w
    return parts

def moba_rows(q, k_means, t, ksel):
    j = t // MOBA_BLOCK
    nb = k_means.shape[2]
    s = jnp.einsum('bhqd,bhnd->bhqn', q.astype(F32), k_means)
    past = jnp.arange(nb, dtype=jnp.int32)[None, :] < j[:, None]
    s = jnp.where(past, s, NEG_SCORE)
    _, idx = lax.top_k(s, ksel)
    own = jnp.broadcast_to(j[:, None], idx.shape[:-1] + (1,)).astype(idx.dtype)
    blocks = jnp.concatenate([idx, own], axis=-1)
    block_ok = jnp.concatenate([idx < j[:, None], jnp.ones(own.shape, bool)], axis=-1)
    pos = blocks[..., None] * MOBA_BLOCK + jnp.arange(MOBA_BLOCK, dtype=jnp.int32)
    valid = block_ok[..., None] & (pos <= t[:, None, None])
    shp = pos.shape[:3] + (-1,)
    return pos.reshape(shp), valid.reshape(shp)

def block_attend(q, k_rows, v_rows, valid):
    s = jnp.einsum('bhqd,bhqrd->bhqr', q, k_rows).astype(F32) * (ATT_HEAD_DIM ** -0.5)
    p = jax.nn.softmax(jnp.where(valid, s, NEG_SCORE), axis=-1)
    return jnp.einsum('bhqr,bhqrd->bhqd', p.astype(v_rows.dtype), v_rows)

def moba_prompt(q, k, v):
    B, S = q.shape[:2]
    qh, kh, vh = (t.transpose(0, 2, 1, 3) for t in (q, k, v))
    nb = -(-S // MOBA_BLOCK)
    pad = nb * MOBA_BLOCK - S
    k_means = jnp.pad(kh.astype(F32), ((0, 0), (0, 0), (0, pad), (0, 0)))
    k_means = k_means.reshape(B, ATT_HEADS, nb, MOBA_BLOCK, ATT_HEAD_DIM).sum(3) / MOBA_BLOCK
    ksel = min(MOBA_TOPK, max(nb - 1, 1))
    qc = ATT_QUERY_CHUNK if S % ATT_QUERY_CHUNK == 0 else S
    nqc = S // qc
    q_chunks = jnp.moveaxis(qh.reshape(B, ATT_HEADS, nqc, qc, ATT_HEAD_DIM), 2, 0)
    t_chunks = jnp.arange(S, dtype=jnp.int32).reshape(nqc, qc)
    gather = jax.vmap(jax.vmap(lambda src, idx: src[idx]))

    def body(inp):
        q_blk, t = inp
        pos, valid = moba_rows(q_blk, k_means, t, ksel)
        pos = jnp.clip(pos, 0, S - 1)
        return block_attend(q_blk, gather(kh, pos), gather(vh, pos), valid)

    out = lax.map(body, (q_chunks, t_chunks))
    out = jnp.moveaxis(out, 0, 2).reshape(B, ATT_HEADS, S, ATT_HEAD_DIM)
    return out.transpose(0, 2, 1, 3).reshape(B, S, ATT_WIDTH)

def rows_from_cache(pool, layer, new, page_table, pos):
    DB, Qn, H = new.shape[:3]
    P = page_table.shape[1] * PAGE_SIZE
    b_idx = jnp.arange(DB, dtype=jnp.int32)[:, None, None, None]
    h_idx = jnp.arange(H, dtype=jnp.int32)[None, :, None, None]
    pp = jnp.clip(pos, 0, P - 1)
    page = page_table[b_idx, pp // PAGE_SIZE]
    past = pool[layer, page, pp % PAGE_SIZE, h_idx]
    fresh = new[b_idx, jnp.clip(pos - P, 0, Qn - 1), h_idx]
    return jnp.where((pos < P)[..., None], past, fresh.astype(past.dtype))

def moba_sample(q, k, v, cache_k, cache_v, page_table, layer):
    DB, Qn = q.shape[:2]
    n_pages = page_table.shape[1]
    P = n_pages * PAGE_SIZE
    nb = -(-(P + Qn) // MOBA_BLOCK)
    ksel = min(MOBA_TOPK, max(nb - 1, 1))
    page_sums = cache_k[layer, page_table].astype(F32).sum(2)
    page_block = jnp.arange(n_pages, dtype=jnp.int32) * PAGE_SIZE // MOBA_BLOCK
    t = P + jnp.arange(Qn, dtype=jnp.int32)
    sums = (jax.ops.segment_sum(jnp.moveaxis(page_sums, 1, 0), page_block, num_segments=nb)
            + jax.ops.segment_sum(jnp.moveaxis(k.astype(F32), 1, 0), t // MOBA_BLOCK, num_segments=nb))
    k_means = jnp.transpose(sums / MOBA_BLOCK, (1, 2, 0, 3))
    qh = q.transpose(0, 2, 1, 3)
    pos, valid = moba_rows(qh, k_means, t, ksel)
    k_rows = rows_from_cache(cache_k, layer, k, page_table, pos)
    v_rows = rows_from_cache(cache_v, layer, v, page_table, pos)
    out = block_attend(qh, k_rows.astype(qh.dtype), v_rows, valid)
    return out.transpose(0, 2, 1, 3).reshape(DB, Qn, ATT_WIDTH).astype(q.dtype)

def mlstm_cell(q, k, v, i_pre, f_pre, C0, n0, m0):
    B, H, L = q.shape[:3]
    lc = M_CHUNK if L % M_CHUNK == 0 else L
    nc = L // lc

    def chunks(a):
        return jnp.moveaxis(a.reshape((B, H, nc, lc) + a.shape[3:]), 2, 0)

    causal = jnp.tril(jnp.ones((lc, lc), bool))
    logf = jax.nn.log_sigmoid(f_pre)

    def step(carry, inp):
        C, n, m = carry
        qc, kc, vc, ic, lfc = inp
        b = jnp.cumsum(lfc, axis=-1)
        d = jnp.where(causal, b[..., :, None] - b[..., None, :] + ic[..., None, :], -jnp.inf)
        inter = b + m[..., None]
        m_t = jnp.maximum(inter, d.max(-1))
        w = jnp.exp(d - m_t[..., None])
        a = jnp.exp(inter - m_t)
        s = jnp.einsum('bhtd,bhsd->bhts', qc, kc) * w
        num = a[..., None] * jnp.einsum('bhvd,bhtd->bhtv', C, qc) + jnp.einsum('bhts,bhsv->bhtv', s, vc)
        den = a * jnp.einsum('bhd,bhtd->bht', n, qc) + s.sum(-1)
        h = num / jnp.maximum(jnp.abs(den), jnp.exp(-m_t))[..., None]
        g = b[..., -1:] - b + ic
        m_new = jnp.maximum(b[..., -1] + m, g.max(-1))
        ws = jnp.exp(g - m_new[..., None])
        a_end = jnp.exp(b[..., -1] + m - m_new)
        C_new = a_end[..., None, None] * C + jnp.einsum('bhs,bhsv,bhsd->bhvd', ws, vc, kc)
        n_new = a_end[..., None] * n + jnp.einsum('bhs,bhsd->bhd', ws, kc)
        return (C_new, n_new, m_new), h

    (C, n, m), h = lax.scan(step, (C0, n0, m0),
                            (chunks(q), chunks(k), chunks(v), chunks(i_pre), chunks(logf)))
    h = jnp.moveaxis(h, 0, 2).reshape(B, H, L, M_V_DIM)
    return h, C, n, m

def mlstm_branch(qk_pre, v, o_pre, if_pre, conv_buf, C0, n0, m0, w_conv, b_conv, m_norm_g):
    B, L, ch = qk_pre.shape
    xp = jnp.concatenate([conv_buf.astype(qk_pre.dtype), qk_pre], axis=1)
    qk = lax.conv_general_dilated(xp, w_conv.astype(xp.dtype)[:, None, :], (1,), 'VALID',
                                  dimension_numbers=('NWC', 'WIO', 'NWC'), feature_group_count=ch)
    qk = jax.nn.silu(qk + b_conv.astype(qk.dtype))
    q, k = jnp.split(qk, 2, axis=-1)

    def to_heads(a, d):
        return a.reshape(B, L, M_HEADS, d).transpose(0, 2, 1, 3).astype(F32)

    qh = to_heads(q, M_QK_DIM)
    kh = to_heads(k, M_QK_DIM) * (M_QK_DIM ** -0.5)
    vh = to_heads(v, M_V_DIM)
    gates = if_pre.transpose(0, 2, 1)
    h, C, n, m = mlstm_cell(qh, kh, vh, gates[:, :M_HEADS], gates[:, M_HEADS:],
                            C0.astype(F32), n0.astype(F32), m0.astype(F32))
    h = h.transpose(0, 2, 1, 3)
    h = h * lax.rsqrt(jnp.mean(h * h, axis=-1, keepdims=True) + NORM_EPS)
    h = h * m_norm_g.astype(F32).reshape(M_HEADS, M_V_DIM)
    h = h.reshape(B, L, M_WIDTH) * jax.nn.sigmoid(o_pre.astype(F32))
    return h.astype(v.dtype), xp[:, -(M_CONV - 1):], C, n, m

def layer(x, c, attend, conv_buf, C0, n0, m0, w_ada, b_ada, norm_g, w_in, b_if, w_conv, b_conv,
          m_norm_g, w_att, w_mlstm, w_out):
    B, L, _ = x.shape
    mod = jax.nn.silu(c) @ w_ada + b_ada
    shift, scale, gate = jnp.split(mod, 3, axis=-1)
    h = rms_norm(x, norm_g) * (1 + scale[:, None]) + shift[:, None]
    aq, ak, av, az, mqk, mv, mo, mz, mif, ga, gm = split_columns(h @ w_in)

    def att_heads(a):
        return a.reshape(B, L, ATT_HEADS, ATT_HEAD_DIM)

    k_rows, v_rows = att_heads(ak), att_heads(av)
    ya = attend(att_heads(aq), k_rows, v_rows)
    ym, conv_new, C, n, m = mlstm_branch(mqk, mv, mo, mif.astype(F32) + b_if.astype(F32), conv_buf,
                                         C0, n0, m0, w_conv, b_conv, m_norm_g)
    ya = (ya * jax.nn.silu(az)) @ w_att
    ym = (ym * jax.nn.silu(mz)) @ w_mlstm
    u = jax.nn.sigmoid(ga) * ya + jax.nn.sigmoid(gm) * ym
    y = x + gate[:, None] * (u @ w_out)
    return y, k_rows, v_rows, C, n, m, conv_new

def setup_inputs(seed: int = 0) -> dict:
    key = jax.random.key(seed)
    ks = jax.random.split(key, 24)
    n_pages = PAST_LEN // PAGE_SIZE
    n_phys = (DEC_BATCH * n_pages * 5) // 4
    d_in = sum(COLUMN_WIDTHS)

    def nrm(k, shape, s=1.0):
        return s * jax.random.normal(k, shape, F32)

    page_table = jax.random.permutation(ks[0], n_phys)[:DEC_BATCH * n_pages]
    page_table = page_table.reshape(DEC_BATCH, n_pages).astype(jnp.int32)
    b_if = jnp.concatenate([nrm(ks[1], (DEPTH, M_HEADS), 0.1),
                            jnp.linspace(3.0, 6.0, M_HEADS, dtype=F32)[None] + nrm(ks[2], (DEPTH, M_HEADS), 0.1)],
                           axis=-1)
    return {
        "x_prompt": nrm(ks[3], (BATCH, SEQ, D_MODEL)),
        "x_sample": nrm(ks[4], (DEC_BATCH, DEC_SEQ, D_MODEL)),
        "cache_k": nrm(ks[5], (DEPTH, n_phys, PAGE_SIZE, ATT_HEADS, ATT_HEAD_DIM)),
        "cache_v": nrm(ks[6], (DEPTH, n_phys, PAGE_SIZE, ATT_HEADS, ATT_HEAD_DIM)),
        "state_C": nrm(ks[7], (DEPTH, DEC_BATCH, M_HEADS, M_V_DIM, M_QK_DIM)),
        "state_n": nrm(ks[8], (DEPTH, DEC_BATCH, M_HEADS, M_QK_DIM)),
        "state_m": nrm(ks[9], (DEPTH, DEC_BATCH, M_HEADS), 0.5),
        "state_conv": nrm(ks[10], (DEPTH, DEC_BATCH, M_CONV - 1, 2 * M_QK_WIDTH)),
        "page_table": page_table,
        "c_prompt": nrm(ks[11], (BATCH, D_MODEL)),
        "c_sample": nrm(ks[12], (DEC_BATCH, D_MODEL)),
        "w_ada": nrm(ks[13], (DEPTH, D_MODEL, 3 * D_MODEL), 0.5 * D_MODEL ** -0.5),
        "b_ada": nrm(ks[14], (DEPTH, 3 * D_MODEL), 0.02),
        "norm_g": 1.0 + nrm(ks[15], (DEPTH, D_MODEL), 0.05),
        "w_in": nrm(ks[16], (DEPTH, D_MODEL, d_in), D_MODEL ** -0.5),
        "b_if": b_if,
        "w_conv": nrm(ks[17], (DEPTH, M_CONV, 2 * M_QK_WIDTH), M_CONV ** -0.5),
        "b_conv": nrm(ks[18], (DEPTH, 2 * M_QK_WIDTH), 0.02),
        "m_norm_g": 1.0 + nrm(ks[19], (DEPTH, M_WIDTH), 0.05),
        "w_att": nrm(ks[20], (DEPTH, ATT_WIDTH, D_MODEL), ATT_WIDTH ** -0.5),
        "w_mlstm": nrm(ks[21], (DEPTH, M_WIDTH, D_MODEL), M_WIDTH ** -0.5),
        "w_out": nrm(ks[22], (DEPTH, D_MODEL, D_MODEL), D_MODEL ** -0.5),
        "final_g": 1.0 + nrm(ks[23], (D_MODEL,), 0.05),
    }

def reference(x_prompt, x_sample, cache_k, cache_v, state_C, state_n, state_m, state_conv, page_table,
              c_prompt, c_sample, w_ada, b_ada, norm_g, w_in, b_if, w_conv, b_conv, m_norm_g,
              w_att, w_mlstm, w_out, final_g):
    B = x_prompt.shape[0]
    xp, xs = x_prompt, x_sample
    outs_p, outs_s = [], []
    for l in range(DEPTH):
        w = (w_ada[l], b_ada[l], norm_g[l], w_in[l], b_if[l], w_conv[l], b_conv[l], m_norm_g[l],
             w_att[l], w_mlstm[l], w_out[l])
        conv0 = jnp.zeros((B, M_CONV - 1, 2 * M_QK_WIDTH), xp.dtype)
        C0 = jnp.zeros((B, M_HEADS, M_V_DIM, M_QK_DIM), F32)
        n0 = jnp.zeros((B, M_HEADS, M_QK_DIM), F32)
        m0 = jnp.zeros((B, M_HEADS), F32)
        xp, *st_p = layer(xp, c_prompt, moba_prompt, conv0, C0, n0, m0, *w)
        attend_s = lambda q, k, v, l=l: moba_sample(q, k, v, cache_k, cache_v, page_table, l)
        xs, *st_s = layer(xs, c_sample, attend_s, state_conv[l], state_C[l], state_n[l], state_m[l], *w)
        outs_p.append(st_p)
        outs_s.append(st_s)
    k_p, v_p, C_p, n_p, m_p, conv_p = [jnp.stack([o[i] for o in outs_p]) for i in range(6)]
    k_s, v_s, C_s, n_s, m_s, conv_s = [jnp.stack([o[i] for o in outs_s]) for i in range(6)]
    y_prompt = rms_norm(xp, final_g)
    y_sample = rms_norm(xs, final_g)
    return (y_prompt, y_sample, k_p, v_p, C_p, n_p, m_p, conv_p, k_s, v_s, C_s, n_s, m_s, conv_s)


_drawn_inputs = setup_inputs


def setup_inputs(seed=0):
    import zlib

    import numpy as np

    out = dict(_drawn_inputs(seed))
    spreads = {}
    factors = {'cache_k': 8.0, 'cache_v': 8.0, 'm_norm_g': 8.0}
    for name, (base, spread) in spreads.items():
        noise = np.random.default_rng([zlib.crc32(name.encode()), seed]).standard_normal(out[name].shape)
        drawn = base * np.exp(spread * noise) if base else spread * noise
        out[name] = __import__('jax').numpy.asarray(drawn.astype(out[name].dtype))
    for name, factor in factors.items():
        out[name] = (out[name] * factor).astype(out[name].dtype)
    return out
```

```python
from contextlib import ExitStack

import concourse.bass as bass
from concourse import mybir

ALU = mybir.AluOpType
ACT = mybir.ActivationFunctionType
F32 = mybir.dt.float32
F32R = mybir.dt.float32r
I32 = mybir.dt.int32
AX = mybir.AxisListType.X

P = 128
D = 1024
KT = D // P
T = 512
TT = T // P
B = 8
NT = T + B
HALF = NT // 2
AH, DH = 8, 64
AW = AH * DH
PAIRS = AW // P
MH, MQ, MV = 4, 128, 256
PAGE, PAGES = 128, 16
NBLK = 8
TOPK = 3
EPS = 1e-6
NEG = -1e30
SCALE = DH ** -0.5
KSCALE = MQ ** -0.5

CQ, CK, CV, CZ = 0, 512, 1024, 1536
CMQK, CMV, CMO, CMZ = 2048, 3072, 4096, 5120
CIF, CGA, CGM = 6144, 6152, 7176

T_ATT, T_ML = 0, 16
T_GATE = T_ML + 32
T_COMB = T_GATE + 16
T_OUT = T_COMB + 16
T_ALL = T_OUT + 8

STEP_PAGES = 4
KV_SLOTS = 2
V_G, V_MG, V_BC, V_WC, V_BA = 0, 8, 16, 24, 56
V_ROWS = V_BA + 24


class Chain:

    def __init__(self, eng, sem):
        self.eng, self.sem, self.base, self.k = eng, sem, 0, 0

    def __call__(self, ins):
        ins.then_inc(self.sem, 1)
        self.k += 1
        self.eng.wait_ge(self.sem, self.base + self.k)

    def loop(self, i, per):
        self.start = self.base + self.k
        self.base, self.k, self.per = self.start + i * per, 0, per

    def end(self, trips):
        assert self.k == self.per, (self.k, self.per)
        self.base, self.k = self.start + trips * self.per, 0


def decoder_step(nc, I, O):
    x_p = I["x_prompt"].rearrange("b s d -> (b s) d")
    x_s = I["x_sample"].rearrange("b s d -> (b s) d")
    w_in = I["w_in"][0].rearrange("(k p) n -> p k n", p=P)
    w_ada = I["w_ada"][0].rearrange("(k p) n -> p k n", p=P)
    w_att = I["w_att"][0].rearrange("(k p) n -> p k n", p=P)
    w_ml = I["w_mlstm"][0].rearrange("(k p) n -> p k n", p=P)
    w_out = I["w_out"][0].rearrange("(k p) n -> p k n", p=P)
    pages_k = I["cache_k"][0].rearrange("n t h d -> t n (h d)")
    pages_v = I["cache_v"][0].rearrange("n t h d -> t n (h d)")
    state_c = I["state_C"][0].rearrange("b h (u v) d -> v b (h u) d", v=P)
    new_c = O["C_s"][0].rearrange("b h (u v) d -> v b (h u) d", v=P)
    n_phys = I["cache_k"].shape[1]

    with ExitStack() as ctx:
        names = set()

        def sb(name, shape, dt=F32):
            return ctx.enter_context(nc.sbuf_tensor("sb_" + name, shape, dt))

        def sem(name):
            assert name not in names
            names.add(name)
            return ctx.enter_context(nc.semaphore(name))

        ps = ctx.enter_context(nc.psum_tensor("ps", [P, 8, 512], F32))

        def zps(slot):
            return ps[:, 2 * slot:2 * slot + 2, 0:HALF]

        def halves(ap):
            return ap.rearrange("p (a n) -> p a n", a=2)

        ident = sb("ident", [P, P])
        ones = sb("ones", [P, P])
        cmask = sb("cmask", [P, P])
        upper = sb("upper", [P, P])
        rowsel = sb("rowsel", [B, B, P])
        colsel = sb("colsel", [P, B, B])
        earlier = sb("earlier", [B, NBLK, NBLK])
        headsel = sb("headsel", [P, 2, P])
        vcol = sb("vcol", [P, V_ROWS])
        modT = sb("modT", [P, 24, 9])
        hscale = sb("hscale", [P, KT, 9])
        ptab = sb("ptab", [1, B * PAGES], I32)
        bif = sb("bif", [P, 2 * MH])
        hH = sb("hH", [P, KT, NT], F32R)
        hL = sb("hL", [P, KT, NT], F32R)
        hS = sb("hS", [P, KT, B])
        wraw = sb("wraw", [P, 4, KT, P])
        wH = sb("wH", [P, 2, KT, P], F32R)
        wL = sb("wL", [P, 2, KT, P], F32R)
        with nc.sbuf_tensor("sb_gated", [P, 6240], F32) as gated:
            pass
        ymT = gated[:, 0:4160].rearrange("p (k n) -> p k n", k=KT)
        yaT = gated[:, 4160:6240].rearrange("p (k n) -> p k n", k=PAIRS)
        uH = sb("uH", [P, KT, NT], F32R)
        sb("uH_rest", [P, 2080])
        mod = gated[0:9, 0:3072]
        cN = gated[0:9, 3072:4096]
        cSg = gated[0:9, 4160:5184]
        stC = gated[0:3 * B, 5184:6208]
        with nc.sbuf_tensor("sb_arenaA", [P, 10240], F32) as arenaA:
            pass
        page = arenaA[:, 0:4096].rearrange("p (s n) -> p s n", s=KV_SLOTS)
        prodD = arenaA[:, 4096:6144]
        prodP = arenaA[:, 6144:8192]
        qbc = arenaA[:, 8192:9216].rearrange("p (s n) -> p s n", s=2)
        vacc = qbc
        score = arenaA[:, 9216:10240]
        ada = arenaA[:, 0:8192].rearrange("p (s k n) -> p s k n", s=2, k=KT)
        yaH = sb("yaH", [P, PAIRS, NT], F32R)
        yaL = sb("yaL", [P, PAIRS, NT], F32R)
        uL = sb("uL", [P, KT, NT], F32R)
        sb("arenaA_rest", [P, 10240 - 8320])
        arenaB = sb("arenaB", [P, 11900])
        used = [0]

        def work(n, shape=None, **kw):
            ap = arenaB[:, used[0]:used[0] + n]
            used[0] += n
            assert used[0] <= 11900, used
            return ap.rearrange(shape, **kw) if shape else ap

        cT = work(KT * 9, "p (k n) -> p k n", k=KT)
        vrow = work(P)[0:V_ROWS, :]
        xt = work(TT * D, "p (s n) -> p s n", s=TT)
        htmp = work(2 * D, "p (s k n) -> p s k n", s=2, k=KT)
        xsN = work(D)[0:B, :]
        sqj = work(D)
        used[0] = 0
        qT = work(NT)
        kT = work(NT)
        vT = work(NT)
        azr = work(NT)
        azs = work(NT)
        vN = work(TT * P, "p (j n) -> p j n", j=TT)
        kN = work(TT * P, "p (j n) -> p j n", j=TT)
        prA = work(2 * TT * T, "p (e j n) -> p e j n", e=2, j=TT)
        pT = work(TT * T, "p (j n) -> p j n", j=TT)
        selc = work(2 * P, "p (e n) -> p e n", e=2)
        used[0] = 0
        pre = work(2 * (NT + 4), "p (e n) -> p e n", e=2)
        cacc = work(2 * T, "p (e n) -> p e n", e=2)
        qkc = work(2 * T, "p (e n) -> p e n", e=2)
        mvT = work(2 * NT, "p (u n) -> p u n", u=2)
        v1 = work(TT * 257, "p (j n) -> p j n", j=TT)
        go = work(2 * NT, "p (u n) -> p u n", u=2)
        gz = work(2 * NT, "p (u n) -> p u n", u=2)
        gzs = work(2 * NT, "p (u n) -> p u n", u=2)
        wtF = work(4 * 640)
        sqh = cacc[:, :, :].rearrange("p e n -> p (e n)").rearrange("p (q n) -> p q n", q=TT)
        wt = wtF.rearrange("p (j n) -> p j n", n=640)
        hn = wtF[:, 0:TT * 257].rearrange("p (j n) -> p j n", j=TT)
        kw = work(TT * P, "p (j n) -> p j n", j=TT)
        cout = work(3 * P)
        selm = work(P)[0:MH, :]
        used[0] = 0
        sga = work(KT * NT, "p (k n) -> p k n", k=KT)
        sgm = work(KT * NT, "p (k n) -> p k n", k=KT)
        cS = work(2 * D, "p (s n) -> p s n", s=2)
        cW = work(D)
        selg = work(2 * P, "p (s n) -> p s n", s=2)
        used[0] = 2 * KT * NT
        utmp = work(2 * NT, "p (s n) -> p s n", s=2)
        uu = work(2 * NT, "p (s n) -> p s n", s=2)
        used[0] = 0
        oT = work(2 * NT, "p (s n) -> p s n", s=2)
        oS = work(2 * B, "p (s n) -> p s n", s=2)
        xN = work(TT * D, "p (j n) -> p j n", j=TT)
        yO = work(D)
        xs2 = work(D)[0:B, :]
        fg = work(D)
        osq = work(D)

        qsN = sb("qsN", [B, AW])
        wif = sb("wif", [P, KT, 2 * MH])
        wifH = sb("wifH", [P, KT, 2 * MH], F32R)
        wifL = sb("wifL", [P, KT, 2 * MH], F32R)
        ss = sb("ss", [P, 5])
        rstd = sb("rstd", [P, 5])
        G = sb("G", [P, 5, 2 * MH])
        gf = sb("gf", [P, 5, MH])
        lf = sb("lf", [P, 5, MH])
        bc = sb("bc", [P, TT, MH])
        ec = sb("ec", [P, TT, MH])
        Mc = sb("Mc", [P, TT, MH])
        mt = sb("mt", [P, TT, MH])
        em = sb("em", [P, TT, MH])
        scr = sb("scr", [P, 1536])
        eR = scr[0:MH, 0:T]
        MR = sb("MR", [MH, T])
        m0 = sb("m0", [B, MH])
        gs = sb("gs", [B, 4, MH])
        aw = sb("aw", [B, 2, MH])
        mx = sb("mx", [P, 2, TT])
        nmx = sb("nmx", [P, 2, TT])
        rsum = sb("rsum", [P, 2, TT])
        rinv = sb("rinv", [P, 2, TT])
        qkvS = sb("qkvS", [P, 3, PAIRS, B])
        selfp = sb("selfp", [P, B, AH])
        yaS = sb("yaS", [P, PAIRS, B + 2])
        tS = sb("tS", [P, PAIRS, B])
        bsum = sb("bsum", [B, AH, NBLK])
        cmpA = scr[0:B, 0:512].rearrange("p (h n m) -> p h n m", h=AH, n=NBLK)
        cmpB = scr[0:B, 512:1024].rearrange("p (h n m) -> p h n m", h=AH, n=NBLK)
        pen = sb("pen", [B, AH * NBLK])
        pend = scr[0:B, 1024:1536].rearrange("p (b n) -> p b n", b=B)
        mxA = sb("mxA", [P, B * AH])
        mx64 = sb("mx64", [B * AH, 1])
        dg64 = sb("dg64", [B * AH, B * AH])
        preS = sb("preS", [P, KT, 11])
        preN = cS[0:11, 0, :]
        stT = sb("stT", [P, KT, 3 * B])
        cvS = sb("cvS", [P, KT, B])
        cvG = sb("cvG", [P, KT, B])
        cvT = sb("cvT", [P, KT, B])
        vS = sb("vS", [P, KT, B])
        wsc = sb("wsc", [P, TT])
        dl = sb("dl", [P, 4, TT])
        ssm = sb("ssm", [P, TT])
        kqN = sb("kqN", [B, 2 * AW])
        ksN = kqN[:, :].rearrange("p (a n) -> p a n", a=2)
        nN = qsN[:, :].rearrange("p (h n) -> p h n", h=MH)
        nT = scr[0:B, 0:512].rearrange("p (h n) -> p h n", h=MH)
        dS = sb("dS", [B, 3, MH])
        abc = sb("abc", [P, B, 2 * MH])
        rbc = sb("rbc", [P, B, MH])
        dgS = sb("dgS", [B, B, 2 * MH])
        Cq = sb("Cq", [P, KT, B])
        sqS = sb("sqS", [P, KT, B])
        rmsS = sb("rmsS", [P, MH, B])

        ld_c, ld_vec, ld_small, ld_x, ld_xs = (sem(n) for n in ("ld_c", "ld_vec", "ld_small", "ld_x", "ld_xs"))
        ld_st, ld_n, ld_fin, ld_xo = (sem(n) for n in ("ld_st", "ld_n", "ld_fin", "ld_xo"))
        ld_ada = [sem(f"ld_ada{i}") for i in range(2)]
        ld_w = [sem(f"ld_w{i}") for i in range(4)]
        ld_page = [sem(f"ld_page{i}") for i in range(KV_SLOTS)]
        ld_C = [sem(f"ld_C{i}") for i in range(2)]
        hi_done = sem("hi_done")
        lo_done = sem("lo_done")
        z_done = sem("z_done")
        z_free = sem("z_free")
        page_free = [sem(f"page_free{i}") for i in range(KV_SLOTS)]
        pprod_rdy, pprod_free = sem("pprod_rdy"), sem("pprod_free")
        consts, c_sig, c_silu, t_c, c_T, t_vec, v_col = (
            sem(n) for n in ("consts", "c_sig", "c_silu", "t_c", "c_T", "t_vec", "v_col"))
        ada_used, ada_ev, t_mod, mod_rdy, x_sq, x_var, x_std, x_nrm = (
            sem(n) for n in ("ada_used", "ada_ev", "t_mod", "mod_rdy", "x_sq", "x_var", "x_std", "x_nrm"))
        t_x, h_rdy, h_hi, h_lo, q_mm, q_ev, if_hi, if_lo = (
            sem(n) for n in ("t_x", "h_rdy", "h_hi", "h_lo", "q_mm", "q_ev", "if_hi", "if_lo"))
        g_mm, g_dve, g_act, g_pe, t_st, st_ev = (
            sem(n) for n in ("g_mm", "g_dve", "g_act", "g_pe", "t_st", "st_ev"))
        selc_rdy, qbc_mm, qbc_rdy, qk_done, smx, sexp, pnorm, pt_mm, pt_ev = (
            sem(n) for n in ("selc_rdy", "qbc_mm", "qbc_rdy", "qk_done", "smx", "sexp", "pnorm", "pt_mm", "pt_ev"))
        kn_mm, kn_ev, vn_mm, vn_ev, pv_done, ya_done = (
            sem(n) for n in ("kn_mm", "kn_ev", "vn_mm", "vn_ev", "pv_done", "ya_done"))
        sel_pe, sel_dve, sel_act = sem("sel_pe"), sem("sel_dve"), sem("sel_act")
        vsum_rdy, ys_mm, ys_ev, selm_rdy, mb_mm, w_exp, w_rdy, mlast_rdy, wsc_rdy = (
            sem(n) for n in ("vsum_rdy", "ys_mm", "ys_ev", "selm_rdy", "mb_mm", "w_exp", "w_rdy", "mlast_rdy", "wsc_rdy"))
        cv_rdy, sg_rdy, qk_rdy, st_mm, vt_mm, vt_ev, mpt_rdy, kt_mm, kw_rdy = (
            sem(n) for n in ("cv_rdy", "sg_rdy", "qk_rdy", "st_mm", "vt_mm", "vt_ev", "mpt_rdy", "kt_mm", "kw_rdy"))
        pv_mm, hn_ev, rs1_rdy, rs2_rdy, hn_rdy, cc_mm, c_ev, ht_mm, ym_done, v_one = (
            sem(n) for n in ("pv_mm", "hn_ev", "rs1_rdy", "rs2_rdy", "hn_rdy", "cc_mm", "c_ev", "ht_mm", "ym_done", "v_one"))
        sam_pe, sam_dve, sam_act = sem("sam_pe"), sem("sam_dve"), sem("sam_act")
        selg_rdy, kq_mm, cw_rdy, c_used, kq_used, cnew_rdy = (
            sem(n) for n in ("selg_rdy", "kq_mm", "cw_rdy", "c_used", "kq_used", "cnew_rdy"))
        fin_pe, fin_dve, fin_act, ya_hi, ym_hi, ya_lo, ym_lo = (
            sem(n) for n in ("fin_pe", "fin_dve", "fin_act", "ya_hi", "ym_hi", "ya_lo", "ym_lo"))
        uu_rdy, u_hi, u_lo, ot_act, ot_rdy, ot_mm, y_acc, y_sq, y_var, y_std, y_rdy = (
            sem(n) for n in ("uu_rdy", "u_hi", "u_lo", "ot_act", "ot_rdy", "ot_mm", "y_acc", "y_sq", "y_var", "y_std", "y_rdy"))
        st_k, st_v, st_misc, st_pre, st_c, st_C, st_y = (
            sem(n) for n in ("st_k", "st_v", "st_misc", "st_pre", "st_c", "st_C", "st_y"))
        dve_chain, act_chain, pool_chain = sem("dve_chain"), sem("act_chain"), sem("pool_chain")

        ADA_COLS = (1024, 1536, 0, 512, 2048, 2560)
        block = ctx.enter_context(nc.Block())

        @block.sync
        def _(sp):
            def tile(j, n, src):
                sp.wait_ge(lo_done, n + 1)
                sp.dma_start(wraw[:, j % 4, 0:src.shape[1], :], src).then_inc(ld_w[j % 4], 16)

            def step(pages, s, count, first):
                sp.wait_ge(page_free[s % 2], count)
                for i in range(STEP_PAGES):
                    number = sp.value_load(ptab[0:1, bass.ds(first + i, 1)], min_val=0, max_val=n_phys - 1)
                    sp.dma_start(page[:, s % 2, i * AW:(i + 1) * AW],
                                 pages[:, bass.ds(number, 1), :].rearrange("t o n -> t (o n)")
                                 ).then_inc(ld_page[s % 2], 16)

            sp.dma_start(cN[0:B, :], I["c_sample"]).then_inc(ld_c, 16)
            sp.dma_start(cN[B:B + 1, :], I["c_prompt"]).then_inc(ld_c, 16)
            for row, name in ((V_G, "norm_g"), (V_MG, "m_norm_g"), (V_BC, "b_conv"), (V_WC, "w_conv"),
                              (V_BA, "b_ada")):
                src = I[name][0:1] if name != "w_conv" else I[name][0]
                n = (src.shape[0] * src.shape[1]) // P
                sp.dma_start(vrow[row:row + n, :], src.rearrange("a (r n) -> (a r) n", n=P)).then_inc(ld_vec, 16)
            for i in range(2):
                sp.dma_start(ada[:, i], w_ada[:, :, ADA_COLS[i]:ADA_COLS[i] + 512]).then_inc(ld_ada[i], 16)
            sp.dma_start(xt, x_p.rearrange("(j p) d -> p j d", p=P)).then_inc(ld_x, 16)
            sp.dma_start(xsN, x_s).then_inc(ld_xs, 16)
            sp.dma_start(ptab[:, :], I["page_table"].rearrange("b n -> (b n)").rearrange("(o n) -> o n", o=1)
                         ).then_inc(ld_small, 16)
            sp.dma_start(bif[:, :], I["b_if"][0:1].broadcast_to([P, 2 * MH])).then_inc(ld_small, 16)
            sp.dma_start(wif[:, :, :], w_in[:, :, CIF:CIF + 2 * MH]).then_inc(ld_small, 16)
            sp.dma_start(m0[:, :], I["state_m"][0]).then_inc(ld_small, 16)
            sp.dma_start(stC, I["state_conv"][0].rearrange("b j d -> (b j) d")).then_inc(ld_st, 16)
            for i in range(2, 7):
                sp.wait_ge(ada_used, i - 1)
                src = w_ada[:, :, ADA_COLS[i]:ADA_COLS[i] + 512] if i < 6 else w_in[:, :, CQ:CQ + AW]
                sp.dma_start(ada[:, i % 2], src).then_inc(ld_ada[i % 2], 16)
            sp.wait_ge(ld_small, 64)

            def att_tile(j, t):
                return w_in[:, :, bass.ds(t * P + (CQ, CK, CV, CZ)[j], P)]

            def ml_tile(j, h):
                col, by = ((CMQK, MQ), (CMQK + MH * MQ, MQ), (CMV, MV), (CMV + P, MV), (CMO, MV), (CMO + P, MV),
                           (CMZ, MV), (CMZ + P, MV))[j]
                return w_in[:, :, bass.ds(h * by + col, P)]

            def gate_tile(j, t):
                return w_in[:, :, bass.ds(t * 2 * P + (j // 2) * P + (CGA, CGM)[j % 2], P)]

            def comb_tile(j, t):
                return (w_att, w_ml)[j % 2][:, :, bass.ds(t * 2 * P + (j // 2) * P, P)]

            def out_tile(j, t):
                return w_out[:, :, bass.ds(t * 4 * P + j * P, P)]

            for j in range(4):
                tile(j, T_ATT + j, att_tile(j, 0))
            sp.wait_ge(ada_used, 7)

            def attention(t, following, tt_):
                n = T_ATT + 4 * t + 4
                tile(0, n, following(0, tt_))
                tile(1, n + 1, following(1, tt_))
                for s in range(8):
                    if s == 2 or s == 4:
                        tile(1 + s // 2, n + 1 + s // 2, following(1 + s // 2, tt_))
                    step(pages_k, s, 4 * t + s // 2 + 1, 32 * t + 4 * s)

            with sp.Fori(0, PAIRS - 1) as t:
                attention(t, att_tile, t + 1)
            attention(PAIRS - 1, ml_tile, 0)
            sp.wait_ge(qbc_mm, 2 * PAIRS)
            sp.dma_start(qsN[:, :], I["state_n"][0].rearrange("b h d -> b (h d)")).then_inc(ld_n, 16)

            def mlstm(h, following, hh):
                n = T_ML + 8 * h + 4
                for j in range(8):
                    tile(j, n + j, ml_tile(j + 4, h) if j < 4 else following(j - 4, hh))
                    step(pages_v, j, 16 + 4 * h + j // 2 + 1, 32 * h + 4 * j)

            with sp.Fori(0, MH - 1) as h:
                mlstm(h, ml_tile, h + 1)
            mlstm(MH - 1, gate_tile, 0)

            def gates(t, following, tt_):
                for j in range(4):
                    tile(j, T_GATE + 4 * t + 4 + j, following(j, tt_))
                    if j % 2 == 0:
                        e = j // 2
                        sp.wait_ge(c_used, 2 * t + e + 1)
                        sp.dma_start(cS[:, e].rearrange("p (u d) -> p u d", u=KT),
                                     state_c[:, bass.ds(2 * t + e, 1)].rearrange("v o u d -> v (o u) d")
                                     ).then_inc(ld_C[e], 16)

            sp.wait_ge(ym_done, 1 + MH)
            sp.wait_ge(st_pre, 32)
            sp.wait_ge(st_c, 16 * (2 * MH + 2))
            with sp.Fori(0, 3) as t:
                gates(t, gate_tile, t + 1)
            gates(3, comb_tile, 0)
            with sp.Fori(0, 3) as t:
                for j in range(4):
                    tile(j, T_COMB + 4 * t + 4 + j, comb_tile(j, t + 1))
            for j in range(8):
                tile(j, T_OUT + j, out_tile(j % 4, j // 4))
                if j == 3:
                    sp.wait_ge(uu_rdy, KT)
                    sp.dma_start(xN, x_p.rearrange("(j p) d -> p j d", p=P)).then_inc(ld_xo, 16)
                    sp.dma_start(xs2, x_s).then_inc(ld_xo, 16)
                    sp.dma_start(fg, I["final_g"].rearrange("(o n) -> o n", o=1).broadcast_to([P, D])).then_inc(ld_xo, 16)
            sp.wait_ge(y_rdy, TT + 1)
            sp.dma_start(O["y_p"].rearrange("o (j p) d -> p (o j) d", p=P), xN).then_inc(st_y, 16)
            sp.dma_start(O["y_s"].rearrange("b o d -> (b o) d"), xs2).then_inc(st_y, 16)
            sp.wait_ge(st_y, 32)

        @block.tensor
        def _(pe):
            mm = nc.tensor.matmul
            tr = nc.tensor.transpose

            def ztile(j, n, xH, xL, ks=KT):
                pe.wait_ge(lo_done, n + 5)
                pe.wait_ge(z_free, n + 1)
                s = j % 2
                for k in range(ks):
                    for w, xs_ in ((wH, (xH, xL)), (wL, (xH,))):
                        for x in xs_:
                            for a in range(2):
                                last = mm(ps[:, 2 * s + a, 0:HALF], w[:, s, k, :], x[:, k, a * HALF:(a + 1) * HALF],
                                          start=(k == 0 and w is wH and x is xH), stop=(k == ks - 1 and w is wL))
                last.then_inc(z_done, 1)

            pe.sem_inc(z_done, 2)
            pe.wait_ge(consts, 1)
            pe.wait_ge(ld_vec, 80)
            tr(ps[:, 5, 0:V_ROWS], vrow, ident[0:V_ROWS, 0:V_ROWS]).then_inc(t_vec, 1)
            pe.wait_ge(c_silu, 1)
            for k in range(KT):
                last = tr(ps[:, 4, 9 * k:9 * k + 9], cN[:, k * P:(k + 1) * P], ident[0:9, 0:9])
            last.then_inc(t_c, 1)
            pe.wait_ge(c_T, 1)
            for i in range(6):
                pe.wait_ge(ld_ada[i % 2], 16 * (i // 2 + 1))
                if i >= 2:
                    pe.wait_ge(ada_ev, i - 1)
                for k in range(KT):
                    last = mm(ps[0:9, i % 2, :], cT[:, k, :], ada[:, i % 2, k, :], start=(k == 0), stop=(k == KT - 1))
                last.then_inc(ada_used, 1)
                if i == 3 or i == 5:
                    pe.wait_ge(ada_ev, i + 1)
                    pe.wait_ge(v_col, 1)
                    b, lo, hi = (5, 0, 16) if i == 3 else (4, 16, 24)
                    for j in range(lo, hi):
                        last = tr(ps[:, b, 9 * (j - lo):9 * (j - lo) + 9], mod[:, j * P:(j + 1) * P], ident[0:9, 0:9])
                    last.then_inc(t_mod, 1)
            pe.wait_ge(x_nrm, 1)
            for j in range(TT):
                b = 2 if j % 2 == 0 else 6
                if j >= 2:
                    pe.wait_ge(h_rdy, j - 1)
                for k in range(KT):
                    last = tr(ps[:, b + k // 4, (k % 4) * P:(k % 4 + 1) * P], xt[:, j, k * P:(k + 1) * P], ident[:, :])
                last.then_inc(t_x, 1)
            pe.wait_ge(mod_rdy, 2)
            for k in range(KT):
                last = tr(ps[:, 4, B * k:B * k + B], xsN[:, k * P:(k + 1) * P], ident[0:B, 0:B])
            last.then_inc(t_x, 1)
            pe.wait_ge(ld_ada[0], 64)
            pe.wait_ge(h_rdy, TT + 1)
            pe.wait_ge(ada_ev, 6)
            for k in range(KT):
                last = mm(ps[0:B, 0, :], hS[:, k, :], ada[:, 0, k, :], start=(k == 0), stop=(k == KT - 1))
            last.then_inc(ada_used, 1)
            pe.wait_ge(ld_st, 16)
            for k in range(KT):
                last = tr(ps[:, 2, 24 * k:24 * k + 24], stC[:, k * P:(k + 1) * P], ident[0:24, 0:24])
            last.then_inc(t_st, 1)
            pe.wait_ge(h_lo, TT + 1)
            pe.wait_ge(if_lo, 1)
            for j in range(TT):
                tok = slice(j * P, (j + 1) * P)
                for k in range(KT):
                    mm(ps[:, 1, 8 * j:8 * j + 8], hH[:, k, tok], wifH[:, k, :], start=(k == 0), stop=False)
                    mm(ps[:, 1, 8 * j:8 * j + 8], hL[:, k, tok], wifH[:, k, :], start=False, stop=False)
                    mm(ps[:, 1, 8 * j:8 * j + 8], hH[:, k, tok], wifL[:, k, :], start=False, stop=(k == KT - 1))
            for k in range(KT):
                last = mm(ps[0:B, 1, 32:40], hS[:, k, :], wif[:, k, :], start=(k == 0), stop=(k == KT - 1))
            last.then_inc(g_mm, 1)
            pe.wait_ge(g_dve, 3)
            for j in range(TT):
                last = mm(ps[:, 5, MH * j:MH * j + MH], upper[:, :], lf[:, j, :], start=True, stop=(j == 0))
                for i in range(j):
                    last = mm(ps[:, 5, MH * j:MH * j + MH], ones[:, :], lf[:, i, :], start=False, stop=(i == j - 1))
            last.then_inc(g_pe, 1)
            pe.wait_ge(g_dve, 4)
            for j in range(TT):
                last = tr(ps[0:MH, 6, j * P:(j + 1) * P], ec[:, j, :], ident[:, :])
            last.then_inc(g_pe, 1)
            pe.wait_ge(g_dve, 5)
            for j in range(TT):
                last = tr(ps[:, 4, MH * j:MH * j + MH], MR[:, j * P:(j + 1) * P], ident[0:MH, 0:MH])
            last.then_inc(g_pe, 1)
            pe.wait_ge(g_dve, 6)
            pe.wait_ge(q_ev, 1)
            pe.wait_ge(st_ev, 1)

            def qk(e):
                r = slice(DH * e, DH * e + DH)
                for q, b, c in ((3, 4, 0), (2, 5, 0), (0, 5, 384), (1, 6, 0)):
                    last = mm(ps[:, b, c:c + (q + 1) * P], qT[r, q * P:(q + 1) * P], kT[r, 0:(q + 1) * P],
                              start=True, stop=True)
                last.then_inc(qk_done, 1)

            def ptrans(e):
                for k, b, c in ((0, 4, 0), (1, 5, 0), (3, 5, 384), (2, 6, 0)):
                    for q in range(k, TT):
                        last = tr(ps[:, b, c + (q - k) * P:c + (q - k + 1) * P], prA[:, e, q, k * P:(k + 1) * P],
                                  ident[:, :])
                last.then_inc(pt_mm, 1)

            def pv(e):
                for k in range(TT):
                    last = mm(ps[DH * e:DH * e + DH, 7, k * P:T], vN[:, k, DH * e:DH * e + DH], pT[:, k, k * P:T],
                              start=(k == 0), stop=(k == TT - 1))
                return last

            with pe.Fori(0, PAIRS) as t:
                n = T_ATT + 4 * t
                pe.wait_ge(pt_ev, 2 * t + 1)
                for e in range(2):
                    pe.wait_ge(selc_rdy, 2 * t + e + 1)
                    mm(ps[:, 4 + e, :], selc[0:B, e, :], qsN[:, :], start=True, stop=True).then_inc(qbc_mm, 1)
                ztile(0, n, hH, hL)
                ztile(1, n + 1, hH, hL)
                pe.wait_ge(z_free, n + 4)
                pe.wait_ge(qbc_rdy, 2 * t + 2)
                qk(0)
                pe.wait_ge(ya_done, t + 1)
                for j in range(TT):
                    last = tr(ps[:, 7, j * P:(j + 1) * P], kT[:, j * P:(j + 1) * P], ident[:, :])
                last.then_inc(kn_mm, 1)
                ztile(2, n + 2, hH, hL)
                pe.wait_ge(pnorm, 2 * t + 1)
                ptrans(0)
                pe.wait_ge(kn_ev, t + 1)
                pe.wait_ge(z_free, n + 5)
                for j in range(TT):
                    last = tr(ps[:, 7, j * P:(j + 1) * P], vT[:, j * P:(j + 1) * P], ident[:, :])
                last.then_inc(vn_mm, 1)
                pe.wait_ge(pt_ev, 2 * t + 2)
                qk(1)
                pe.wait_ge(vn_ev, t + 1)
                pv(0)
                ztile(3, n + 3, hH, hL)
                pe.wait_ge(pnorm, 2 * t + 2)
                ptrans(1)
                pe.wait_ge(pt_ev, 2 * t + 3)
                pv(1).then_inc(pv_done, 1)

            pe.wait_ge(sel_dve, 1)
            for e in range(2):
                last = mm(ps[:, 4, 32 * e:32 * e + 32], headsel[:, e, :], tS[:, :, :].rearrange("p a b -> p (a b)"),
                          start=True, stop=True)
            last.then_inc(sel_pe, 1)
            for a in range(2):
                for t in range(PAIRS):
                    last = tr(ps[0:B, 5 + a, t * P:(t + 1) * P], qkvS[:, 1 + a, t, :], ident[:, :])
            last.then_inc(sel_pe, 1)
            pe.wait_ge(ya_done, 1 + PAIRS)
            pe.wait_ge(sel_dve, 2)
            for b in range(B):
                last = mm(ps[0:B, 7, 0:P], colsel[:, b, :], score[:, b * P:(b + 1) * P], start=(b == 0), stop=(b == B - 1))
            last.then_inc(sel_pe, 1)
            pe.wait_ge(sel_dve, 3)
            mm(ps[:, 7, :], ones[0:B, :], pend.rearrange("p b n -> p (b n)"), start=True, stop=True).then_inc(sel_pe, 1)
            pe.wait_ge(sel_dve, 4)
            tr(ps[0:B * AH, 4, 0:P], mxA[:, :], ident[:, :]).then_inc(sel_pe, 1)
            pe.wait_ge(sel_dve, 5)
            mm(ps[:, 4, 128:192], ones[0:B * AH, :], dg64[:, :], start=True, stop=True).then_inc(sel_pe, 1)
            pe.wait_ge(sel_dve, 7)
            mm(ps[:, 4, 256:320], ones[:, :], mxA[:, :], start=True, stop=True).then_inc(sel_pe, 1)
            pe.wait_ge(sel_act, 2)
            pe.wait_ge(sel_dve, 8)

            def page_sums(h):
                pe.wait_ge(vsum_rdy, h + 1)
                for e in range(2):
                    for c in range(PAIRS):
                        last = mm(ps[:, 6, PAIRS * e + c:PAIRS * e + c + 1], vacc[:, e, c * P:(c + 1) * P], ones[:, 0:1],
                                  start=True, stop=True)
                last.then_inc(ys_mm, 1)

            with pe.Fori(0, MH) as h:
                n = T_ML + 8 * h
                pe.wait_ge(hn_ev, 4 * h + 1)
                page_sums(h)
                ztile(0, n, hH, hL)
                ztile(1, n + 1, hH, hL)
                pe.wait_ge(selm_rdy, h + 1)
                pe.wait_ge(c_ev, h + 1)
                mm(ps[:, 7, :], selm, MR[:, :], start=True, stop=True).then_inc(mb_mm, 1)
                ztile(2, n + 2, hH, hL)
                ztile(3, n + 3, hH, hL)
                pe.wait_ge(qk_rdy, h + 1)
                pe.wait_ge(ym_done, h + 1)
                pe.wait_ge(ys_ev, h + 1)
                for k, b, c in ((0, 4, 0), (1, 5, 0), (3, 5, 384), (2, 6, 0)):
                    last = mm(ps[:, b, c:c + T - k * P], qkc[:, 1, k * P:(k + 1) * P], qkc[:, 0, k * P:T],
                              start=True, stop=True)
                last.then_inc(st_mm, 1)
                pe.wait_ge(w_exp, h + 1)
                pe.wait_ge(mlast_rdy, h + 1)
                pe.wait_ge(z_free, n + 6)
                for u in range(2):
                    if u == 1:
                        pe.wait_ge(vt_ev, 2 * h + 1)
                    for j in range(TT):
                        last = tr(ps[:, 7, j * P:(j + 1) * P], mvT[:, u, j * P:(j + 1) * P], ident[:, :])
                    last.then_inc(vt_mm, 1)
                    ztile(u, n + 4 + u, hH, hL)
                pe.wait_ge(mpt_rdy, h + 1)
                for j in range(TT):
                    last = tr(ps[:, 6, j * P:(j + 1) * P], qkc[:, 1, j * P:(j + 1) * P], ident[:, :])
                last.then_inc(kt_mm, 1)
                pe.wait_ge(vt_ev, 2 * h + 2)
                pe.wait_ge(v_one, 1)
                for q, b in ((0, 4), (1, 5), (2, 7), (3, 6)):
                    if q == 3:
                        pe.wait_ge(kw_rdy, h + 1)
                    for k in range(q + 1):
                        last = mm(ps[:, b, 0:MV + 1], wt[:, k, (q - k) * P:(q - k + 1) * P], v1[:, k, :],
                                  start=(k == 0), stop=(k == q))
                last.then_inc(pv_mm, 1)
                ztile(2, n + 6, hH, hL)
                ztile(3, n + 7, hH, hL)
                pe.wait_ge(hn_ev, 4 * h + 5)
                for u in range(3):
                    for j in range(TT):
                        if u < 2:
                            last = mm(ps[:, 7, u * P:(u + 1) * P], v1[:, j, u * P:(u + 1) * P], kw[:, j, :],
                                      start=(j == 0), stop=(j == TT - 1))
                        else:
                            last = mm(ps[0:1, 7, 2 * P:3 * P], ones[:, 0:1], kw[:, j, :],
                                      start=(j == 0), stop=(j == TT - 1))
                last.then_inc(cc_mm, 1)
                pe.wait_ge(hn_rdy, h + 1)
                for u in range(2):
                    for j in range(TT):
                        last = tr(ps[:, 4 + u, j * P:(j + 1) * P], hn[:, j, u * P:(u + 1) * P], ident[:, :])
                last.then_inc(ht_mm, 1)
            page_sums(MH)

            pe.wait_ge(c_ev, 1 + MH)
            pe.wait_ge(ym_done, 1 + MH)
            pe.wait_ge(sam_dve, 1)
            mm(ps[:, 7, 0:64], ones[0:B, :], dgS[:, :, :].rearrange("p b n -> p (b n)"), start=True, stop=True)\
                .then_inc(sam_pe, 1)
            for k in range(KT):
                last = tr(ps[0:11, 4 + k // 4, (k % 4) * P:(k % 4 + 1) * P], preS[:, k, :], ident[:, :])
            last.then_inc(sam_pe, 1)
            pe.wait_ge(sam_dve, 3)
            pe.wait_ge(sam_act, 2)
            for k in range(KT):
                last = tr(ps[0:B, 4 + k // 4, (k % 4) * P:(k % 4 + 1) * P], cvS[:, (k + 4) % KT, :], ident[:, :])
            last.then_inc(sam_pe, 1)
            pe.wait_ge(sam_dve, 4)
            mm(ps[:, 7, 64:96], ones[0:B, :], dgS[:, :, 0:MH], start=True, stop=True).then_inc(sam_pe, 1)
            pe.wait_ge(sam_dve, 5)
            pe.wait_ge(sam_act, 3)

            with pe.Fori(0, 4) as t:
                n = T_GATE + 4 * t
                for e in range(2):
                    pe.wait_ge(selg_rdy, 2 * t + e + 1)
                    pe.wait_ge(kq_used, 2 * t + e + 1)
                    for a in range(2):
                        last = mm(ps[:, 4 + 2 * e + a, :], selg[0:B, e, :], kqN[:, a * AW:(a + 1) * AW],
                                  start=True, stop=True)
                    last.then_inc(kq_mm, 1)
                    ztile(0, n + 2 * e, hH, hL)
                    ztile(1, n + 2 * e + 1, hH, hL)
            pe.wait_ge(fin_dve, 1)
            mm(ps[:, 4, 0:64], ones[:, :], sqS[:, :, :].rearrange("p k b -> p (k b)"), start=True, stop=True)\
                .then_inc(fin_pe, 1)

            pe.wait_ge(ya_lo, 1)
            pe.wait_ge(ym_lo, 1)
            with pe.Fori(0, 4) as t:
                n = T_COMB + 4 * t
                for c in range(2):
                    ztile(0, n + 2 * c, yaH, yaL, PAIRS)
                    ztile(1, n + 2 * c + 1, hH, hL)
            pe.wait_ge(u_lo, 2 + KT)
            with pe.Fori(0, 2) as t:
                for j in range(4):
                    ztile(j, T_OUT + 4 * t + j, uH, uL)
                    pe.wait_ge(ot_rdy, 4 * t + j + 1)
                    pe.wait_ge(y_acc, 4 * t + j + 1)
                    s = j % 2
                    for i in range(TT):
                        tr(ps[:, 4 + 2 * s, i * P:(i + 1) * P], oT[:, s, i * P:(i + 1) * P], ident[:, :])
                    tr(ps[0:B, 5 + 2 * s, 0:P], oT[:, s, T:NT], ident[:, :]).then_inc(ot_mm, 1)

        @block.scalar
        def _(act):
            chain = Chain(act, act_chain)
            f = nc.scalar.activation

            def high(j, n, quad):
                act.wait_ge(ld_w[j % 4], 16 * (quad + 1))
                act.wait_ge(z_done, n + 1)
                f(wH[:, j % 2], wraw[:, j % 4], ACT.Copy).then_inc(hi_done, 1)

            def leave(j, n, *dests):
                act.wait_ge(z_done, n + 3)
                for dst, func in dests:
                    ins = f(halves(dst), zps(j % 2), func)
                ins.then_inc(z_free, 1)

            act.sem_inc(z_free, 2)
            act.sem_inc(pt_ev, 1)
            act.sem_inc(hn_ev, 1)
            act.sem_inc(c_ev, 1)
            act.sem_inc(st_k, 16)
            act.sem_inc(st_v, 16)
            act.sem_inc(st_C, 16)
            act.sem_inc(st_c, 32)
            act.wait_ge(ld_c, 32)
            f(cSg, cN, ACT.Sigmoid).then_inc(c_sig, 1)

            def ada_leave(i):
                act.wait_ge(ada_used, i + 1)
                f(mod[:, ADA_COLS[i]:ADA_COLS[i] + 512], ps[0:9, i % 2, :], ACT.Copy).then_inc(ada_ev, 1)

            ada_leave(0)
            ada_leave(1)
            act.wait_ge(ld_x, 16)
            act.wait_ge(ld_xs, 16)
            act.wait_ge(v_col, 1)
            for j in range(TT):
                chain(f(sqj, xt[:, j, :], ACT.Square, accum_out=ss[:, j:j + 1]))
            f(sqj[0:B, :], xsN, ACT.Square, accum_out=ss[0:B, 4:5]).then_inc(x_sq, 1)
            act.wait_ge(x_var, 1)
            f(ss[:, :], rstd[:, :], ACT.Sqrt).then_inc(x_std, 1)
            for i in range(2, 6):
                ada_leave(i)
            act.wait_ge(ld_small, 64)
            f(wifH[:, :, :], wif[:, :, :], ACT.Copy).then_inc(if_hi, 1)
            for j in range(TT):
                act.wait_ge(h_rdy, j + 1)
                f(hH[:, :, j * P:(j + 1) * P], htmp[:, j % 2], ACT.Copy).then_inc(h_hi, 1)
            act.wait_ge(h_rdy, TT + 1)
            f(hH[:, :, T:NT], hS[:, :, :], ACT.Copy).then_inc(h_hi, 1)
            act.wait_ge(ada_used, 7)
            f(qsN[:, :], ps[0:B, 0, :], ACT.Copy).then_inc(q_ev, 1)
            act.wait_ge(t_st, 1)
            f(stT[:, :, :].rearrange("p k n -> p (k n)"), ps[:, 2, 0:192], ACT.Copy).then_inc(st_ev, 1)
            for n in range(2):
                high(n, n, 0)
            act.wait_ge(g_dve, 2)
            chain(f(gf[:, :, :], gf[:, :, :], ACT.Exp))
            f(gf[:, :, :], gf[:, :, :], ACT.Ln, bias=1.0).then_inc(g_act, 1)
            act.wait_ge(g_dve, 6)
            f(em[:, :, :], mt[:, :, :], ACT.Exp, scale=-1.0).then_inc(g_act, 1)
            act.wait_ge(g_dve, 7)
            f(aw[:, :, :], aw[:, :, :], ACT.Exp)
            f(gs[:, 2, :], gs[:, 1, :], ACT.Exp, scale=-1.0).then_inc(g_act, 1)
            act.dma_start(O["m_s"][0], gs[:, 1, :]).then_inc(st_misc, 16)
            act.dma_start(O["m_p"][0], mt[P - 1:P, TT - 1, :]).then_inc(st_misc, 16)

            def rows_out(dst, t):
                return dst.rearrange("o b (j p) h d -> p (o b j) (h d)", p=P)[:, :, bass.ds(t * P, P)]

            def weights(e, t):
                act.wait_ge(smx, 2 * t + e + 1)
                for q, b, c in ((3, 4, 0), (2, 5, 0), (0, 5, 384), (1, 6, 0)):
                    last = f(prA[:, e, q, 0:(q + 1) * P], ps[:, b, c:c + (q + 1) * P], ACT.Exp,
                             bias=nmx[:, e, q:q + 1], scale=SCALE, accum_out=rsum[:, e, q:q + 1])
                last.then_inc(sexp, 1)

            def turned(e, t):
                act.wait_ge(pt_mm, 2 * t + e + 1)
                for k, b, c in ((0, 4, 0), (1, 5, 0), (3, 5, 384), (2, 6, 0)):
                    last = f(pT[:, k, k * P:T], ps[:, b, c:c + T - k * P], ACT.Copy)
                last.then_inc(pt_ev, 1)

            with act.Fori(0, PAIRS) as t:
                n, quad = T_ATT + 4 * t, t
                act.wait_ge(page_free[0], 4 * t + 1)
                act.wait_ge(page_free[1], 4 * t + 1)
                for e in range(2):
                    act.wait_ge(qbc_mm, 2 * t + e + 1)
                    f(qbc[:, e, :], ps[:, 4 + e, :], ACT.Copy).then_inc(qbc_rdy, 1)
                high(2, n + 2, quad)
                leave(0, n, (qT, ACT.Copy))
                high(3, n + 3, quad)
                leave(1, n + 1, (kT, ACT.Copy))
                act.wait_ge(kn_mm, t + 1)
                act.wait_ge(st_k, 16 * t + 16)
                f(kN, ps[:, 7, :].rearrange("p (j n) -> p j n", j=TT), ACT.Copy).then_inc(kn_ev, 1)
                act.wait_ge(kn_ev, t + 1)
                act.dma_start(rows_out(O["k_p"], t), kN).then_inc(st_k, 16)
                weights(0, t)
                high(0, n + 4, quad + 1)
                leave(0, n + 2, (vT, ACT.Copy))
                turned(0, t)
                act.wait_ge(vn_mm, t + 1)
                act.wait_ge(st_v, 16 * t + 16)
                f(vN, ps[:, 7, :].rearrange("p (j n) -> p j n", j=TT), ACT.Copy).then_inc(vn_ev, 1)
                act.wait_ge(vn_ev, t + 1)
                act.dma_start(rows_out(O["v_p"], t), vN).then_inc(st_v, 16)
                weights(1, t)
                high(1, n + 5, quad + 1)
                leave(1, n + 3, (azr, ACT.Copy), (azs, ACT.Sigmoid))
                turned(1, t)
            act.wait_ge(ya_done, 1 + PAIRS)
            act.wait_ge(st_k, 16 * (1 + PAIRS))
            act.wait_ge(st_v, 16 * (1 + PAIRS))
            act.wait_ge(sel_pe, 2)
            for a in range(2):
                last = f(ksN[:, a, :], ps[0:B, 5 + a, :], ACT.Copy)
            last.then_inc(sel_act, 1)
            act.wait_ge(sel_act, 1)
            act.dma_start(O["k_s"].rearrange("o b q h d -> (o b q) (h d)"), ksN[:, 0, :]).then_inc(st_misc, 16)
            act.dma_start(O["v_s"].rearrange("o b q h d -> (o b q) (h d)"), ksN[:, 1, :]).then_inc(st_misc, 16)
            act.wait_ge(sel_dve, 6)
            f(score, score, ACT.Exp, scale=SCALE)
            f(selfp[:, :, :], selfp[:, :, :], ACT.Exp, scale=SCALE).then_inc(sel_act, 1)

            def sums_leave(h):
                act.wait_ge(ys_mm, h + 1)
                f(yaS[:, :, bass.ds(2 * h, 2)].rearrange("p c e -> p e c"),
                  ps[:, 6, 0:2 * PAIRS].rearrange("p (e c) -> p e c", e=2), ACT.Copy).then_inc(ys_ev, 1)

            with act.Fori(0, MH) as h:
                n, quad = T_ML + 8 * h, T_ML // 4 + 2 * h
                sums_leave(h)
                high(2, n + 2, quad)
                leave(0, n, (pre[:, 0, 3:3 + NT], ACT.Copy))
                high(3, n + 3, quad)
                leave(1, n + 1, (pre[:, 1, 3:3 + NT], ACT.Copy))
                act.wait_ge(mb_mm, h + 1)
                for k in range(TT):
                    last = f(wt[:, k, 0:T - k * P], ps[:, 7, k * P:T], ACT.Exp, bias=ec[:, k, bass.ds(h, 1)], scale=-1.0)
                last.then_inc(w_exp, 1)
                act.wait_ge(mlast_rdy, h + 1)
                f(wsc[:, :], dl[:, 0, :], ACT.Exp).then_inc(wsc_rdy, 1)
                for e in range(2):
                    act.wait_ge(cv_rdy, 2 * h + e + 1)
                    f(qkc[:, e, :], cacc[:, e, :], ACT.Sigmoid).then_inc(sg_rdy, 1)
                high(0, n + 4, quad + 1)
                leave(0, n + 2, (mvT[:, 0, :], ACT.Copy))
                high(1, n + 5, quad + 1)
                leave(1, n + 3, (mvT[:, 1, :], ACT.Copy))
                for u in range(2):
                    act.wait_ge(vt_mm, 2 * h + u + 1)
                    f(v1[:, :, u * P:(u + 1) * P], ps[:, 7, :].rearrange("p (j n) -> p j n", j=TT), ACT.Copy)\
                        .then_inc(vt_ev, 1)
                    high(2 + u, n + 6 + u, quad + 1)
                    leave(u, n + 4 + u, (go[:, u, :], ACT.Sigmoid))
                act.wait_ge(pv_mm, h + 1)
                for q, b in ((0, 4), (1, 5), (2, 7), (3, 6)):
                    f(sqh[:, q, :], ps[:, b, 0:MV], ACT.Square, accum_out=ssm[:, q:q + 1])
                    f(hn[:, q, :], ps[:, b, 0:MV + 1], ACT.Copy).then_inc(hn_ev, 1)
                act.wait_ge(rs1_rdy, h + 1)
                f(dl[:, 1, :], dl[:, 3, :], ACT.Sqrt).then_inc(rs2_rdy, 1)
                high(0, n + 8, quad + 2)
                leave(0, n + 6, (gz[:, 0, :], ACT.Copy), (gzs[:, 0, :], ACT.Sigmoid))
                high(1, n + 9, quad + 2)
                leave(1, n + 7, (gz[:, 1, :], ACT.Copy), (gzs[:, 1, :], ACT.Sigmoid))
                act.wait_ge(cc_mm, h + 1)
                act.wait_ge(st_c, 32 * h + 32)
                f(cout[:, 0:2 * P], ps[:, 7, 0:2 * P], ACT.Copy)
                f(cout[0:1, 2 * P:3 * P], ps[0:1, 7, 2 * P:3 * P], ACT.Copy).then_inc(c_ev, 1)
                act.wait_ge(c_ev, h + 2)
                act.dma_start(O["C_p"][0, 0].rearrange("h (u v) d -> v (h u) d", v=P)[:, bass.ds(2 * h, 2), :],
                              cout[:, 0:2 * P].rearrange("p (u d) -> p u d", u=2)).then_inc(st_c, 16)
                act.dma_start(O["n_p"][0, 0][bass.ds(h, 1), :], cout[0:1, 2 * P:3 * P]).then_inc(st_c, 16)
            sums_leave(MH)
            act.dma_start(O["conv_s"][0, :, 0:2, :], I["state_conv"][0, :, 1:3, :]).then_inc(st_misc, 16)
            act.wait_ge(ym_done, 1 + MH)
            act.wait_ge(st_c, 32 * MH + 32)
            act.wait_ge(sam_dve, 2)
            f(cvG[:, :, :], cvS[:, :, :], ACT.Sigmoid).then_inc(sam_act, 1)
            act.wait_ge(sam_pe, 2)
            f(preN.rearrange("p (a n) -> p a n", a=2), ps[0:11, 4:6, :], ACT.Copy).then_inc(sam_act, 1)
            act.wait_ge(sam_act, 2)
            act.dma_start(O["conv_p"][0, 0], preN[0:3, :]).then_inc(st_pre, 16)
            act.dma_start(O["conv_s"][0, :, 2, :], preN[3:11, :]).then_inc(st_pre, 16)
            act.wait_ge(sam_pe, 3)
            act.wait_ge(st_misc, 16 * 5)
            f(kqN[:, :].rearrange("p (a n) -> p a n", a=2), ps[0:B, 4:6, :], ACT.Copy).then_inc(sam_act, 1)
            act.wait_ge(sam_dve, 4)
            act.dma_start(O["n_s"][0], nN).then_inc(st_misc, 16)

            with act.Fori(0, 4) as t:
                n, quad = T_GATE + 4 * t, T_GATE // 4 + t
                for j in range(4):
                    high((j + 2) % 4, n + j + 2, quad + (j + 2) // 4)
                    leave(j, n + j, ((sga, sgm)[j % 2][:, bass.ds(2 * t + j // 2, 1), :].rearrange("p o n -> p (o n)"),
                                     ACT.Sigmoid))
                    if j % 2 == 1:
                        act.wait_ge(cnew_rdy, 2 * t + j // 2 + 1)
                        act.dma_start(new_c[:, bass.ds(2 * t + j // 2, 1)].rearrange("v o u d -> v (o u) d"),
                                      cW.rearrange("p (u d) -> p u d", u=KT)).then_inc(st_C, 16)
            act.wait_ge(fin_dve, 2)
            f(rmsS[:, :, :], rmsS[:, :, :], ACT.Sqrt).then_inc(fin_act, 1)
            act.wait_ge(fin_dve, 3)
            f(yaH[:, :, :], yaT, ACT.Copy).then_inc(ya_hi, 1)
            act.wait_ge(z_done, 2 + T_COMB)
            f(hH[:, :, :], ymT, ACT.Copy).then_inc(ym_hi, 1)
            act.wait_ge(ym_lo, 1)
            act.wait_ge(ya_lo, 1)
            with act.Fori(0, 4) as t:
                n, quad = T_COMB + 4 * t, T_COMB // 4 + t
                for j in range(4):
                    high((j + 2) % 4, n + j + 2, quad + (j + 2) // 4)
                    if j % 2 == 1:
                        c = j // 2
                        act.wait_ge(uu_rdy, 2 * t + c + 1)
                        f(uH[:, bass.ds(2 * t + c, 1), :].rearrange("p o n -> p (o n)"), uu[:, c, :], ACT.Copy)\
                            .then_inc(u_hi, 1)
            act.wait_ge(uu_rdy, KT)
            for j in range(8):
                n = T_OUT + j
                if j < 6:
                    high(j + 2, n + 2, (n + 2) // 4)
                if j >= 2:
                    act.wait_ge(ot_mm, j - 1)
                else:
                    act.wait_ge(u_lo, 2 + KT)
                act.wait_ge(z_done, n + 3)
                f(halves(oT[:, j % 2, :]), zps(j % 2), ACT.Copy, scale=modT[:, 16 + j, B:B + 1])
                f(oS[:, j % 2, :], ps[:, 2 * (j % 2) + 1, HALF - B:HALF], ACT.Copy).then_inc(ot_act, 1)
                act.wait_ge(ot_act, j + 1)
                act.sem_inc(z_free, 1)
            act.wait_ge(y_acc, 2 + 8)
            for j in range(TT):
                chain(f(osq, xN[:, j, :], ACT.Square, accum_out=ss[:, j:j + 1]))
            f(osq[0:B, :], xs2, ACT.Square, accum_out=ss[0:B, 4:5]).then_inc(y_sq, 1)
            act.wait_ge(y_var, 1)
            f(ss[:, :], rstd[:, :], ACT.Sqrt).then_inc(y_std, 1)
            act.wait_ge(st_misc, 16 * 6)
            act.wait_ge(st_pre, 32)
            act.wait_ge(st_C, 16 + 16 * B)

        @block.gpsimd
        def _(pool):
            chain = Chain(pool, pool_chain)
            tt = nc.gpsimd.tensor_tensor

            def fill(ap, value, pattern, mult, op, other, base=0):
                chain(nc.gpsimd.memset(ap, value))
                return nc.gpsimd.affine_select(out=ap, in_=ap, compare_op=op, fill=other, base=base, pattern=pattern,
                                               channel_multiplier=mult)

            def low(j, n, quad):
                pool.wait_ge(hi_done, n + 1)
                tt(wL[:, j % 2], wraw[:, j % 4], wH[:, j % 2].bitcast(F32), ALU.subtract).then_inc(lo_done, 1)

            pool.sem_inc(lo_done, 4)
            pool.sem_inc(page_free[0], 1)
            pool.sem_inc(page_free[1], 1)
            pool.sem_inc(u_lo, 2)
            chain(fill(ident[:, :], 0.0, [[-1, P]], 1, ALU.not_equal, 1.0))
            nc.gpsimd.memset(ones[:, :], 1.0)
            chain(fill(cmask[:, :], 0.0, [[-1, P]], 1, ALU.is_ge, NEG))
            chain(fill(upper[:, :], 1.0, [[1, P]], -1, ALU.is_ge, 0.0))
            chain(fill(rowsel[:, :, :], 0.0, [[-1, B], [0, P]], 1, ALU.not_equal, 1.0))
            chain(fill(colsel[:, :, :], 0.0, [[1, B], [-1, B]], 0, ALU.not_equal, 1.0))
            chain(fill(earlier[:, :, :], 1.0, [[1, NBLK], [-1, NBLK]], 0, ALU.is_gt, 0.0))
            chain(nc.gpsimd.memset(headsel[:, :, :], 0.0))
            nc.gpsimd.memset(headsel[0:DH, 0, :], 1.0)
            chain(nc.gpsimd.memset(headsel[DH:P, 1, :], 1.0))
            chain(nc.gpsimd.memset(G[:, :, :], 0.0))
            nc.gpsimd.memset(yaS[:, :, :], 0.0).then_inc(consts, 1)
            pool.wait_ge(if_hi, 1)
            tt(wifL[:, :, :], wif[:, :, :], wifH[:, :, :].bitcast(F32), ALU.subtract).then_inc(if_lo, 1)
            for j in range(TT):
                pool.wait_ge(h_hi, j + 1)
                tok = slice(j * P, (j + 1) * P)
                tt(hL[:, :, tok], htmp[:, j % 2], hH[:, :, tok].bitcast(F32), ALU.subtract).then_inc(h_lo, 1)
            pool.wait_ge(h_hi, TT + 1)
            tt(hL[:, :, T:NT], hS[:, :, :], hH[:, :, T:NT].bitcast(F32), ALU.subtract).then_inc(h_lo, 1)
            for n in range(2):
                low(n, n, 0)

            with pool.Fori(0, PAIRS) as t:
                n, quad = T_ATT + 4 * t, t
                for j in range(4):
                    low((j + 2) % 4, n + j + 2, 0)
                    if j % 2 == 1:
                        s, e = 2 * j + 1, j // 2
                        pool.wait_ge(ld_page[1], 64 * (4 * t + s // 2 + 1))
                        pool.wait_ge(qbc_rdy, 2 * t + e + 1)
                        pool.wait_ge(pprod_free, 2 * t + e + 1)
                        tt(prodP.rearrange("p (g n) -> p g n", g=STEP_PAGES),
                           page[:, 1, :].rearrange("p (g n) -> p g n", g=STEP_PAGES),
                           qbc[:, e:e + 1, :].broadcast_to([P, STEP_PAGES, AW]), ALU.mult).then_inc(page_free[1], 1)
                        pool.wait_ge(page_free[1], 4 * t + s // 2 + 2)
                        pool.sem_inc(pprod_rdy, 1)
            pool.wait_ge(ya_done, 1 + PAIRS)
            pool.wait_ge(st_k, 16 * (1 + PAIRS))
            pool.wait_ge(st_v, 16 * (1 + PAIRS))
            nc.gpsimd.memset(v1[:, :, MV:MV + 1], 1.0).then_inc(v_one, 1)
            nc.gpsimd.memset(pre[:, :, 0:3], 0.0).then_inc(v_one, 1)
            pool.wait_ge(sel_dve, 8)
            with pool.Fori(0, MH) as h:
                n = T_ML + 8 * h
                for j in range(8):
                    if j == 2:
                        pool.wait_ge(w_exp, h + 1)
                    low((j + 2) % 4, n + j + 2, 0)
                    if j == 2:
                        diag = wt[:, :, 0:P]
                        nc.gpsimd.affine_select(out=diag, in_=diag, compare_op=ALU.is_ge, fill=0.0, base=0,
                                                pattern=[[0, TT], [1, P]], channel_multiplier=-1).then_inc(w_rdy, 1)
                    if j % 2 == 1:
                        pool.wait_ge(ld_page[1], 64 * (16 + 4 * h + j // 2 + 1))
                        pool.wait_ge(pprod_free, 8 + 4 * h + j // 2 + 1)
                        tt(prodP.rearrange("p (g n) -> p g n", n=DH),
                           page[:, 1, :].rearrange("p (g n) -> p g n", n=DH),
                           score[:, bass.ds((8 * h + j) * 32, 32)].unsqueeze(2).broadcast_to([P, 32, DH]),
                           ALU.mult).then_inc(page_free[1], 1)
                        pool.wait_ge(page_free[1], 16 + 4 * h + j // 2 + 2)
                        pool.sem_inc(pprod_rdy, 1)
            pool.wait_ge(sam_dve, 5)
            with pool.Fori(0, 4) as t:
                n = T_GATE + 4 * t
                for e in range(2):
                    low(2, n + 2 * e + 2, 0) if e == 0 else low(0, n + 4, 0)
                    low(3, n + 2 * e + 3, 0) if e == 0 else low(1, n + 5, 0)
                    pool.wait_ge(ld_C[e], 16 * t + 16)
                    pool.wait_ge(st_C, 32 * t + 16 * e + 16)
                    pool.wait_ge(c_used, 2 * t + e + 2)
                    tt(cW.rearrange("p (h n) -> p h n", h=MH), cS[:, e].rearrange("p (h n) -> p h n", h=MH),
                       abc[:, bass.ds(2 * t + e, 1), 0:MH].rearrange("p o h -> p (o h)").unsqueeze(2)
                       .broadcast_to([P, MH, 2 * MQ]), ALU.mult).then_inc(cw_rdy, 1)
            pool.wait_ge(ya_hi, 1)
            tt(yaL[:, :, :], yaT, yaH[:, :, :].bitcast(F32), ALU.subtract).then_inc(ya_lo, 1)
            with pool.Fori(0, 4) as t:
                n = T_COMB + 4 * t
                for j in range(4):
                    low((j + 2) % 4, n + j + 2, 0)
                    if j % 2 == 1:
                        c = j // 2
                        pool.wait_ge(u_hi, 2 * t + c + 1)
                        tt(uL[:, bass.ds(2 * t + c, 1), :].rearrange("p o n -> p (o n)"), uu[:, c, :],
                           uH[:, bass.ds(2 * t + c, 1), :].rearrange("p o n -> p (o n)").bitcast(F32),
                           ALU.subtract).then_inc(u_lo, 1)
            for j in range(6):
                low(j + 2, T_OUT + j + 2, 0)

        @block.vector
        def _(dve):
            chain = Chain(dve, dve_chain)
            v = nc.vector
            tt = v.tensor_tensor

            def over(ap, n):
                return ap.unsqueeze(len(ap.shape)).broadcast_to(list(ap.shape) + [n])

            dve.sem_inc(pprod_free, 1)
            dve.sem_inc(ya_done, 1)
            dve.sem_inc(ym_done, 1)
            dve.sem_inc(c_used, 2)
            dve.sem_inc(kq_used, 2)
            dve.sem_inc(y_acc, 2)
            chain(v.memset(ss[:, :], 1.0))
            dve.wait_ge(c_sig, 1)
            tt(cN, cN, cSg, ALU.mult).then_inc(c_silu, 1)
            dve.wait_ge(t_vec, 1)
            v.tensor_copy(vcol[:, :], ps[:, 5, 0:V_ROWS]).then_inc(v_col, 1)
            dve.wait_ge(t_c, 1)
            v.tensor_copy(cT.rearrange("p k n -> p (k n)"), ps[:, 4, 0:9 * KT]).then_inc(c_T, 1)
            dve.wait_ge(x_sq, 1)
            v.tensor_scalar(rstd[:, :], ss[:, :], 1.0 / D, EPS, ALU.mult, ALU.add).then_inc(x_var, 1)
            dve.wait_ge(x_std, 1)
            chain(v.reciprocal(rstd[:, :], ss[:, :]))
            for j in range(TT):
                v.tensor_scalar(xt[:, j, :], xt[:, j, :], rstd[:, j:j + 1], None, ALU.mult)
            v.tensor_scalar(xsN, xsN, rstd[0:B, 4:5], None, ALU.mult).then_inc(x_nrm, 1)
            dve.wait_ge(t_mod, 1)
            chain(tt(modT[:, 0:16, :], ps[:, 5, 0:144].rearrange("p (k n) -> p k n", n=9),
                     over(vcol[:, V_BA:V_BA + 16], 9), ALU.add))
            v.scalar_tensor_tensor(hscale[:, :, :], modT[:, 8:16, :], 1.0, over(vcol[:, V_G:V_G + KT], 9),
                                   ALU.add, ALU.mult).then_inc(mod_rdy, 1)
            dve.wait_ge(t_mod, 2)
            tt(modT[:, 16:24, :], ps[:, 4, 0:72].rearrange("p (k n) -> p k n", n=9),
               over(vcol[:, V_BA + 16:V_BA + 24], 9), ALU.add).then_inc(mod_rdy, 1)
            dve.wait_ge(mod_rdy, 2)
            for j in range(TT):
                b = 2 if j % 2 == 0 else 6
                dve.wait_ge(t_x, j + 1)
                if j >= 2:
                    dve.wait_ge(h_lo, j - 1)
                chain(tt(htmp[:, j % 2], ps[:, b:b + 2, :].rearrange("p a (k n) -> p (a k) n", n=P),
                         over(hscale[:, :, B], P), ALU.mult))
                tt(htmp[:, j % 2], htmp[:, j % 2], over(modT[:, 0:KT, B], P), ALU.add).then_inc(h_rdy, 1)
            dve.wait_ge(t_x, TT + 1)
            chain(tt(hS[:, :, :], ps[:, 4, 0:B * KT].rearrange("p (k n) -> p k n", n=B), hscale[:, :, 0:B], ALU.mult))
            tt(hS[:, :, :], hS[:, :, :], modT[:, 0:KT, 0:B], ALU.add).then_inc(h_rdy, 1)
            dve.wait_ge(g_mm, 1)
            dve.wait_ge(ld_small, 64)
            tt(G[:, 0:TT, :], ps[:, 1, 0:32].rearrange("p (j n) -> p j n", n=8),
               bif[:, :].unsqueeze(1).broadcast_to([P, TT, 8]), ALU.add)
            tt(G[0:B, TT, :], ps[0:B, 1, 32:40], bif[0:B, :], ALU.add).then_inc(g_dve, 1)
            dve.wait_ge(g_dve, 1)
            ig, fg_ = G[:, :, 0:MH], G[:, :, MH:2 * MH]
            chain(v.tensor_scalar(gf[:, :, :], fg_, -1.0, None, ALU.mult))
            tt(gf[:, :, :], gf[:, :, :], fg_, ALU.min).then_inc(g_dve, 1)
            dve.wait_ge(g_act, 1)
            v.scalar_tensor_tensor(lf[:, :, :], fg_, 0.0, gf[:, :, :], ALU.min, ALU.subtract).then_inc(g_dve, 1)
            dve.wait_ge(g_dve, 3)
            dve.wait_ge(g_pe, 1)
            chain(v.tensor_copy(bc[:, :, :].rearrange("p j h -> p (j h)"), ps[:, 5, 0:16]))
            tt(ec[:, :, :], G[:, 0:TT, 0:MH], bc[:, :, :], ALU.subtract).then_inc(g_dve, 1)
            dve.wait_ge(g_pe, 2)
            chain(v.tensor_copy(eR, ps[0:MH, 6, :]))
            v.tensor_tensor_scan(MR[:, :], eR, eR, 0.0, ALU.max, ALU.max).then_inc(g_dve, 1)
            dve.wait_ge(g_pe, 3)
            tt(mt[:, :, :].rearrange("p j h -> p (j h)"), ps[:, 4, 0:16], bc[:, :, :].rearrange("p j h -> p (j h)"),
               ALU.add).then_inc(g_dve, 1)
            chain(tt(gs[:, 0, :], lf[0:B, TT, :], m0[:, :], ALU.add))
            chain(tt(gs[:, 1, :], gs[:, 0, :], G[0:B, TT, 0:MH], ALU.max))
            tt(aw[:, 0, :], gs[:, 0, :], gs[:, 1, :], ALU.subtract)
            tt(aw[:, 1, :], G[0:B, TT, 0:MH], gs[:, 1, :], ALU.subtract).then_inc(g_dve, 1)

            def causal_max(e, t):
                dve.wait_ge(qk_done, 2 * t + e + 1)
                for q, b, c in ((3, 4, 0), (2, 5, 0), (0, 5, 384), (1, 6, 0)):
                    own = ps[:, b, c + q * P:c + (q + 1) * P]
                    last = tt(own, own, cmask[:, :], ALU.add)
                chain(last)
                for q, b, c in ((3, 4, 0), (2, 5, 0), (0, 5, 384), (1, 6, 0)):
                    last = v.tensor_reduce(mx[:, e, q:q + 1], ps[:, b, c:c + (q + 1) * P], AX, ALU.max)
                chain(last)
                v.tensor_scalar(nmx[:, e, :], mx[:, e, :], -SCALE, None, ALU.mult).then_inc(smx, 1)

            def normalise(e, t):
                dve.wait_ge(sexp, 2 * t + e + 1)
                chain(v.reciprocal(rinv[:, e, :], rsum[:, e, :]))
                for q in range(TT):
                    last = v.tensor_scalar(prA[:, e, q, 0:(q + 1) * P], prA[:, e, q, 0:(q + 1) * P],
                                           rinv[:, e, q:q + 1], None, ALU.mult)
                last.then_inc(pnorm, 1)

            def key_step(s, t):
                out = score[:, bass.ds((8 * t + s) * 32, 32)]
                if s % 4 == 3:
                    dve.wait_ge(pprod_rdy, 2 * t + s // 4 + 1)
                    v.tensor_reduce(out, prodP.rearrange("p (g n) -> p g n", n=DH), AX, ALU.add)\
                        .then_inc(pprod_free, 1)
                    return
                count = 4 * t + s // 2
                dve.wait_ge(ld_page[s % 2], 64 * (count + 1))
                dve.wait_ge(qbc_rdy, 2 * t + s // 4 + 1)
                tt(prodD.rearrange("p (g n) -> p g n", g=STEP_PAGES),
                   page[:, s % 2, :].rearrange("p (g n) -> p g n", g=STEP_PAGES),
                   qbc[:, s // 4:s // 4 + 1, :].broadcast_to([P, STEP_PAGES, AW]), ALU.mult)\
                    .then_inc(page_free[s % 2], 1)
                dve.wait_ge(page_free[s % 2], count + 2)
                chain(v.tensor_reduce(out, prodD.rearrange("p (g n) -> p g n", n=DH), AX, ALU.add))

            with dve.Fori(0, PAIRS) as t:
                n = T_ATT + 4 * t
                chain.loop(t, 2 * 3 + 6 + 1)
                for e in range(2):
                    v.tensor_copy(selc[0:B, e, :], rowsel[:, bass.ds(2 * t + e, 1), :].rearrange("p o n -> p (o n)"))\
                        .then_inc(selc_rdy, 1)
                key_step(0, t)
                key_step(1, t)
                causal_max(0, t)
                key_step(2, t)
                normalise(0, t)
                key_step(3, t)
                for i, src, at in ((0, qT, 3), (1, kT, 4), (2, vT, 5)):
                    dve.wait_ge(z_free, n + at)
                    v.tensor_copy(qkvS[:, i, bass.ds(t, 1), :].rearrange("p o n -> p (o n)"), src[:, T:NT])
                causal_max(1, t)
                key_step(4, t)
                normalise(1, t)
                for s in (5, 6, 7):
                    key_step(s, t)
                dve.wait_ge(z_free, n + 6)
                ya = yaT[:, bass.ds(t, 1), :].rearrange("p o n -> p (o n)")
                chain(tt(ya, azr, azs, ALU.mult))
                dve.wait_ge(pv_done, t + 1)
                ya = yaT[:, bass.ds(t, 1), 0:T].rearrange("p o n -> p (o n)")
                tt(ya, ya, ps[:, 7, :], ALU.mult).then_inc(ya_done, 1)
            chain.end(PAIRS)

            dve.wait_ge(ya_done, 1 + PAIRS)
            tt(tS[:, :, :], qkvS[:, 0], qkvS[:, 1], ALU.mult).then_inc(sel_dve, 1)
            dve.wait_ge(pprod_free, 1 + 2 * PAIRS)
            dve.wait_ge(sel_dve, 1)
            dve.sem_inc(sel_dve, 1)
            dve.wait_ge(sel_pe, 1)
            chain(v.tensor_copy(selfp[:, :, :].rearrange("p b (t e) -> p e t b", e=2),
                                ps[:, 4, 0:64].rearrange("p (e t b) -> p e t b", e=2, t=PAIRS)))
            dve.wait_ge(sel_pe, 3)
            chain(v.tensor_reduce(bsum[:, :, :], ps[0:B, 7, 0:P].rearrange("p (n w h) -> p h n w", n=NBLK, w=2),
                                  AX, ALU.add))
            sm = bsum[:, :, :].unsqueeze(2).broadcast_to([B, AH, NBLK, NBLK])
            sn = bsum[:, :, :].unsqueeze(3).broadcast_to([B, AH, NBLK, NBLK])
            tt(cmpA, sm, sn, ALU.is_gt)
            chain(tt(cmpB, sm, sn, ALU.is_equal))
            chain(tt(cmpB, cmpB, earlier[:, :, :].unsqueeze(1).broadcast_to([B, AH, NBLK, NBLK]), ALU.mult))
            chain(tt(cmpA, cmpA, cmpB, ALU.add))
            chain(v.tensor_reduce(pen[:, :].rearrange("p (h n) -> p h n", n=NBLK), cmpA, AX, ALU.add))
            chain(v.tensor_scalar(pen[:, :], pen[:, :], float(TOPK), NEG, ALU.is_ge, ALU.mult))
            tt(pend, pen[:, :].unsqueeze(1).broadcast_to([B, B, AH * NBLK]), over(ident[0:B, 0:B], AH * NBLK),
               ALU.mult).then_inc(sel_dve, 1)
            dve.wait_ge(sel_pe, 4)
            sc = score.rearrange("p (b n w h) -> p b n w h", b=B, n=NBLK, w=2)
            for w in range(2):
                last = tt(sc[:, :, :, w, :], sc[:, :, :, w, :],
                          ps[:, 7, :].rearrange("p (b h n) -> p b n h", b=B, h=AH), ALU.add)
            chain(last)
            by_bh = score.rearrange("p (b g h) -> p b h g", b=B, g=PAGES)
            mx3 = mxA[:, :].rearrange("p (b h) -> p b h", b=B)
            v.tensor_reduce(mx3, by_bh, AX, ALU.max).then_inc(sel_dve, 1)
            dve.wait_ge(sel_pe, 5)
            chain(v.tensor_reduce(mx64[:, :], ps[0:B * AH, 4, 0:P], AX, ALU.max))
            v.tensor_scalar(dg64[:, :], ident[0:B * AH, 0:B * AH], mx64[:, 0:1], None, ALU.mult).then_inc(sel_dve, 1)
            dve.wait_ge(sel_pe, 6)
            chain(tt(mx3, ps[:, 4, 128:192].rearrange("p (b h) -> p b h", b=B), selfp[:, :, :], ALU.max))
            tt(by_bh, by_bh, over(mx3, PAGES), ALU.subtract)
            tt(selfp[:, :, :], selfp[:, :, :], mx3, ALU.subtract).then_inc(sel_dve, 1)
            dve.wait_ge(sel_act, 2)
            v.tensor_reduce(mx3, by_bh, AX, ALU.add).then_inc(sel_dve, 1)
            dve.wait_ge(sel_pe, 7)
            chain(tt(mx3, ps[:, 4, 256:320].rearrange("p (b h) -> p b h", b=B), selfp[:, :, :], ALU.add))
            chain(v.reciprocal(mx3, mx3))
            tt(by_bh, by_bh, over(mx3, PAGES), ALU.mult)
            tt(selfp[:, :, :], selfp[:, :, :], mx3, ALU.mult).then_inc(sel_dve, 1)
            dve.wait_ge(sel_dve, 8)
            dve.sem_inc(vsum_rdy, 1)

            def value_step(s, h):
                if s % 2 == 0:
                    count = 16 + 4 * h + s // 2
                    prod = prodD
                    dve.wait_ge(ld_page[0], 64 * (count + 1))
                    tt(prod.rearrange("p (g n) -> p g n", n=DH), page[:, 0, :].rearrange("p (g n) -> p g n", n=DH),
                       over(score[:, bass.ds((8 * h + s) * 32, 32)], DH), ALU.mult).then_inc(page_free[0], 1)
                    dve.wait_ge(page_free[0], count + 2)
                else:
                    prod = prodP
                    dve.wait_ge(pprod_rdy, 8 + 4 * h + s // 2 + 1)
                chain(tt(prod[:, 0:1024], prod[:, 0:1024], prod[:, 1024:2048], ALU.add))
                acc = vacc[:, s // 4, :]
                if s % 4 == 0:
                    dve.wait_ge(ys_mm, h + 1)
                    chain(tt(acc, prod[:, 0:512], prod[:, 512:1024], ALU.add))
                    return
                chain(tt(prod[:, 0:512], prod[:, 0:512], prod[:, 512:1024], ALU.add))
                ins = tt(acc, acc, prod[:, 0:512], ALU.add)
                chain(ins)
                if s % 2 == 1:
                    dve.sem_inc(pprod_free, 1)
                if s == 7:
                    dve.sem_inc(vsum_rdy, 1)

            dve.wait_ge(st_k, 16 * (1 + PAIRS))
            dve.wait_ge(st_v, 16 * (1 + PAIRS))
            dve.wait_ge(v_one, 2)
            with dve.Fori(0, MH) as h:
                n = T_ML + 8 * h
                chain.loop(h, 2 * 3 + 2 * 2 + 6 * 3 + 6 + 2 + 4)
                v.tensor_copy(selm, rowsel[0:MH, bass.ds(h, 1), :].rearrange("p o n -> p (o n)")).then_inc(selm_rdy, 1)
                for e in range(2):
                    dve.wait_ge(z_free, n + 3 + e)
                    acc = cacc[:, e, :]

                    def tap(j):
                        return vcol[:, bass.ds(h + (V_WC + KT * j + MH * e), 1)]

                    chain(v.tensor_scalar(acc, pre[:, e, 0:T], tap(0), vcol[:, bass.ds(h + (V_BC + MH * e), 1)],
                                          ALU.mult, ALU.add))
                    for j in range(1, 4):
                        last = v.scalar_tensor_tensor(acc, pre[:, e, j:j + T], tap(j), acc, ALU.mult, ALU.add)
                        if j < 3:
                            chain(last)
                    last.then_inc(cv_rdy, 1)
                    v.tensor_copy(preS[:, bass.ds(h + MH * e, 1), :].rearrange("p o n -> p (o n)"),
                                  pre[:, e, T:T + 11])
                dve.wait_ge(mb_mm, h + 1)
                dve.wait_ge(w_exp, h + 1)
                v.tensor_scalar(dl[:, 0, :], ec[:, :, bass.ds(h, 1)].rearrange("p j o -> p (j o)"),
                                ps[:, 7, T - 1:T], None, ALU.subtract).then_inc(mlast_rdy, 1)
                value_step(0, h)
                dve.wait_ge(sg_rdy, 2 * h + 2)
                tt(qkc[:, 0, :], qkc[:, 0, :], cacc[:, 0, :], ALU.mult)
                v.scalar_tensor_tensor(qkc[:, 1, :], cacc[:, 1, :], KSCALE, qkc[:, 1, :], ALU.mult, ALU.mult)\
                    .then_inc(qk_rdy, 1)
                value_step(1, h)
                dve.wait_ge(st_mm, h + 1)
                dve.wait_ge(w_rdy, h + 1)
                for k, b, c in ((0, 4, 0), (1, 5, 0), (3, 5, 384), (2, 6, 0)):
                    last = tt(wt[:, k, 0:T - k * P], wt[:, k, 0:T - k * P], ps[:, b, c:c + T - k * P], ALU.mult)
                last.then_inc(mpt_rdy, 1)
                dve.wait_ge(z_free, n + 6)
                v.tensor_copy(vS[:, bass.ds(2 * h, 2), :], mvT[:, :, T:NT])
                value_step(2, h)
                dve.wait_ge(kt_mm, h + 1)
                dve.wait_ge(wsc_rdy, h + 1)
                tt(kw, ps[:, 6, :].rearrange("p (j n) -> p j n", j=TT), over(wsc[:, :], P), ALU.mult)\
                    .then_inc(kw_rdy, 1)
                value_step(3, h)
                dve.wait_ge(hn_ev, 4 * h + 5)
                den = hn[:, :, MV]
                chain(v.tensor_scalar(dl[:, 1, :], den, -1.0, None, ALU.mult))
                chain(tt(dl[:, 1, :], dl[:, 1, :], den, ALU.max))
                chain(tt(dl[:, 1, :], dl[:, 1, :], em[:, :, bass.ds(h, 1)].rearrange("p j o -> p (j o)"), ALU.max))
                chain(v.reciprocal(dl[:, 2, :], dl[:, 1, :]))
                chain(tt(dl[:, 3, :], dl[:, 2, :], dl[:, 2, :], ALU.mult))
                chain(tt(dl[:, 3, :], dl[:, 3, :], ssm[:, :], ALU.mult))
                v.tensor_scalar(dl[:, 3, :], dl[:, 3, :], 1.0 / MV, EPS, ALU.mult, ALU.add).then_inc(rs1_rdy, 1)
                dve.wait_ge(rs2_rdy, h + 1)
                chain(v.reciprocal(dl[:, 3, :], dl[:, 1, :]))
                chain(tt(dl[:, 3, :], dl[:, 3, :], dl[:, 2, :], ALU.mult))
                tt(hn[:, :, 0:MV], hn[:, :, 0:MV], over(dl[:, 3, :], MV), ALU.mult).then_inc(hn_rdy, 1)
                value_step(4, h)
                value_step(5, h)
                for u in range(2):
                    dve.wait_ge(z_free, n + 9 + u)
                    chain(v.scalar_tensor_tensor(go[:, u, :], go[:, u, :], vcol[:, bass.ds(2 * h + (V_MG + u), 1)],
                                                 gzs[:, u, :], ALU.mult, ALU.mult))
                    chain(tt(go[:, u, :], go[:, u, :], gz[:, u, :], ALU.mult))
                v.tensor_copy(ymT[:, bass.ds(2 * h, 2), T:NT], go[:, :, T:NT])
                dve.wait_ge(ht_mm, h + 1)
                tt(ymT[:, bass.ds(2 * h, 2), 0:T], ps[:, 4:6, :], go[:, :, 0:T], ALU.mult).then_inc(ym_done, 1)
                value_step(6, h)
                value_step(7, h)
            chain.end(MH)

            dve.wait_ge(ym_done, 1 + MH)
            awf = aw[:, :, :].rearrange("p a h -> p (a h)")
            dve.wait_ge(g_act, 3)
            tt(dgS[:, :, :], awf.unsqueeze(1).broadcast_to([B, B, 2 * MH]), over(ident[0:B, 0:B], 2 * MH), ALU.mult)\
                .then_inc(sam_dve, 1)
            st3 = stT[:, :, :].rearrange("p k (b j) -> p k b j", j=3)
            chain(tt(cvS[:, :, :], preS[:, :, 3:11], over(vcol[:, V_WC + 3 * KT:V_WC + 4 * KT], B), ALU.mult))
            for j in range(3):
                chain(tt(cvT[:, :, :], st3[:, :, :, j], over(vcol[:, V_WC + j * KT:V_WC + (j + 1) * KT], B), ALU.mult))
                chain(tt(cvS[:, :, :], cvS[:, :, :], cvT[:, :, :], ALU.add))
            tt(cvS[:, :, :], cvS[:, :, :], over(vcol[:, V_BC:V_BC + KT], B), ALU.add).then_inc(sam_dve, 1)
            dve.wait_ge(sam_act, 1)
            tt(cvS[:, 0:MH, :], cvS[:, 0:MH, :], cvG[:, 0:MH, :], ALU.mult)
            v.scalar_tensor_tensor(cvS[:, MH:KT, :], cvS[:, MH:KT, :], KSCALE, cvG[:, MH:KT, :], ALU.mult, ALU.mult)\
                .then_inc(sam_dve, 1)
            dve.wait_ge(sam_pe, 1)
            chain(v.tensor_copy(abc[:, :, :].rearrange("p b n -> p (b n)"), ps[:, 7, 0:64]))
            v4 = vS[:, :, :].rearrange("p (h u) b -> p h u b", u=2)
            chain(tt(v4, v4, abc[:, :, MH:2 * MH].rearrange("p b h -> p h b").unsqueeze(2).broadcast_to([P, MH, 2, B]),
                     ALU.mult))
            dve.wait_ge(sam_act, 3)
            dve.wait_ge(ld_n, 16)
            kS = kqN[:, 0:AW].rearrange("p (h n) -> p h n", h=MH)
            qS = kqN[:, AW:2 * AW].rearrange("p (h n) -> p h n", h=MH)
            tt(nT, kS, over(aw[:, 1, :], MQ), ALU.mult)
            chain(tt(nN, nN, over(aw[:, 0, :], MQ), ALU.mult))
            chain(tt(nN, nN, nT, ALU.add))
            chain(tt(nT, nN, qS, ALU.mult))
            chain(v.tensor_reduce(dS[:, 0, :], nT, AX, ALU.add))
            chain(v.tensor_scalar(dS[:, 1, :], dS[:, 0, :], -1.0, None, ALU.mult))
            chain(tt(dS[:, 1, :], dS[:, 1, :], dS[:, 0, :], ALU.max))
            chain(tt(dS[:, 1, :], dS[:, 1, :], gs[:, 2, :], ALU.max))
            chain(v.reciprocal(dS[:, 2, :], dS[:, 1, :]))
            tt(dgS[:, :, 0:MH], dS[:, 2, :].unsqueeze(1).broadcast_to([B, B, MH]), over(ident[0:B, 0:B], MH), ALU.mult)\
                .then_inc(sam_dve, 1)
            dve.wait_ge(sam_pe, 4)
            v.tensor_copy(rbc[:, :, :].rearrange("p b n -> p (b n)"), ps[:, 7, 64:96]).then_inc(sam_dve, 1)
            dve.wait_ge(ys_ev, 1 + MH)
            sp_t = selfp[:, :, :].rearrange("p b (t e) -> p e t b", e=2)
            for e in range(2):
                r = slice(DH * e, DH * e + DH)
                last = tt(tS[r], qkvS[r, 2], sp_t[r, e], ALU.mult)
            chain(last)
            chain(tt(tS[:, :, :], tS[:, :, :], yaS[:, :, 2:2 + B], ALU.add))
            chain(tt(yaT[:, :, T:NT], yaT[:, :, T:NT], tS[:, :, :], ALU.mult))

            with dve.Fori(0, 4) as t:
                chain.loop(t, 2 * 1)
                for e in range(2):
                    v.tensor_copy(selg[0:B, e, :], rowsel[:, bass.ds(2 * t + e, 1), :].rearrange("p o n -> p (o n)"))\
                        .then_inc(selg_rdy, 1)
                for e in range(2):
                    dve.wait_ge(kq_mm, 2 * t + e + 1)
                    dve.wait_ge(cw_rdy, 2 * t + e + 1)
                    four = cS[:, e].rearrange("p (h u n) -> p h u n", h=MH, u=2)
                    key = ps[:, 4 + 2 * e, :].rearrange("p (h n) -> p h n", h=MH).unsqueeze(2)
                    query = ps[:, 5 + 2 * e, :].rearrange("p (h n) -> p h n", h=MH).unsqueeze(2)
                    val = vS[:, :, bass.ds(2 * t + e, 1)].rearrange("p (h u) o -> p h (u o)", u=2)
                    chain(tt(four, key.broadcast_to([P, MH, 2, MQ]), over(val, MQ), ALU.mult))
                    tt(cW, cW, cS[:, e], ALU.add).then_inc(cnew_rdy, 1)
                    dve.wait_ge(cnew_rdy, 2 * t + e + 1)
                    tt(four, cW.rearrange("p (h u n) -> p h u n", h=MH, u=2), query.broadcast_to([P, MH, 2, MQ]),
                       ALU.mult).then_inc(kq_used, 1)
                    dve.wait_ge(kq_used, 2 * t + e + 3)
                    v.tensor_reduce(Cq[:, :, bass.ds(2 * t + e, 1)].rearrange("p k o -> p (k o)"),
                                    cS[:, e].rearrange("p (k n) -> p k n", k=KT), AX, ALU.add).then_inc(c_used, 1)
            chain.end(4)
            dve.wait_ge(c_used, 2 + B)
            C4 = Cq[:, :, :].rearrange("p (h u) b -> p h u b", u=2)
            chain(tt(C4, C4, rbc[:, :, :].rearrange("p b h -> p h b").unsqueeze(2).broadcast_to([P, MH, 2, B]), ALU.mult))
            tt(sqS[:, :, :], Cq[:, :, :], Cq[:, :, :], ALU.mult).then_inc(fin_dve, 1)
            dve.wait_ge(fin_pe, 1)
            chain(v.tensor_reduce(rmsS[:, :, :], ps[:, 4, 0:64].rearrange("p (h u b) -> p h b u", u=2, b=B), AX, ALU.add))
            v.tensor_scalar(rmsS[:, :, :], rmsS[:, :, :], 1.0 / MV, EPS, ALU.mult, ALU.add).then_inc(fin_dve, 1)
            dve.wait_ge(fin_act, 1)
            chain(v.reciprocal(rmsS[:, :, :], rmsS[:, :, :]))
            chain(tt(C4, C4, rmsS[:, :, :].unsqueeze(2).broadcast_to([P, MH, 2, B]), ALU.mult))
            tt(ymT[:, :, T:NT], ymT[:, :, T:NT], Cq[:, :, :], ALU.mult).then_inc(fin_dve, 1)
            dve.wait_ge(ym_hi, 1)
            tt(hL[:, :, :], ymT, hH[:, :, :].bitcast(F32), ALU.subtract).then_inc(ym_lo, 1)

            dve.wait_ge(st_C, 16 + 16 * B)
            with dve.Fori(0, 4) as t:
                n = T_COMB + 4 * t
                for c in range(2):
                    ga = sga[:, bass.ds(2 * t + c, 1), :].rearrange("p o (a n) -> p (o a) n", a=2)
                    gm = sgm[:, bass.ds(2 * t + c, 1), :].rearrange("p o (a n) -> p (o a) n", a=2)
                    dve.wait_ge(u_lo, 2 * t + c + 1)
                    dve.wait_ge(z_done, n + 2 * c + 3)
                    tt(halves(utmp[:, c, :]), zps(0), ga, ALU.mult).then_inc(z_free, 1)
                    dve.wait_ge(z_done, n + 2 * c + 4)
                    tt(halves(uu[:, c, :]), zps(1), gm, ALU.mult).then_inc(z_free, 1)
                    dve.wait_ge(z_free, n + 2 * c + 4)
                    tt(uu[:, c, :], uu[:, c, :], utmp[:, c, :], ALU.add).then_inc(uu_rdy, 1)

            def gated_sample(j):
                dve.wait_ge(ot_act, j + 1)
                tt(oT[:, j % 2, T:NT], oS[:, j % 2, :], modT[:, 16 + j, 0:B], ALU.mult).then_inc(ot_rdy, 1)

            dve.wait_ge(ld_xo, 48)
            for j in range(8):
                gated_sample(j)
                s = j % 2
                col = slice(j * P, (j + 1) * P)
                dve.wait_ge(ot_mm, j + 1)
                tt(xN[:, :, col], xN[:, :, col], ps[:, 4 + 2 * s, :].rearrange("p (i n) -> p i n", i=TT), ALU.add)
                tt(xs2[:, col], xs2[:, col], ps[0:B, 5 + 2 * s, 0:P], ALU.add).then_inc(y_acc, 1)
            dve.wait_ge(y_sq, 1)
            v.tensor_scalar(rstd[:, :], ss[:, :], 1.0 / D, EPS, ALU.mult, ALU.add).then_inc(y_var, 1)
            dve.wait_ge(y_std, 1)
            chain(v.reciprocal(rstd[:, :], ss[:, :]))
            for j in range(TT):
                v.scalar_tensor_tensor(xN[:, j, :], xN[:, j, :], rstd[:, j:j + 1], fg, ALU.mult, ALU.mult)\
                    .then_inc(y_rdy, 1)
            v.scalar_tensor_tensor(xs2, xs2, rstd[0:B, 4:5], fg[0:B, :], ALU.mult, ALU.mult).then_inc(y_rdy, 1)

_INS = ["x_prompt", "x_sample", "cache_k", "cache_v", "state_C", "state_n", "state_m", "state_conv",
        "page_table", "c_prompt", "c_sample", "w_ada", "b_ada", "norm_g", "w_in", "b_if", "w_conv",
        "b_conv", "m_norm_g", "w_att", "w_mlstm", "w_out", "final_g"]
_OUTS = [("y_p", (1, T, D)), ("y_s", (B, 1, D)),
         ("k_p", (1, 1, T, AH, DH)), ("v_p", (1, 1, T, AH, DH)),
         ("C_p", (1, 1, MH, MV, MQ)), ("n_p", (1, 1, MH, MQ)), ("m_p", (1, 1, MH)),
         ("conv_p", (1, 1, 3, D)),
         ("k_s", (1, B, 1, AH, DH)), ("v_s", (1, B, 1, AH, DH)),
         ("C_s", (1, B, MH, MV, MQ)), ("n_s", (1, B, MH, MQ)), ("m_s", (1, B, MH)),
         ("conv_s", (1, B, 3, D))]


def kernel(**inputs):
    import numpy as np
    import concourse.bacc as bacc
    from concourse.bass_utils import run_bass_kernel_spmd

    nc = bacc.Bacc("TRN2", target_bir_lowering=False, num_devices=1)
    arrays, ins, outs = {}, {}, {}
    for name in _INS:
        a = np.ascontiguousarray(inputs[name])
        arrays["in_" + name] = a
        ins[name] = nc.dram_tensor("in_" + name, a.shape, mybir.dt.from_np(a.dtype), kind="ExternalInput").ap()
    for name, shape in _OUTS:
        outs[name] = nc.dram_tensor("out_" + name, shape, F32, kind="ExternalOutput").ap()
    decoder_step(nc, ins, outs)
    r = run_bass_kernel_spmd(nc, [arrays], core_ids=[0])
    return tuple(r.results[0]["out_" + name] for name, _ in _OUTS)
```

```python
from contextlib import ExitStack

import concourse.bass as bass
from concourse import mybir

ALU = mybir.AluOpType
ACT = mybir.ActivationFunctionType
F32 = mybir.dt.float32
F32R = mybir.dt.float32r
I32 = mybir.dt.int32
AX = mybir.AxisListType.X

P = 128
D = 1024
KT = D // P
T = 512
TT = T // P
B = 8
NT = T + B
HALF = NT // 2
AH, DH = 8, 64
AW = AH * DH
PAIRS = AW // P
MH, MQ, MV = 4, 128, 256
PAGE, PAGES = 128, 16
NBLK = 8
TOPK = 3
EPS = 1e-6
NEG = -1e30
SCALE = DH ** -0.5
KSCALE = MQ ** -0.5

CQ, CK, CV, CZ = 0, 512, 1024, 1536
CMQK, CMV, CMO, CMZ = 2048, 3072, 4096, 5120
CIF, CGA, CGM = 6144, 6152, 7176

T_ATT, T_ML = 0, 16
T_GATE = T_ML + 32
T_WA = T_GATE + 16
T_WM = T_WA + 8
T_OUT = T_WM + 8
T_ALL = T_OUT + 8

STEP_PAGES = 4
KV_SLOTS = 4
V_G, V_MG, V_BC, V_WC, V_BA = 0, 8, 16, 24, 56
V_ROWS = V_BA + 24


class Chain:

    def __init__(self, eng, sem):
        self.eng, self.sem, self.base, self.k = eng, sem, 0, 0

    def __call__(self, ins):
        ins.then_inc(self.sem, 1)
        self.k += 1
        self.eng.wait_ge(self.sem, self.base + self.k)

    def loop(self, i, per):
        self.start = self.base + self.k
        self.base, self.k, self.per = self.start + i * per, 0, per

    def end(self, trips):
        assert self.k == self.per, (self.k, self.per)
        self.base, self.k = self.start + trips * self.per, 0


def decoder_step(nc, I, O):
    x_p = I["x_prompt"].rearrange("b s d -> (b s) d")
    x_s = I["x_sample"].rearrange("b s d -> (b s) d")
    w_in = I["w_in"][0].rearrange("(k p) n -> p k n", p=P)
    w_ada = I["w_ada"][0].rearrange("(k p) n -> p k n", p=P)
    w_att = I["w_att"][0].rearrange("(k p) n -> p k n", p=P)
    w_ml = I["w_mlstm"][0].rearrange("(k p) n -> p k n", p=P)
    w_out = I["w_out"][0].rearrange("(k p) n -> p k n", p=P)
    pages_k = I["cache_k"][0].rearrange("n t h d -> t n (h d)")
    pages_v = I["cache_v"][0].rearrange("n t h d -> t n (h d)")
    state_c = I["state_C"][0].rearrange("b h (u v) d -> v b (h u) d", v=P)
    new_c = O["C_s"][0].rearrange("b h (u v) d -> v b (h u) d", v=P)
    n_phys = I["cache_k"].shape[1]

    with ExitStack() as ctx:
        names = set()

        def sb(name, shape, dt=F32):
            return ctx.enter_context(nc.sbuf_tensor("sb_" + name, shape, dt))

        def sem(name):
            assert name not in names
            names.add(name)
            return ctx.enter_context(nc.semaphore(name))

        ps = ctx.enter_context(nc.psum_tensor("ps", [P, 8, 512], F32))

        def zps(slot):
            return ps[:, 2 * slot:2 * slot + 2, 0:HALF]

        def halves(ap):
            return ap.rearrange("p (a n) -> p a n", a=2)

        ident = sb("ident", [P, P])
        ones = sb("ones", [P, P])
        cmask = sb("cmask", [P, P])
        upper = sb("upper", [P, P])
        rowsel = sb("rowsel", [B, B + 2, P])
        colsel = sb("colsel", [P, B, B])
        earlier = sb("earlier", [B, NBLK, NBLK])
        headsel = sb("headsel", [P, 2, P])
        vcol = sb("vcol", [P, V_ROWS])
        modT = sb("modT", [P, 24, 9])
        hscale = sb("hscale", [P, KT, 9])
        ptab = sb("ptab", [1, B * PAGES], I32)
        bif = sb("bif", [P, 2 * MH])
        hH = sb("hH", [P, KT, NT], F32R)
        hL = sb("hL", [P, KT, NT], F32R)
        hS = sb("hS", [P, KT, B])
        wraw = sb("wraw", [P, 4, KT, P])
        wH = sb("wH", [P, 2, KT, P], F32R)
        wL = sb("wL", [P, 2, KT, P], F32R)
        with nc.sbuf_tensor("sb_gated", [P, 6240], F32) as gated:
            pass
        ymT = gated[:, 0:4160].rearrange("p (k n) -> p k n", k=KT)
        yaT = gated[:, 4160:6240].rearrange("p (k n) -> p k n", k=PAIRS)
        uH = sb("uH", [P, KT, NT], F32R)
        sb("uH_rest", [P, 2080])
        mod = gated[0:9, 0:3072]
        cN = gated[0:9, 3072:4096]
        stC = gated[0:3 * B, 5184:6208]
        with nc.sbuf_tensor("sb_arenaA", [P, 10240], F32) as arenaA:
            pass
        page = arenaA[:, 0:8192].rearrange("p (s n) -> p s n", s=KV_SLOTS)
        qbc = arenaA[:, 8192:9216].rearrange("p (s n) -> p s n", s=2)
        vacc = qbc
        score = arenaA[:, 9216:10240]
        ada = arenaA[:, 0:8192].rearrange("p (s k n) -> p s k n", s=2, k=KT)
        yaH = sb("yaH", [P, PAIRS, NT], F32R)
        yaL = sb("yaL", [P, PAIRS, NT], F32R)
        uL = sb("uL", [P, KT, NT], F32R)
        sb("arenaA_rest", [P, 10240 - 8320])
        arenaB = sb("arenaB", [P, 11900])
        used = [0]

        def work(n, shape=None, **kw):
            ap = arenaB[:, used[0]:used[0] + n]
            used[0] += n
            assert used[0] <= 11900, used
            return ap.rearrange(shape, **kw) if shape else ap

        cT = work(KT * 9, "p (k n) -> p k n", k=KT)
        vrow = work(P)[0:V_ROWS, :]
        xt = work(TT * D, "p (s n) -> p s n", s=TT)
        htmp = work(2 * D, "p (s k n) -> p s k n", s=2, k=KT)
        xsN = work(D)[0:B, :]
        sqj = work(D)
        used[0] = 0
        qT = work(NT)
        kT = work(NT)
        vT = work(NT)
        vN = work(TT * P, "p (j n) -> p j n", j=TT)
        kN = work(TT * P, "p (j n) -> p j n", j=TT)
        prA = work(2 * TT * T, "p (e j n) -> p e j n", e=2, j=TT)
        pT = work(TT * T, "p (j n) -> p j n", j=TT)
        selc = work(2 * P, "p (e n) -> p e n", e=2)
        used[0] = 0
        pre = work(2 * (NT + 4), "p (e n) -> p e n", e=2)
        cacc = work(2 * T, "p (e n) -> p e n", e=2)
        qkc = work(2 * T, "p (e n) -> p e n", e=2)
        mvT = work(2 * NT, "p (u n) -> p u n", u=2)
        v1 = work(TT * 257, "p (j n) -> p j n", j=TT)
        go = work(2 * NT, "p (u n) -> p u n", u=2)
        gz = work(2 * NT, "p (u n) -> p u n", u=2)
        wtF = work(4 * 640)
        sqh = cacc[:, :, :].rearrange("p e n -> p (e n)").rearrange("p (q n) -> p q n", q=TT)
        wt = wtF.rearrange("p (j n) -> p j n", n=640)
        hn = wtF[:, 0:TT * 257].rearrange("p (j n) -> p j n", j=TT)
        kw = work(TT * P, "p (j n) -> p j n", j=TT)
        cout = work(3 * P)
        selm = work(P)[0:MH, :]
        used[0] = 0
        sga = work(KT * NT, "p (k n) -> p k n", k=KT)
        sgm = work(KT * NT, "p (k n) -> p k n", k=KT)
        cS = work(2 * D, "p (s n) -> p s n", s=2)
        cW = work(D)
        selg = work(2 * P, "p (s n) -> p s n", s=2)
        used[0] = 0
        oT = work(2 * NT, "p (s n) -> p s n", s=2)
        oS = work(2 * B, "p (s n) -> p s n", s=2)
        xN = work(TT * D, "p (j n) -> p j n", j=TT)
        yO = work(D)
        xs2 = work(D)[0:B, :]
        fg = work(D)
        osq = work(D)

        qsN = sb("qsN", [B, AW])
        wif = sb("wif", [P, KT, 2 * MH])
        wifH = sb("wifH", [P, KT, 2 * MH], F32R)
        wifL = sb("wifL", [P, KT, 2 * MH], F32R)
        ss = sb("ss", [P, 5])
        rstd = sb("rstd", [P, 5])
        G = sb("G", [P, 5, 2 * MH])
        gf = sb("gf", [P, 5, MH])
        lf = sb("lf", [P, 5, MH])
        bc = sb("bc", [P, TT, MH])
        ec = sb("ec", [P, TT, MH])
        Mc = sb("Mc", [P, TT, MH])
        mt = sb("mt", [P, TT, MH])
        em = sb("em", [P, TT, MH])
        scr = sb("scr", [P, 1536])
        eR = scr[0:MH, 0:T]
        MR = sb("MR", [MH, T])
        m0 = sb("m0", [B, MH])
        gs = sb("gs", [B, 4, MH])
        aw = sb("aw", [B, 2, MH])
        mx = sb("mx", [P, 2, TT])
        nmx = sb("nmx", [P, 2, TT])
        rsum = sb("rsum", [P, 2, TT])
        rinv = sb("rinv", [P, 2, TT])
        qkvS = sb("qkvS", [P, 3, PAIRS, B])
        selfp = sb("selfp", [P, B, AH])
        yaS = sb("yaS", [P, PAIRS, B])
        tS = sb("tS", [P, PAIRS, B])
        bsum = sb("bsum", [B, AH, NBLK])
        cmpA = scr[0:B, 0:512].rearrange("p (h n m) -> p h n m", h=AH, n=NBLK)
        cmpB = scr[0:B, 512:1024].rearrange("p (h n m) -> p h n m", h=AH, n=NBLK)
        pen = sb("pen", [B, AH * NBLK])
        pend = scr[0:B, 1024:1536].rearrange("p (b n) -> p b n", b=B)
        mxA = sb("mxA", [P, B * AH])
        mx64 = sb("mx64", [B * AH, 1])
        dg64 = sb("dg64", [B * AH, B * AH])
        preS = sb("preS", [P, KT, 11])
        preN = scr[0:11, 512:1536]
        stT = sb("stT", [P, KT, 3 * B])
        cvS = sb("cvS", [P, KT, B])
        cvT = sb("cvT", [P, KT, B])
        vS = sb("vS", [P, KT, B])
        wsc = sb("wsc", [P, TT])
        dl = sb("dl", [P, 4, TT])
        ssm = sb("ssm", [P, TT])
        kqN = sb("kqN", [B, 2 * AW])
        ksN = kqN[:, :].rearrange("p (a n) -> p a n", a=2)
        nN = qsN[:, :].rearrange("p (h n) -> p h n", h=MH)
        nT = scr[0:B, 0:512].rearrange("p (h n) -> p h n", h=MH)
        dS = sb("dS", [B, 3, MH])
        abc = sb("abc", [P, B, 2 * MH])
        rbc = sb("rbc", [P, B, MH])
        dgS = sb("dgS", [B, B, 2 * MH])
        Cq = sb("Cq", [P, KT, B])
        sqS = sb("sqS", [P, KT, B])
        rmsS = sb("rmsS", [P, MH, B])

        ld_c, ld_vec, ld_small, ld_x, ld_xs = (sem(n) for n in ("ld_c", "ld_vec", "ld_small", "ld_x", "ld_xs"))
        ld_st, ld_n, ld_fin, ld_xo = (sem(n) for n in ("ld_st", "ld_n", "ld_fin", "ld_xo"))
        ld_ada = [sem(f"ld_ada{i}") for i in range(2)]
        ld_w = [sem(f"ld_w{i}") for i in range(4)]
        ld_page = [sem(f"ld_page{i}") for i in range(KV_SLOTS)]
        ld_C = [sem(f"ld_C{i}") for i in range(2)]
        hi_done = sem("hi_done")
        lo_done = sem("lo_done")
        z_done = sem("z_done")
        z_free = sem("z_free")
        page_free = [sem(f"page_free{i}") for i in range(KV_SLOTS)]
        pool_mult = sem("pool_mult")
        consts, c_silu, t_c, c_T, t_vec, v_col = (
            sem(n) for n in ("consts", "c_silu", "t_c", "c_T", "t_vec", "v_col"))
        ada_used, ada_ev, t_mod, mod_rdy, x_sq, x_var, x_std, x_nrm = (
            sem(n) for n in ("ada_used", "ada_ev", "t_mod", "mod_rdy", "x_sq", "x_var", "x_std", "x_nrm"))
        t_x, h_rdy, h_hi, h_lo, q_mm, q_ev, if_hi, if_lo = (
            sem(n) for n in ("t_x", "h_rdy", "h_hi", "h_lo", "q_mm", "q_ev", "if_hi", "if_lo"))
        g_mm, g_dve, g_act, g_pe, t_st, st_ev = (
            sem(n) for n in ("g_mm", "g_dve", "g_act", "g_pe", "t_st", "st_ev"))
        selc_rdy, qbc_mm, qbc_rdy, qk_done, smx, sexp, pnorm, pt_mm, pt_ev = (
            sem(n) for n in ("selc_rdy", "qbc_mm", "qbc_rdy", "qk_done", "smx", "sexp", "pnorm", "pt_mm", "pt_ev"))
        kn_mm, kn_ev, vn_mm, vn_ev, pv_done, ya_done = (
            sem(n) for n in ("kn_mm", "kn_ev", "vn_mm", "vn_ev", "pv_done", "ya_done"))
        sel_pe, sel_dve, sel_act = sem("sel_pe"), sem("sel_dve"), sem("sel_act")
        vsum_rdy, ys_mm, ys_ev, selm_rdy, mb_mm, w_exp, w_rdy, mlast_rdy, wsc_rdy = (
            sem(n) for n in ("vsum_rdy", "ys_mm", "ys_ev", "selm_rdy", "mb_mm", "w_exp", "w_rdy", "mlast_rdy", "wsc_rdy"))
        cv_rdy, sg_rdy, qk_rdy, st_mm, vt_mm, vt_ev, mpt_rdy, kt_mm, kw_rdy = (
            sem(n) for n in ("cv_rdy", "sg_rdy", "qk_rdy", "st_mm", "vt_mm", "vt_ev", "mpt_rdy", "kt_mm", "kw_rdy"))
        pv_mm, hn_ev, rs1_rdy, rs2_rdy, hn_rdy, cc_mm, c_ev, ht_mm, ym_done, v_one = (
            sem(n) for n in ("pv_mm", "hn_ev", "rs1_rdy", "rs2_rdy", "hn_rdy", "cc_mm", "c_ev", "ht_mm", "ym_done", "v_one"))
        sam_pe, sam_dve, sam_act = sem("sam_pe"), sem("sam_dve"), sem("sam_act")
        selg_rdy, kq_mm, cw_rdy, c_used, kq_used, cnew_rdy = (
            sem(n) for n in ("selg_rdy", "kq_mm", "cw_rdy", "c_used", "kq_used", "cnew_rdy"))
        fin_pe, fin_dve, fin_act, ya_rdy, ya_hi, ym_hi, ya_lo, ym_lo = (
            sem(n) for n in ("fin_pe", "fin_dve", "fin_act", "ya_rdy", "ya_hi", "ym_hi", "ya_lo", "ym_lo"))
        uu_rdy, u_hi, u_lo, ot_act, ot_rdy, ot_mm, y_acc, y_sq, y_var, y_std, y_rdy = (
            sem(n) for n in ("uu_rdy", "u_hi", "u_lo", "ot_act", "ot_rdy", "ot_mm", "y_acc", "y_sq", "y_var", "y_std", "y_rdy"))
        st_k, st_v, st_misc, st_pre, st_c, st_C, st_y = (
            sem(n) for n in ("st_k", "st_v", "st_misc", "st_pre", "st_c", "st_C", "st_y"))
        dve_chain, act_chain, pool_chain = sem("dve_chain"), sem("act_chain"), sem("pool_chain")

        ADA_COLS = (1024, 1536, 0, 512, 2048, 2560)
        block = ctx.enter_context(nc.Block())

        @block.sync
        def _(sp):
            def tile(j, n, src):
                sp.wait_ge(lo_done, n + 1)
                sp.dma_start(wraw[:, j % 4, 0:src.shape[1], :], src).then_inc(ld_w[j % 4], 16)

            def step(pages, s, count, first):
                sp.wait_ge(page_free[s % 4], count)
                for i in range(STEP_PAGES):
                    number = sp.value_load(ptab[0:1, bass.ds(first + i, 1)], min_val=0, max_val=n_phys - 1)
                    sp.dma_start(page[:, s % 4, i * AW:(i + 1) * AW],
                                 pages[:, bass.ds(number, 1), :].rearrange("t o n -> t (o n)")
                                 ).then_inc(ld_page[s % 4], 16)

            sp.dma_start(cN[0:B, :], I["c_sample"]).then_inc(ld_c, 16)
            sp.dma_start(cN[B:B + 1, :], I["c_prompt"]).then_inc(ld_c, 16)
            for row, name in ((V_G, "norm_g"), (V_MG, "m_norm_g"), (V_BC, "b_conv"), (V_WC, "w_conv"),
                              (V_BA, "b_ada")):
                src = I[name][0:1] if name != "w_conv" else I[name][0]
                n = (src.shape[0] * src.shape[1]) // P
                sp.dma_start(vrow[row:row + n, :], src.rearrange("a (r n) -> (a r) n", n=P)).then_inc(ld_vec, 16)
            for i in range(2):
                sp.dma_start(ada[:, i], w_ada[:, :, ADA_COLS[i]:ADA_COLS[i] + 512]).then_inc(ld_ada[i], 16)
            sp.dma_start(xt, x_p.rearrange("(j p) d -> p j d", p=P)).then_inc(ld_x, 16)
            sp.dma_start(xsN, x_s).then_inc(ld_xs, 16)
            sp.dma_start(ptab[:, :], I["page_table"].rearrange("b n -> (b n)").rearrange("(o n) -> o n", o=1)
                         ).then_inc(ld_small, 16)
            sp.dma_start(bif[:, :], I["b_if"][0:1].broadcast_to([P, 2 * MH])).then_inc(ld_small, 16)
            sp.dma_start(wif[:, :, :], w_in[:, :, CIF:CIF + 2 * MH]).then_inc(ld_small, 16)
            sp.dma_start(m0[:, :], I["state_m"][0]).then_inc(ld_small, 16)
            sp.dma_start(stC, I["state_conv"][0].rearrange("b j d -> (b j) d")).then_inc(ld_st, 16)
            for i in range(2, 7):
                sp.wait_ge(ada_used, i - 1)
                src = w_ada[:, :, ADA_COLS[i]:ADA_COLS[i] + 512] if i < 6 else w_in[:, :, CQ:CQ + AW]
                sp.dma_start(ada[:, i % 2], src).then_inc(ld_ada[i % 2], 16)
            sp.wait_ge(ld_small, 64)

            def att_tile(j, t):
                return w_in[:, :, bass.ds(t * P + (CQ, CK, CV, CZ)[j], P)]

            def ml_tile(j, h):
                col, by = ((CMQK, MQ), (CMQK + MH * MQ, MQ), (CMV, MV), (CMV + P, MV), (CMO, MV), (CMO + P, MV),
                           (CMZ, MV), (CMZ + P, MV))[j]
                return w_in[:, :, bass.ds(h * by + col, P)]

            def gate_tile(j, t):
                return w_in[:, :, bass.ds(t * 2 * P + (j // 2) * P + (CGA, CGM)[j % 2], P)]

            def four(w):
                return lambda j, t: w[:, :, bass.ds(t * 4 * P + j * P, P)]

            for j in range(4):
                tile(j, T_ATT + j, att_tile(j, 0))
            sp.wait_ge(ada_used, 7)

            def attention(t, following, tt_):
                n = T_ATT + 4 * t + 4
                tile(0, n, following(0, tt_))
                tile(1, n + 1, following(1, tt_))
                for s in range(8):
                    if s in (2, 4):
                        tile(1 + s // 2, n + 1 + s // 2, following(1 + s // 2, tt_))
                    step(pages_k, s, 2 * t + s // 4 + 1, 32 * t + 4 * s)

            with sp.Fori(0, PAIRS - 1) as t:
                attention(t, att_tile, t + 1)
            attention(PAIRS - 1, ml_tile, 0)
            sp.wait_ge(qbc_mm, 2 * PAIRS)
            sp.dma_start(qsN[:, :], I["state_n"][0].rearrange("b h d -> b (h d)")).then_inc(ld_n, 16)

            def mlstm(h, following, hh):
                n = T_ML + 8 * h + 4
                for j in range(8):
                    tile(j, n + j, ml_tile(j + 4, h) if j < 4 else following(j - 4, hh))
                    step(pages_v, j, 8 + 2 * h + j // 4 + 1, 32 * h + 4 * j)

            for j in (0, 1, 2, 3, "v0", "v1", 4, "v2", 5, "v3", 6, "v4", "v5", 7, "v6", "v7"):
                if isinstance(j, int):
                    tile(j, T_ML + 4 + j, ml_tile(j + 4, 0) if j < 4 else ml_tile(j - 4, 1))
                else:
                    s = int(j[1])
                    step(pages_v, s, 8 + s // 4 + 1, 4 * s)
            with sp.Fori(0, MH - 2) as h:
                mlstm(h + 1, ml_tile, h + 2)
            mlstm(MH - 1, gate_tile, 0)

            def states(e, t):
                sp.wait_ge(c_used, 2 * t + e + 1)
                sp.dma_start(cS[:, e].rearrange("p (u d) -> p u d", u=KT),
                             state_c[:, bass.ds(2 * t + e, 1)].rearrange("v o u d -> v (o u) d")).then_inc(ld_C[e], 16)

            for j in range(4):
                tile(j, T_GATE + 4 + j, gate_tile(j, 1))
                if j == 1:
                    sp.wait_ge(ym_done, 1 + MH)
                    sp.wait_ge(st_c, 16 * (2 * MH + 2))
                    states(0, 0)
            states(1, 0)
            with sp.Fori(0, 2) as t:
                for j in range(4):
                    tile(j, T_GATE + 4 * t + 8 + j, gate_tile(j, t + 2))
                    if j % 2 == 1:
                        states(j // 2, t + 1)
            for j in range(4):
                tile(j, T_WA + j, four(w_att)(j, 0))
            for e in range(2):
                states(e, 3)
            for n, w in ((T_WA + 4, w_att), (T_WM, w_ml), (T_WM + 4, w_ml), (T_OUT, w_out), (T_OUT + 4, w_out)):
                for j in range(4):
                    tile(j, n + j, four(w)(j, 1 if n in (T_WA + 4, T_WM + 4, T_OUT + 4) else 0))
                if n == T_OUT:
                    sp.wait_ge(u_lo, 2 + KT)
                    sp.dma_start(xN, x_p.rearrange("(j p) d -> p j d", p=P)).then_inc(ld_xo, 16)
                    sp.dma_start(xs2, x_s).then_inc(ld_xo, 16)
                    sp.dma_start(fg, I["final_g"].rearrange("(o n) -> o n", o=1).broadcast_to([P, D])).then_inc(ld_xo, 16)
            sp.wait_ge(y_rdy, TT + 1)
            sp.dma_start(O["y_p"].rearrange("o (j p) d -> p (o j) d", p=P), xN).then_inc(st_y, 16)
            sp.dma_start(O["y_s"].rearrange("b o d -> (b o) d"), xs2).then_inc(st_y, 16)
            sp.wait_ge(st_y, 32)

        @block.tensor
        def _(pe):
            mm = nc.tensor.matmul
            tr = nc.tensor.transpose

            def ztile(j, n, xH, xL, ks=KT, part_ready=None):
                pe.wait_ge(lo_done, n + 5)
                pe.wait_ge(z_free, n + 1)
                s = j % 2
                for k in range(ks):
                    if part_ready:
                        pe.wait_ge(part_ready, 2 + k + 1)
                    for w, xs_ in ((wH, (xH, xL)), (wL, (xH,))):
                        for x in xs_:
                            for a in range(2):
                                last = mm(ps[:, 2 * s + a, 0:HALF], w[:, s, k, :], x[:, k, a * HALF:(a + 1) * HALF],
                                          start=(k == 0 and w is wH and x is xH), stop=(k == ks - 1 and w is wL))
                last.then_inc(z_done, 1)

            pe.sem_inc(z_done, 2)
            pe.wait_ge(consts, 1)
            pe.wait_ge(ld_vec, 80)
            tr(ps[:, 5, 0:V_ROWS], vrow, ident[0:V_ROWS, 0:V_ROWS]).then_inc(t_vec, 1)
            pe.wait_ge(c_silu, 1)
            for k in range(KT):
                last = tr(ps[:, 4, 9 * k:9 * k + 9], cN[:, k * P:(k + 1) * P], ident[0:9, 0:9])
            last.then_inc(t_c, 1)
            pe.wait_ge(c_T, 1)
            for i in range(6):
                pe.wait_ge(ld_ada[i % 2], 16 * (i // 2 + 1))
                if i >= 2:
                    pe.wait_ge(ada_ev, i - 1)
                for k in range(KT):
                    last = mm(ps[0:9, i % 2, :], cT[:, k, :], ada[:, i % 2, k, :], start=(k == 0), stop=(k == KT - 1))
                last.then_inc(ada_used, 1)
                if i == 3 or i == 5:
                    pe.wait_ge(ada_ev, i + 1)
                    pe.wait_ge(v_col, 1)
                    b, lo, hi = (5, 0, 16) if i == 3 else (4, 16, 24)
                    for j in range(lo, hi):
                        last = tr(ps[:, b, 9 * (j - lo):9 * (j - lo) + 9], mod[:, j * P:(j + 1) * P], ident[0:9, 0:9])
                    last.then_inc(t_mod, 1)
            pe.wait_ge(x_nrm, 1)
            for j in range(TT):
                b = 2 if j % 2 == 0 else 6
                if j >= 2:
                    pe.wait_ge(h_rdy, j - 1)
                for k in range(KT):
                    last = tr(ps[:, b + k // 4, (k % 4) * P:(k % 4 + 1) * P], xt[:, j, k * P:(k + 1) * P], ident[:, :])
                last.then_inc(t_x, 1)
            pe.wait_ge(mod_rdy, 2)
            for k in range(KT):
                last = tr(ps[:, 4, B * k:B * k + B], xsN[:, k * P:(k + 1) * P], ident[0:B, 0:B])
            last.then_inc(t_x, 1)
            pe.wait_ge(ld_ada[0], 64)
            pe.wait_ge(h_rdy, TT + 1)
            pe.wait_ge(ada_ev, 6)
            for k in range(KT):
                last = mm(ps[0:B, 0, :], hS[:, k, :], ada[:, 0, k, :], start=(k == 0), stop=(k == KT - 1))
            last.then_inc(ada_used, 1)
            pe.wait_ge(ld_st, 16)
            for k in range(KT):
                last = tr(ps[:, 2, 24 * k:24 * k + 24], stC[:, k * P:(k + 1) * P], ident[0:24, 0:24])
            last.then_inc(t_st, 1)
            pe.wait_ge(h_lo, TT + 1)
            pe.wait_ge(if_lo, 1)
            for j in range(TT):
                tok = slice(j * P, (j + 1) * P)
                for k in range(KT):
                    mm(ps[:, 1, 8 * j:8 * j + 8], hH[:, k, tok], wifH[:, k, :], start=(k == 0), stop=False)
                    mm(ps[:, 1, 8 * j:8 * j + 8], hL[:, k, tok], wifH[:, k, :], start=False, stop=False)
                    mm(ps[:, 1, 8 * j:8 * j + 8], hH[:, k, tok], wifL[:, k, :], start=False, stop=(k == KT - 1))
            for k in range(KT):
                last = mm(ps[0:B, 1, 32:40], hS[:, k, :], wif[:, k, :], start=(k == 0), stop=(k == KT - 1))
            last.then_inc(g_mm, 1)
            pe.wait_ge(g_dve, 3)
            for j in range(TT):
                last = mm(ps[:, 5, MH * j:MH * j + MH], upper[:, :], lf[:, j, :], start=True, stop=(j == 0))
                for i in range(j):
                    last = mm(ps[:, 5, MH * j:MH * j + MH], ones[:, :], lf[:, i, :], start=False, stop=(i == j - 1))
            last.then_inc(g_pe, 1)
            pe.wait_ge(g_dve, 4)
            for j in range(TT):
                last = tr(ps[0:MH, 6, j * P:(j + 1) * P], ec[:, j, :], ident[:, :])
            last.then_inc(g_pe, 1)
            pe.wait_ge(g_dve, 5)
            for j in range(TT):
                last = tr(ps[:, 4, MH * j:MH * j + MH], MR[:, j * P:(j + 1) * P], ident[0:MH, 0:MH])
            last.then_inc(g_pe, 1)
            pe.wait_ge(g_dve, 6)
            pe.wait_ge(q_ev, 1)
            pe.wait_ge(st_ev, 1)

            def qk(e):
                r = slice(DH * e, DH * e + DH)
                for q, b, c in ((3, 4, 0), (2, 5, 0), (0, 5, 384), (1, 6, 0)):
                    last = mm(ps[:, b, c:c + (q + 1) * P], qT[r, q * P:(q + 1) * P], kT[r, 0:(q + 1) * P],
                              start=True, stop=True)
                last.then_inc(qk_done, 1)

            def ptrans(e):
                for k, b, c in ((0, 4, 0), (1, 5, 0), (3, 5, 384), (2, 6, 0)):
                    for q in range(k, TT):
                        last = tr(ps[:, b, c + (q - k) * P:c + (q - k + 1) * P], prA[:, e, q, k * P:(k + 1) * P],
                                  ident[:, :])
                last.then_inc(pt_mm, 1)

            def pv(e):
                for k in range(TT):
                    last = mm(ps[DH * e:DH * e + DH, 7, k * P:T], vN[:, k, DH * e:DH * e + DH], pT[:, k, k * P:T],
                              start=(k == 0), stop=(k == TT - 1))
                return last

            def query_copy(e, t, bank):
                pe.wait_ge(selc_rdy, 2 * t + e + 1)
                mm(ps[:, bank, :], selc[0:B, e, :], qsN[:, :], start=True, stop=True).then_inc(qbc_mm, 1)

            def attention(t, before):
                n = T_ATT + 4 * t
                ztile(0, n, hH, hL)
                if before:
                    pe.wait_ge(pnorm, 2 * t)
                    ptrans(1)
                ztile(1, n + 1, hH, hL)
                pe.wait_ge(pt_ev, 2 * t + 1)
                query_copy(0, t, 4)
                if before:
                    pv(1).then_inc(pv_done, 1)
                pe.wait_ge(z_free, n + 4)
                pe.wait_ge(qbc_rdy, 2 * t + 1)
                qk(0)
                ztile(2, n + 2, hH, hL)
                pe.wait_ge(ya_done, t + 1)
                for j in range(TT):
                    last = tr(ps[:, 7, j * P:(j + 1) * P], kT[:, j * P:(j + 1) * P], ident[:, :])
                last.then_inc(kn_mm, 1)
                ztile(3, n + 3, hH, hL)
                pe.wait_ge(kn_ev, t + 1)
                pe.wait_ge(z_free, n + 5)
                for j in range(TT):
                    last = tr(ps[:, 7, j * P:(j + 1) * P], vT[:, j * P:(j + 1) * P], ident[:, :])
                last.then_inc(vn_mm, 1)
                pe.wait_ge(pnorm, 2 * t + 1)
                ptrans(0)
                pe.wait_ge(vn_ev, t + 1)
                query_copy(1, t, 7)
                pe.wait_ge(pt_ev, 2 * t + 2)
                qk(1)
                pe.wait_ge(qbc_rdy, 2 * t + 2)
                pv(0)

            attention(0, False)
            with pe.Fori(0, PAIRS - 1) as t:
                attention(t + 1, True)
            def page_sums(h):
                pe.wait_ge(vsum_rdy, h)
                for e in range(2):
                    for c in range(PAIRS):
                        last = mm(ps[:, 6, PAIRS * e + c:PAIRS * e + c + 1], vacc[:, e, c * P:(c + 1) * P], ones[:, 0:1],
                                  start=True, stop=True)
                last.then_inc(ys_mm, 1)

            def spread_max(h):
                pe.wait_ge(selm_rdy, h + 1)
                pe.wait_ge(c_ev, h + 1)
                mm(ps[:, 7, :], selm, MR[:, :], start=True, stop=True).then_inc(mb_mm, 1)

            def mlstm(h, first):
                n = T_ML + 8 * h
                if not first:
                    ztile(0, n, hH, hL)
                    ztile(1, n + 1, hH, hL)
                    spread_max(h)
                    ztile(2, n + 2, hH, hL)
                    pe.wait_ge(hn_ev, 4 * h + 1)
                    page_sums(h)
                    ztile(3, n + 3, hH, hL)
                pe.wait_ge(sg_rdy, 2 * h + 2)
                pe.wait_ge(qk_rdy, h + 1)
                pe.wait_ge(ym_done, h + 1)
                if not first:
                    pe.wait_ge(ys_ev, h)
                for k, b, c in ((0, 4, 0), (1, 5, 0), (3, 5, 384), (2, 6, 0)):
                    last = mm(ps[:, b, c:c + T - k * P], qkc[:, 1, k * P:(k + 1) * P], qkc[:, 0, k * P:T],
                              start=True, stop=True)
                last.then_inc(st_mm, 1)
                pe.wait_ge(w_exp, h + 1)
                pe.wait_ge(mlast_rdy, h + 1)
                pe.wait_ge(z_free, n + 6)
                for u in range(2):
                    if u == 1:
                        pe.wait_ge(vt_ev, 2 * h + 1)
                    for j in range(TT):
                        last = tr(ps[:, 7, j * P:(j + 1) * P], mvT[:, u, j * P:(j + 1) * P], ident[:, :])
                    last.then_inc(vt_mm, 1)
                    ztile(u, n + 4 + u, hH, hL) if not first else None
                pe.wait_ge(mpt_rdy, h + 1)
                for j in range(TT):
                    last = tr(ps[:, 6, j * P:(j + 1) * P], qkc[:, 1, j * P:(j + 1) * P], ident[:, :])
                last.then_inc(kt_mm, 1)
                pe.wait_ge(vt_ev, 2 * h + 2)
                pe.wait_ge(v_one, 1)
                for q, b in ((0, 4), (1, 5), (2, 7), (3, 6)):
                    if q == 3:
                        pe.wait_ge(kw_rdy, h + 1)
                    for k in range(q + 1):
                        last = mm(ps[:, b, 0:MV + 1], wt[:, k, (q - k) * P:(q - k + 1) * P], v1[:, k, :],
                                  start=(k == 0), stop=(k == q))
                last.then_inc(pv_mm, 1)
                ztile(2, n + 6, hH, hL)
                ztile(3, n + 7, hH, hL)
                pe.wait_ge(hn_ev, 4 * h + 5)
                for u in range(3):
                    for j in range(TT):
                        if u < 2:
                            last = mm(ps[:, 7, u * P:(u + 1) * P], v1[:, j, u * P:(u + 1) * P], kw[:, j, :],
                                      start=(j == 0), stop=(j == TT - 1))
                        else:
                            last = mm(ps[0:1, 7, 2 * P:3 * P], ones[:, 0:1], kw[:, j, :],
                                      start=(j == 0), stop=(j == TT - 1))
                last.then_inc(cc_mm, 1)
                pe.wait_ge(hn_rdy, h + 1)
                for u in range(2):
                    for j in range(TT):
                        last = tr(ps[:, 4 + u, j * P:(j + 1) * P], hn[:, j, u * P:(u + 1) * P], ident[:, :])
                last.then_inc(ht_mm, 1)

            ztile(0, T_ML, hH, hL)
            pe.wait_ge(pnorm, 2 * PAIRS)
            ptrans(1)
            ztile(1, T_ML + 1, hH, hL)
            pe.wait_ge(pt_ev, 2 * PAIRS + 1)
            pv(1).then_inc(pv_done, 1)
            pe.wait_ge(sel_dve, 1)
            for e in range(2):
                last = mm(ps[:, 4, 32 * e:32 * e + 32], headsel[:, e, :], tS[:, :, :].rearrange("p a b -> p (a b)"),
                          start=True, stop=True)
            last.then_inc(sel_pe, 1)
            for a in range(2):
                for t in range(PAIRS):
                    last = tr(ps[0:B, 5 + a, t * P:(t + 1) * P], qkvS[:, 1 + a, t, :], ident[:, :])
            last.then_inc(sel_pe, 1)
            ztile(2, T_ML + 2, hH, hL)
            ztile(3, T_ML + 3, hH, hL)
            pe.wait_ge(ya_done, 1 + PAIRS)
            pe.wait_ge(sel_dve, 2)
            for b in range(B):
                last = mm(ps[0:B, 7, 0:P], colsel[:, b, :], score[:, b * P:(b + 1) * P], start=(b == 0), stop=(b == B - 1))
            last.then_inc(sel_pe, 1)
            ztile(4, T_ML + 4, hH, hL)
            pe.wait_ge(sel_dve, 3)
            mm(ps[:, 7, :], ones[0:B, :], pend.rearrange("p b n -> p (b n)"), start=True, stop=True).then_inc(sel_pe, 1)
            pe.wait_ge(sel_dve, 4)
            spread_max(0)
            pe.wait_ge(sel_dve, 4)
            tr(ps[0:B * AH, 4, 0:P], mxA[:, :], ident[:, :]).then_inc(sel_pe, 1)
            pe.wait_ge(sel_dve, 5)
            mm(ps[:, 4, 128:192], ones[0:B * AH, :], dg64[:, :], start=True, stop=True).then_inc(sel_pe, 1)
            ztile(5, T_ML + 5, hH, hL)
            pe.wait_ge(sel_dve, 7)
            mm(ps[:, 4, 256:320], ones[:, :], mxA[:, :], start=True, stop=True).then_inc(sel_pe, 1)
            pe.wait_ge(sel_act, 2)
            pe.wait_ge(sel_dve, 8)
            mlstm(0, True)
            with pe.Fori(0, MH - 1) as h:
                mlstm(h + 1, False)
            ztile(0, T_GATE, hH, hL)
            ztile(1, T_GATE + 1, hH, hL)
            page_sums(MH)
            pe.wait_ge(c_ev, 1 + MH)
            pe.wait_ge(ym_done, 1 + MH)
            pe.wait_ge(sam_dve, 1)
            mm(ps[:, 7, 0:64], ones[0:B, :], dgS[:, :, :].rearrange("p b n -> p (b n)"), start=True, stop=True)\
                .then_inc(sam_pe, 1)
            for k in range(KT):
                last = tr(ps[0:11, 4 + k // 4, (k % 4) * P:(k % 4 + 1) * P], preS[:, k, :], ident[:, :])
            last.then_inc(sam_pe, 1)
            ztile(2, T_GATE + 2, hH, hL)
            pe.wait_ge(sam_dve, 3)
            pe.wait_ge(sam_act, 2)
            for k in range(KT):
                last = tr(ps[0:B, 4 + k // 4, (k % 4) * P:(k % 4 + 1) * P], cvS[:, (k + 4) % KT, :], ident[:, :])
            last.then_inc(sam_pe, 1)
            ztile(3, T_GATE + 3, hH, hL)
            pe.wait_ge(sam_dve, 4)
            mm(ps[:, 7, 64:96], ones[0:B, :], dgS[:, :, 0:MH], start=True, stop=True).then_inc(sam_pe, 1)
            pe.wait_ge(sam_dve, 5)
            pe.wait_ge(sam_act, 3)
            pe.wait_ge(ys_ev, MH)

            def key_query(e, t):
                pe.wait_ge(selg_rdy, 2 * t + e + 1)
                pe.wait_ge(kq_used, 2 * t + e + 1)
                for a in range(2):
                    last = mm(ps[:, 4 + 2 * e + a, :], selg[0:B, e, :], kqN[:, a * AW:(a + 1) * AW],
                              start=True, stop=True)
                last.then_inc(kq_mm, 1)

            with pe.Fori(0, 3) as t:
                n = T_GATE + 4 * t + 4
                for e in range(2):
                    key_query(e, t)
                    ztile(0, n + 2 * e, hH, hL)
                    ztile(1, n + 2 * e + 1, hH, hL)
            pe.wait_ge(ya_lo, 1)
            for j in range(8):
                if j in (0, 2):
                    key_query(j // 2, 3)
                ztile(j, T_WA + j, yaH, yaL, PAIRS)
                if j == 6:
                    pe.wait_ge(fin_dve, 1)
                    mm(ps[:, 4, 0:64], ones[:, :], sqS[:, :, :].rearrange("p k b -> p (k b)"), start=True, stop=True)\
                        .then_inc(fin_pe, 1)
            pe.wait_ge(ym_lo, 3)
            with pe.Fori(0, 2) as t:
                for j in range(4):
                    ztile(j, T_WM + 4 * t + j, hH, hL)

            def out_turn(s, j):
                pe.wait_ge(ot_rdy, j + 1)
                pe.wait_ge(y_acc, j + 1)
                for i in range(TT):
                    tr(ps[:, 4 + 2 * s, i * P:(i + 1) * P], oT[:, s, i * P:(i + 1) * P], ident[:, :])
                tr(ps[0:B, 5 + 2 * s, 0:P], oT[:, s, T:NT], ident[:, :]).then_inc(ot_mm, 1)

            ztile(0, T_OUT, uH, uL, part_ready=u_lo)
            ztile(1, T_OUT + 1, uH, uL)
            with pe.Fori(0, 3) as t:
                for s in range(2):
                    out_turn(s, 2 * t + s)
                    ztile(s, T_OUT + 2 * t + 2 + s, uH, uL)
            out_turn(0, 6)
            out_turn(1, 7)

        @block.scalar
        def _(act):
            chain = Chain(act, act_chain)
            f = nc.scalar.activation

            def high(j, n, quad, ks=KT):
                act.wait_ge(ld_w[j % 4], 16 * (quad + 1))
                act.wait_ge(z_done, n + 1)
                f(wH[:, j % 2, 0:ks], wraw[:, j % 4, 0:ks], ACT.Copy).then_inc(hi_done, 1)

            def leave(j, n, *dests):
                act.wait_ge(z_done, n + 3)
                for dst, func in dests:
                    ins = f(halves(dst), zps(j % 2), func)
                ins.then_inc(z_free, 1)

            act.sem_inc(z_free, 2)
            act.sem_inc(pt_ev, 1)
            act.sem_inc(hn_ev, 1)
            act.sem_inc(c_ev, 1)
            act.sem_inc(st_k, 16)
            act.sem_inc(st_v, 16)
            act.sem_inc(st_C, 16)
            act.sem_inc(st_c, 32)
            act.wait_ge(ld_c, 32)
            f(cN, cN, ACT.Silu).then_inc(c_silu, 1)

            def ada_leave(i):
                act.wait_ge(ada_used, i + 1)
                f(mod[:, ADA_COLS[i]:ADA_COLS[i] + 512], ps[0:9, i % 2, :], ACT.Copy).then_inc(ada_ev, 1)

            ada_leave(0)
            ada_leave(1)
            act.wait_ge(ld_x, 16)
            act.wait_ge(ld_xs, 16)
            act.wait_ge(v_col, 1)
            for j in range(TT):
                chain(f(sqj, xt[:, j, :], ACT.Square, accum_out=ss[:, j:j + 1]))
            f(sqj[0:B, :], xsN, ACT.Square, accum_out=ss[0:B, 4:5]).then_inc(x_sq, 1)
            act.wait_ge(x_var, 1)
            f(ss[:, :], rstd[:, :], ACT.Sqrt).then_inc(x_std, 1)
            for i in range(2, 6):
                ada_leave(i)
            act.wait_ge(ld_small, 64)
            f(wifH[:, :, :], wif[:, :, :], ACT.Copy).then_inc(if_hi, 1)
            for j in range(TT):
                act.wait_ge(h_rdy, j + 1)
                f(hH[:, :, j * P:(j + 1) * P], htmp[:, j % 2], ACT.Copy).then_inc(h_hi, 1)
            act.wait_ge(h_rdy, TT + 1)
            f(hH[:, :, T:NT], hS[:, :, :], ACT.Copy).then_inc(h_hi, 1)
            act.wait_ge(ada_used, 7)
            f(qsN[:, :], ps[0:B, 0, :], ACT.Copy).then_inc(q_ev, 1)
            act.wait_ge(t_st, 1)
            f(stT[:, :, :].rearrange("p k n -> p (k n)"), ps[:, 2, 0:192], ACT.Copy).then_inc(st_ev, 1)
            for n in range(2):
                high(n, n, 0)
            act.wait_ge(g_dve, 2)
            chain(f(gf[:, :, :], gf[:, :, :], ACT.Exp))
            f(gf[:, :, :], gf[:, :, :], ACT.Ln, bias=1.0).then_inc(g_act, 1)
            act.wait_ge(g_dve, 6)
            f(em[:, :, :], mt[:, :, :], ACT.Exp, scale=-1.0).then_inc(g_act, 1)
            act.wait_ge(g_dve, 7)
            f(aw[:, :, :], aw[:, :, :], ACT.Exp)
            f(gs[:, 2, :], gs[:, 1, :], ACT.Exp, scale=-1.0).then_inc(g_act, 1)
            act.dma_start(O["m_s"][0], gs[:, 1, :]).then_inc(st_misc, 16)
            act.dma_start(O["m_p"][0], mt[P - 1:P, TT - 1, :]).then_inc(st_misc, 16)

            def rows_out(dst, t):
                return dst.rearrange("o b (j p) h d -> p (o b j) (h d)", p=P)[:, :, bass.ds(t * P, P)]

            def weights(e, t):
                act.wait_ge(smx, 2 * t + e + 1)
                for q, b, c in ((3, 4, 0), (2, 5, 0), (0, 5, 384), (1, 6, 0)):
                    last = f(prA[:, e, q, 0:(q + 1) * P], ps[:, b, c:c + (q + 1) * P], ACT.Exp,
                             bias=nmx[:, e, q:q + 1], scale=SCALE, accum_out=rsum[:, e, q:q + 1])
                last.then_inc(sexp, 1)

            def turned(e, t):
                act.wait_ge(pt_mm, 2 * t + e + 1)
                for k, b, c in ((0, 4, 0), (1, 5, 0), (3, 5, 384), (2, 6, 0)):
                    last = f(pT[:, k, k * P:T], ps[:, b, c:c + T - k * P], ACT.Copy)
                last.then_inc(pt_ev, 1)

            def copy_out(e, t, before):
                if before:
                    for slot in range(KV_SLOTS):
                        act.wait_ge(page_free[slot], 2 * t + e)
                act.wait_ge(qbc_mm, 2 * t + e + 1)
                f(qbc[:, e, :], ps[:, 4 + 3 * e, :], ACT.Copy).then_inc(qbc_rdy, 1)

            def attention(t, before):
                n, quad = T_ATT + 4 * t, t
                high(2, n + 2, quad)
                leave(0, n, (qT, ACT.Copy))
                if before:
                    turned(1, t - 1)
                leave(1, n + 1, (kT, ACT.Copy))
                copy_out(0, t, before)
                high(3, n + 3, quad)
                weights(0, t)
                leave(0, n + 2, (vT, ACT.Copy))
                act.wait_ge(kn_mm, t + 1)
                act.wait_ge(st_k, 16 * t + 16)
                f(kN, ps[:, 7, :].rearrange("p (j n) -> p j n", j=TT), ACT.Copy).then_inc(kn_ev, 1)
                act.wait_ge(kn_ev, t + 1)
                act.dma_start(rows_out(O["k_p"], t), kN).then_inc(st_k, 16)
                high(0, n + 4, quad + 1)
                act.wait_ge(vn_mm, t + 1)
                act.wait_ge(st_v, 16 * t + 16)
                f(vN, ps[:, 7, :].rearrange("p (j n) -> p j n", j=TT), ACT.Copy).then_inc(vn_ev, 1)
                act.wait_ge(vn_ev, t + 1)
                act.dma_start(rows_out(O["v_p"], t), vN).then_inc(st_v, 16)
                turned(0, t)
                copy_out(1, t, before)
                leave(1, n + 3, (yaT[:, bass.ds(t, 1), :].rearrange("p o n -> p (o n)"), ACT.Silu))
                high(1, n + 5, quad + 1)
                weights(1, t)

            attention(0, False)
            with act.Fori(0, PAIRS - 1) as t:
                attention(t + 1, True)
            high(2, T_ML + 2, T_ML // 4)
            leave(0, T_ML, (pre[:, 0, 3:3 + NT], ACT.Copy))
            turned(1, PAIRS - 1)
            high(3, T_ML + 3, T_ML // 4)
            leave(1, T_ML + 1, (pre[:, 1, 3:3 + NT], ACT.Copy))
            act.wait_ge(sel_pe, 2)
            for a in range(2):
                last = f(ksN[:, a, :], ps[0:B, 5 + a, :], ACT.Copy)
            last.then_inc(sel_act, 1)
            act.wait_ge(sel_act, 1)
            act.dma_start(O["k_s"].rearrange("o b q h d -> (o b q) (h d)"), ksN[:, 0, :]).then_inc(st_misc, 16)
            act.dma_start(O["v_s"].rearrange("o b q h d -> (o b q) (h d)"), ksN[:, 1, :]).then_inc(st_misc, 16)
            high(0, T_ML + 4, T_ML // 4 + 1)
            leave(0, T_ML + 2, (mvT[:, 0, :], ACT.Copy))
            high(1, T_ML + 5, T_ML // 4 + 1)
            leave(1, T_ML + 3, (mvT[:, 1, :], ACT.Copy))
            act.wait_ge(ya_done, 1 + PAIRS)
            act.wait_ge(st_k, 16 * (1 + PAIRS))
            act.wait_ge(st_v, 16 * (1 + PAIRS))
            for e in range(2):
                act.wait_ge(cv_rdy, e + 1)
                f(qkc[:, e, :], cacc[:, e, :], ACT.Silu).then_inc(sg_rdy, 1)
            high(2, T_ML + 6, T_ML // 4 + 1)
            leave(0, T_ML + 4, (go[:, 0, :], ACT.Sigmoid))
            act.wait_ge(sel_dve, 6)
            f(score, score, ACT.Exp, scale=SCALE)
            f(selfp[:, :, :], selfp[:, :, :], ACT.Exp, scale=SCALE).then_inc(sel_act, 1)

            def sums_leave(h):
                act.wait_ge(ys_mm, h)
                f(yaS[:, :, bass.ds(2 * h - 2, 2)].rearrange("p c e -> p e c"),
                  ps[:, 6, 0:2 * PAIRS].rearrange("p (e c) -> p e c", e=2), ACT.Copy).then_inc(ys_ev, 1)

            def decays(h):
                act.wait_ge(mb_mm, h + 1)
                for k in range(TT):
                    last = f(wt[:, k, 0:T - k * P], ps[:, 7, k * P:T], ACT.Exp, bias=ec[:, k, bass.ds(h, 1)], scale=-1.0)
                last.then_inc(w_exp, 1)
                act.wait_ge(mlast_rdy, h + 1)
                f(wsc[:, :], dl[:, 0, :], ACT.Exp).then_inc(wsc_rdy, 1)

            def mlstm(h, first):
                n, quad = T_ML + 8 * h, T_ML // 4 + 2 * h
                if first:
                    decays(h)
                    high(3, n + 7, quad + 1)
                    leave(1, n + 5, (go[:, 1, :], ACT.Sigmoid))
                else:
                    high(2, n + 2, quad)
                    leave(0, n, (pre[:, 0, 3:3 + NT], ACT.Copy))
                    high(3, n + 3, quad)
                    leave(1, n + 1, (pre[:, 1, 3:3 + NT], ACT.Copy))
                    decays(h)
                    for e in range(2):
                        act.wait_ge(cv_rdy, 2 * h + e + 1)
                        f(qkc[:, e, :], cacc[:, e, :], ACT.Silu).then_inc(sg_rdy, 1)
                    high(0, n + 4, quad + 1)
                    leave(0, n + 2, (mvT[:, 0, :], ACT.Copy))
                    sums_leave(h)
                    high(1, n + 5, quad + 1)
                    leave(1, n + 3, (mvT[:, 1, :], ACT.Copy))
                for u in range(2):
                    act.wait_ge(vt_mm, 2 * h + u + 1)
                    f(v1[:, :, u * P:(u + 1) * P], ps[:, 7, :].rearrange("p (j n) -> p j n", j=TT), ACT.Copy)\
                        .then_inc(vt_ev, 1)
                    if not first:
                        high(2 + u, n + 6 + u, quad + 1)
                        leave(u, n + 4 + u, (go[:, u, :], ACT.Sigmoid))
                act.wait_ge(pv_mm, h + 1)
                for q, b in ((0, 4), (1, 5), (2, 7), (3, 6)):
                    f(sqh[:, q, :], ps[:, b, 0:MV], ACT.Square, accum_out=ssm[:, q:q + 1])
                    f(hn[:, q, :], ps[:, b, 0:MV + 1], ACT.Copy).then_inc(hn_ev, 1)
                act.wait_ge(rs1_rdy, h + 1)
                f(dl[:, 1, :], dl[:, 3, :], ACT.Sqrt).then_inc(rs2_rdy, 1)
                high(0, n + 8, quad + 2)
                leave(0, n + 6, (gz[:, 0, :], ACT.Silu))
                high(1, n + 9, quad + 2)
                leave(1, n + 7, (gz[:, 1, :], ACT.Silu))
                act.wait_ge(cc_mm, h + 1)
                act.wait_ge(st_c, 32 * h + 32)
                f(cout[:, 0:2 * P], ps[:, 7, 0:2 * P], ACT.Copy)
                f(cout[0:1, 2 * P:3 * P], ps[0:1, 7, 2 * P:3 * P], ACT.Copy).then_inc(c_ev, 1)
                act.wait_ge(c_ev, h + 2)
                act.dma_start(O["C_p"][0, 0].rearrange("h (u v) d -> v (h u) d", v=P)[:, bass.ds(2 * h, 2), :],
                              cout[:, 0:2 * P].rearrange("p (u d) -> p u d", u=2)).then_inc(st_c, 16)
                act.dma_start(O["n_p"][0, 0][bass.ds(h, 1), :], cout[0:1, 2 * P:3 * P]).then_inc(st_c, 16)

            mlstm(0, True)
            with act.Fori(0, MH - 1) as h:
                mlstm(h + 1, False)
            act.dma_start(O["conv_s"][0, :, 0:2, :], I["state_conv"][0, :, 1:3, :]).then_inc(st_misc, 16)

            def gate_leave(j, t):
                leave(j, T_GATE + 4 * t + j, ((sga, sgm)[j % 2][:, bass.ds(2 * t + j // 2, 1), :]
                                              .rearrange("p o n -> p (o n)"), ACT.Sigmoid))

            act.wait_ge(ym_done, 1 + MH)
            act.wait_ge(st_c, 32 * MH + 32)
            high(2, T_GATE + 2, T_GATE // 4)
            gate_leave(0, 0)
            high(3, T_GATE + 3, T_GATE // 4)
            gate_leave(1, 0)
            sums_leave(MH)
            act.wait_ge(sam_dve, 2)
            f(cvS[:, :, :], cvS[:, :, :], ACT.Silu).then_inc(sam_act, 1)
            act.wait_ge(sam_pe, 2)
            f(preN.rearrange("p (a n) -> p a n", a=2), ps[0:11, 4:6, :], ACT.Copy).then_inc(sam_act, 1)
            act.wait_ge(sam_act, 2)
            act.dma_start(O["conv_p"][0, 0], preN[0:3, :]).then_inc(st_pre, 16)
            act.dma_start(O["conv_s"][0, :, 2, :], preN[3:11, :]).then_inc(st_pre, 16)
            high(0, T_GATE + 4, T_GATE // 4 + 1)
            gate_leave(2, 0)
            act.wait_ge(sam_pe, 3)
            act.wait_ge(st_misc, 16 * 5)
            f(kqN[:, :].rearrange("p (a n) -> p a n", a=2), ps[0:B, 4:6, :], ACT.Copy).then_inc(sam_act, 1)
            high(1, T_GATE + 5, T_GATE // 4 + 1)
            gate_leave(3, 0)
            act.wait_ge(sam_dve, 4)
            act.dma_start(O["n_s"][0], nN).then_inc(st_misc, 16)
            act.wait_ge(ya_rdy, 1)
            f(yaH[:, :, :], yaT, ACT.Copy).then_inc(ya_hi, 1)

            def states_out(e, t):
                act.wait_ge(cnew_rdy, 2 * t + e + 1)
                act.dma_start(new_c[:, bass.ds(2 * t + e, 1)].rearrange("v o u d -> v (o u) d"),
                              cW.rearrange("p (u d) -> p u d", u=KT)).then_inc(st_C, 16)

            with act.Fori(0, 3) as i:
                n, quad = T_GATE + 4 * i + 4, T_GATE // 4 + i + 1
                for j in range(4):
                    high((j + 2) % 4, n + j + 2, quad + (j + 2) // 4)
                    gate_leave(j, i + 1)
                    if j % 2 == 1:
                        states_out(j // 2, i)
            for j in range(8):
                if j == 2:
                    act.wait_ge(z_done, 2 + T_WA)
                    f(hH[:, :, 0:T], ymT[:, :, 0:T], ACT.Copy).then_inc(ym_hi, 1)
                if j in (2, 4):
                    states_out(j // 2 - 1, 3)
                if j == 6:
                    act.wait_ge(fin_dve, 2)
                    f(rmsS[:, :, :], rmsS[:, :, :], ACT.Sqrt).then_inc(fin_act, 1)
                    act.wait_ge(fin_dve, 3)
                    f(hH[:, :, T:NT], ymT[:, :, T:NT], ACT.Copy).then_inc(ym_hi, 1)
                high(j + 2, T_WA + j + 2, (T_WA + j + 2) // 4, PAIRS if j < 6 else KT)
            with act.Fori(0, 2) as t:
                n, quad = T_WM + 4 * t, T_WM // 4 + t
                for j in range(4):
                    high((j + 2) % 4, n + j + 2, quad + (j + 2) // 4)
                    act.wait_ge(uu_rdy, 4 * t + j + 1)
                    act.wait_ge(ym_lo, 3)
                    c = bass.ds(4 * t + j, 1)
                    f(uH[:, c, :], sgm[:, c, :], ACT.Copy).then_inc(u_hi, 1)
            act.wait_ge(uu_rdy, KT)
            for j in range(8):
                n = T_OUT + j
                if j < 6:
                    high(j + 2, n + 2, (n + 2) // 4)
                if j >= 2:
                    act.wait_ge(ot_mm, j - 1)
                else:
                    act.wait_ge(u_lo, 2 + KT)
                act.wait_ge(z_done, n + 3)
                f(halves(oT[:, j % 2, :]), zps(j % 2), ACT.Copy, scale=modT[:, 16 + j, B:B + 1])
                f(oS[:, j % 2, :], ps[:, 2 * (j % 2) + 1, HALF - B:HALF], ACT.Copy).then_inc(ot_act, 1)
                act.wait_ge(ot_act, j + 1)
                act.sem_inc(z_free, 1)
            act.wait_ge(y_acc, 2 + 8)
            for j in range(TT):
                chain(f(osq, xN[:, j, :], ACT.Square, accum_out=ss[:, j:j + 1]))
            f(osq[0:B, :], xs2, ACT.Square, accum_out=ss[0:B, 4:5]).then_inc(y_sq, 1)
            act.wait_ge(y_var, 1)
            f(ss[:, :], rstd[:, :], ACT.Sqrt).then_inc(y_std, 1)
            act.wait_ge(st_misc, 16 * 6)
            act.wait_ge(st_pre, 32)
            act.wait_ge(st_C, 16 + 16 * B)

        @block.gpsimd
        def _(pool):
            chain = Chain(pool, pool_chain)
            tt = nc.gpsimd.tensor_tensor

            def fill(ap, value, pattern, mult, op, other, base=0):
                chain(nc.gpsimd.memset(ap, value))
                return nc.gpsimd.affine_select(out=ap, in_=ap, compare_op=op, fill=other, base=base, pattern=pattern,
                                               channel_multiplier=mult)

            def low(j, n, ks=KT):
                pool.wait_ge(hi_done, n + 1)
                tt(wL[:, j % 2, 0:ks], wraw[:, j % 4, 0:ks], wH[:, j % 2, 0:ks].bitcast(F32), ALU.subtract)\
                    .then_inc(lo_done, 1)

            pool.sem_inc(lo_done, 4)
            for slot in range(KV_SLOTS):
                pool.sem_inc(page_free[slot], 1)
            pool.sem_inc(u_lo, 2)
            chain(fill(ident[:, :], 0.0, [[-1, P]], 1, ALU.not_equal, 1.0))
            nc.gpsimd.memset(ones[:, :], 1.0)
            chain(fill(cmask[:, :], 0.0, [[-1, P]], 1, ALU.is_ge, NEG))
            chain(fill(upper[:, :], 1.0, [[1, P]], -1, ALU.is_ge, 0.0))
            chain(fill(rowsel[:, :, :], 0.0, [[-1, B + 2], [0, P]], 1, ALU.not_equal, 1.0))
            chain(fill(colsel[:, :, :], 0.0, [[1, B], [-1, B]], 0, ALU.not_equal, 1.0))
            chain(fill(earlier[:, :, :], 1.0, [[1, NBLK], [-1, NBLK]], 0, ALU.is_gt, 0.0))
            chain(nc.gpsimd.memset(headsel[:, :, :], 0.0))
            nc.gpsimd.memset(headsel[0:DH, 0, :], 1.0)
            chain(nc.gpsimd.memset(headsel[DH:P, 1, :], 1.0))
            nc.gpsimd.memset(G[:, :, :], 0.0).then_inc(consts, 1)
            pool.wait_ge(if_hi, 1)
            tt(wifL[:, :, :], wif[:, :, :], wifH[:, :, :].bitcast(F32), ALU.subtract).then_inc(if_lo, 1)
            for j in range(TT):
                pool.wait_ge(h_hi, j + 1)
                tok = slice(j * P, (j + 1) * P)
                tt(hL[:, :, tok], htmp[:, j % 2], hH[:, :, tok].bitcast(F32), ALU.subtract).then_inc(h_lo, 1)
            pool.wait_ge(h_hi, TT + 1)
            tt(hL[:, :, T:NT], hS[:, :, :], hH[:, :, T:NT].bitcast(F32), ALU.subtract).then_inc(h_lo, 1)
            for n in range(2):
                low(n, n)

            def key_step(s, t):
                pool.wait_ge(ld_page[s % 4], 64 * (2 * t + s // 4 + 1))
                pool.wait_ge(qbc_rdy, 2 * t + s // 4 + 1)
                four = page[:, s % 4, :].rearrange("p (g n) -> p g n", g=STEP_PAGES)
                tt(four, four, qbc[:, s // 4:s // 4 + 1, :].broadcast_to([P, STEP_PAGES, AW]), ALU.mult)\
                    .then_inc(pool_mult, 1)

            def attention(t, before):
                n = T_ATT + 4 * t
                if before:
                    key_step(3, t - 1)
                low(2, n + 2)
                if before:
                    key_step(5, t - 1)
                low(3, n + 3)
                if before:
                    key_step(7, t - 1)
                low(0, n + 4)
                low(1, n + 5)

            attention(0, False)
            with pool.Fori(0, PAIRS - 1) as t:
                attention(t + 1, True)

            def causal_weights(h):
                diag = wt[:, :, 0:P]
                nc.gpsimd.affine_select(out=diag, in_=diag, compare_op=ALU.is_ge, fill=0.0, base=0,
                                        pattern=[[0, TT], [1, P]], channel_multiplier=-1).then_inc(w_rdy, 1)

            def value_step(s, h):
                pool.wait_ge(ld_page[s % 4], 64 * (8 + 2 * h + s // 4 + 1))
                heads = page[:, s % 4, :].rearrange("p (g n) -> p g n", n=DH)
                tt(heads, heads, score[:, bass.ds((8 * h + s) * 32, 32)].unsqueeze(2).broadcast_to([P, 32, DH]),
                   ALU.mult).then_inc(pool_mult, 1)

            key_step(3, PAIRS - 1)
            low(2, T_ML + 2)
            key_step(5, PAIRS - 1)
            low(3, T_ML + 3)
            key_step(7, PAIRS - 1)
            pool.wait_ge(ya_done, 1 + PAIRS)
            nc.gpsimd.memset(v1[:, :, MV:MV + 1], 1.0).then_inc(v_one, 1)
            nc.gpsimd.memset(pre[:, :, 0:3], 0.0).then_inc(v_one, 1)
            for j in range(3):
                low(j, T_ML + 4 + j)
            pool.wait_ge(w_exp, 1)
            low(3, T_ML + 7)
            causal_weights(0)
            pool.wait_ge(sel_dve, 8)
            value_step(1, 0)
            value_step(3, 0)
            low(0, T_ML + 8)
            value_step(5, 0)
            low(1, T_ML + 9)
            value_step(7, 0)
            with pool.Fori(0, MH - 1) as i:
                h = i + 1
                n = T_ML + 8 * h
                for j in range(8):
                    if j == 2:
                        pool.wait_ge(w_exp, h + 1)
                    low((j + 2) % 4, n + j + 2)
                    if j == 2:
                        causal_weights(h)
                    if j % 2 == 1:
                        value_step(j, h)
            for j in range(4):
                low((j + 2) % 4, T_GATE + j + 2)
            pool.wait_ge(ya_hi, 1)
            tt(yaL[:, :, :], yaT, yaH[:, :, :].bitcast(F32), ALU.subtract).then_inc(ya_lo, 1)
            pool.wait_ge(sam_dve, 5)

            def decayed_state(e, t):
                pool.wait_ge(ld_C[e], 16 * t + 16)
                pool.wait_ge(st_C, 32 * t + 16 * e + 16)
                pool.wait_ge(c_used, 2 * t + e + 2)
                tt(cW.rearrange("p (h n) -> p h n", h=MH), cS[:, e].rearrange("p (h n) -> p h n", h=MH),
                   abc[:, bass.ds(2 * t + e, 1), 0:MH].rearrange("p o h -> p (o h)").unsqueeze(2)
                   .broadcast_to([P, MH, 2 * MQ]), ALU.mult).then_inc(cw_rdy, 1)

            with pool.Fori(0, 3) as t:
                n = T_GATE + 4 * t + 4
                for e in range(2):
                    decayed_state(e, t)
                    low(2 + 2 * e, n + 2 * e + 2)
                    low(3 + 2 * e, n + 2 * e + 3)
            decayed_state(0, 3)
            for j in range(8):
                if j == 2:
                    decayed_state(1, 3)
                if j == 4:
                    pool.wait_ge(ym_hi, 1)
                    tt(hL[:, 0:4, 0:T], ymT[:, 0:4, 0:T], hH[:, 0:4, 0:T].bitcast(F32), ALU.subtract).then_inc(ym_lo, 1)
                low(j + 2, T_WA + j + 2, PAIRS if j < 6 else KT)
            with pool.Fori(0, 2) as t:
                n = T_WM + 4 * t
                for j in range(4):
                    low((j + 2) % 4, n + j + 2)
                    pool.wait_ge(u_hi, 4 * t + j + 1)
                    c = bass.ds(4 * t + j, 1)
                    tt(uL[:, c, :], sgm[:, c, :], uH[:, c, :].bitcast(F32), ALU.subtract).then_inc(u_lo, 1)
            for j in range(6):
                low(j + 2, T_OUT + j + 2)

        @block.vector
        def _(dve):
            chain = Chain(dve, dve_chain)
            v = nc.vector
            tt = v.tensor_tensor

            def over(ap, n):
                return ap.unsqueeze(len(ap.shape)).broadcast_to(list(ap.shape) + [n])

            dve.sem_inc(ya_done, 1)
            dve.sem_inc(ym_done, 1)
            dve.sem_inc(c_used, 2)
            dve.sem_inc(kq_used, 2)
            dve.sem_inc(y_acc, 2)
            chain(v.memset(ss[:, :], 1.0))
            dve.wait_ge(t_vec, 1)
            v.tensor_copy(vcol[:, :], ps[:, 5, 0:V_ROWS]).then_inc(v_col, 1)
            dve.wait_ge(t_c, 1)
            v.tensor_copy(cT.rearrange("p k n -> p (k n)"), ps[:, 4, 0:9 * KT]).then_inc(c_T, 1)
            dve.wait_ge(x_sq, 1)
            v.tensor_scalar(rstd[:, :], ss[:, :], 1.0 / D, EPS, ALU.mult, ALU.add).then_inc(x_var, 1)
            dve.wait_ge(x_std, 1)
            chain(v.reciprocal(rstd[:, :], ss[:, :]))
            for j in range(TT):
                v.tensor_scalar(xt[:, j, :], xt[:, j, :], rstd[:, j:j + 1], None, ALU.mult)
            v.tensor_scalar(xsN, xsN, rstd[0:B, 4:5], None, ALU.mult).then_inc(x_nrm, 1)
            dve.wait_ge(t_mod, 1)
            chain(tt(modT[:, 0:16, :], ps[:, 5, 0:144].rearrange("p (k n) -> p k n", n=9),
                     over(vcol[:, V_BA:V_BA + 16], 9), ALU.add))
            v.scalar_tensor_tensor(hscale[:, :, :], modT[:, 8:16, :], 1.0, over(vcol[:, V_G:V_G + KT], 9),
                                   ALU.add, ALU.mult).then_inc(mod_rdy, 1)
            dve.wait_ge(t_mod, 2)
            tt(modT[:, 16:24, :], ps[:, 4, 0:72].rearrange("p (k n) -> p k n", n=9),
               over(vcol[:, V_BA + 16:V_BA + 24], 9), ALU.add).then_inc(mod_rdy, 1)
            dve.wait_ge(mod_rdy, 2)
            for j in range(TT):
                b = 2 if j % 2 == 0 else 6
                dve.wait_ge(t_x, j + 1)
                if j >= 2:
                    dve.wait_ge(h_lo, j - 1)
                chain(tt(htmp[:, j % 2], ps[:, b:b + 2, :].rearrange("p a (k n) -> p (a k) n", n=P),
                         over(hscale[:, :, B], P), ALU.mult))
                tt(htmp[:, j % 2], htmp[:, j % 2], over(modT[:, 0:KT, B], P), ALU.add).then_inc(h_rdy, 1)
            dve.wait_ge(t_x, TT + 1)
            chain(tt(hS[:, :, :], ps[:, 4, 0:B * KT].rearrange("p (k n) -> p k n", n=B), hscale[:, :, 0:B], ALU.mult))
            tt(hS[:, :, :], hS[:, :, :], modT[:, 0:KT, 0:B], ALU.add).then_inc(h_rdy, 1)
            dve.wait_ge(g_mm, 1)
            dve.wait_ge(ld_small, 64)
            tt(G[:, 0:TT, :], ps[:, 1, 0:32].rearrange("p (j n) -> p j n", n=8),
               bif[:, :].unsqueeze(1).broadcast_to([P, TT, 8]), ALU.add)
            tt(G[0:B, TT, :], ps[0:B, 1, 32:40], bif[0:B, :], ALU.add).then_inc(g_dve, 1)
            dve.wait_ge(g_dve, 1)
            ig, fg_ = G[:, :, 0:MH], G[:, :, MH:2 * MH]
            chain(v.tensor_scalar(gf[:, :, :], fg_, -1.0, None, ALU.mult))
            tt(gf[:, :, :], gf[:, :, :], fg_, ALU.min).then_inc(g_dve, 1)
            dve.wait_ge(g_act, 1)
            v.scalar_tensor_tensor(lf[:, :, :], fg_, 0.0, gf[:, :, :], ALU.min, ALU.subtract).then_inc(g_dve, 1)
            dve.wait_ge(g_dve, 3)
            dve.wait_ge(g_pe, 1)
            chain(v.tensor_copy(bc[:, :, :].rearrange("p j h -> p (j h)"), ps[:, 5, 0:16]))
            tt(ec[:, :, :], G[:, 0:TT, 0:MH], bc[:, :, :], ALU.subtract).then_inc(g_dve, 1)
            dve.wait_ge(g_pe, 2)
            chain(v.tensor_copy(eR, ps[0:MH, 6, :]))
            v.tensor_tensor_scan(MR[:, :], eR, eR, 0.0, ALU.max, ALU.max).then_inc(g_dve, 1)
            dve.wait_ge(g_pe, 3)
            tt(mt[:, :, :].rearrange("p j h -> p (j h)"), ps[:, 4, 0:16], bc[:, :, :].rearrange("p j h -> p (j h)"),
               ALU.add).then_inc(g_dve, 1)
            chain(tt(gs[:, 0, :], lf[0:B, TT, :], m0[:, :], ALU.add))
            chain(tt(gs[:, 1, :], gs[:, 0, :], G[0:B, TT, 0:MH], ALU.max))
            tt(aw[:, 0, :], gs[:, 0, :], gs[:, 1, :], ALU.subtract)
            tt(aw[:, 1, :], G[0:B, TT, 0:MH], gs[:, 1, :], ALU.subtract).then_inc(g_dve, 1)

            def causal_max(e, t):
                dve.wait_ge(qk_done, 2 * t + e + 1)
                for q, b, c in ((3, 4, 0), (2, 5, 0), (0, 5, 384), (1, 6, 0)):
                    own = ps[:, b, c + q * P:c + (q + 1) * P]
                    last = tt(own, own, cmask[:, :], ALU.add)
                chain(last)
                for q, b, c in ((3, 4, 0), (2, 5, 0), (0, 5, 384), (1, 6, 0)):
                    last = v.tensor_reduce(mx[:, e, q:q + 1], ps[:, b, c:c + (q + 1) * P], AX, ALU.max)
                chain(last)
                v.tensor_scalar(nmx[:, e, :], mx[:, e, :], -SCALE, None, ALU.mult).then_inc(smx, 1)

            def normalise(e, t):
                dve.wait_ge(sexp, 2 * t + e + 1)
                chain(v.reciprocal(rinv[:, e, :], rsum[:, e, :]))
                for q in range(TT):
                    last = v.tensor_scalar(prA[:, e, q, 0:(q + 1) * P], prA[:, e, q, 0:(q + 1) * P],
                                           rinv[:, e, q:q + 1], None, ALU.mult)
                last.then_inc(pnorm, 1)

            def key_step(s, t):
                if s in (3, 5, 7):
                    dve.wait_ge(pool_mult, 3 * t + (s - 3) // 2 + 1)
                else:
                    dve.wait_ge(ld_page[s % 4], 64 * (2 * t + s // 4 + 1))
                    dve.wait_ge(qbc_rdy, 2 * t + s // 4 + 1)
                    four = page[:, s % 4, :].rearrange("p (g n) -> p g n", g=STEP_PAGES)
                    chain(tt(four, four, qbc[:, s // 4:s // 4 + 1, :].broadcast_to([P, STEP_PAGES, AW]), ALU.mult))
                v.tensor_reduce(score[:, bass.ds((8 * t + s) * 32, 32)],
                                page[:, s % 4, :].rearrange("p (g n) -> p g n", n=DH), AX, ALU.add)\
                    .then_inc(page_free[s % 4], 1)

            def next_selector(e, t):
                dve.wait_ge(qbc_mm, 2 * t + e + 1)
                v.tensor_copy(selc[0:B, e, :], rowsel[:, bass.ds(2 * t + e + 2, 1), :].rearrange("p o n -> p (o n)"))\
                    .then_inc(selc_rdy, 1)

            def finish(t):
                normalise(1, t)
                for s in (2, 3, 4):
                    key_step(s, t)
                dve.wait_ge(z_free, T_ATT + 4 * t + 6)
                dve.wait_ge(pv_done, t + 1)
                ya = yaT[:, bass.ds(t, 1), 0:T].rearrange("p o n -> p (o n)")
                tt(ya, ya, ps[:, 7, :], ALU.mult).then_inc(ya_done, 1)

            def attention(t, before):
                n = T_ATT + 4 * t
                if before:
                    finish(t - 1)
                next_selector(0, t)
                causal_max(0, t)
                if before:
                    key_step(5, t - 1)
                    key_step(7, t - 1)
                normalise(0, t)
                if before:
                    key_step(6, t - 1)
                key_step(0, t)
                for i, src, at in ((0, qT, 3), (1, kT, 4), (2, vT, 5)):
                    dve.wait_ge(z_free, n + at)
                    v.tensor_copy(qkvS[:, i, bass.ds(t, 1), :].rearrange("p o n -> p (o n)"), src[:, T:NT])
                causal_max(1, t)
                next_selector(1, t)
                key_step(1, t)

            for e in range(2):
                v.tensor_copy(selc[0:B, e, :], rowsel[:, e, :]).then_inc(selc_rdy, 1)
            attention(0, False)
            with dve.Fori(0, PAIRS - 1) as t:
                chain.loop(t, 2 * 1 + 2 * 2 + 5 * 1)
                attention(t + 1, True)
            chain.end(PAIRS - 1)
            finish(PAIRS - 1)

            def convolve(e, h):
                dve.wait_ge(z_free, T_ML + 8 * h + 3 + e)
                acc = cacc[:, e, :]

                def tap(j):
                    return vcol[:, bass.ds(h + (V_WC + KT * j + MH * e), 1)]

                chain(v.tensor_scalar(acc, pre[:, e, 0:T], tap(0), vcol[:, bass.ds(h + (V_BC + MH * e), 1)],
                                      ALU.mult, ALU.add))
                for j in range(1, 4):
                    last = v.scalar_tensor_tensor(acc, pre[:, e, j:j + T], tap(j), acc, ALU.mult, ALU.add)
                    if j < 3:
                        chain(last)
                last.then_inc(cv_rdy, 1)
                v.tensor_copy(preS[:, bass.ds(h + MH * e, 1), :].rearrange("p o n -> p (o n)"), pre[:, e, T:T + 11])

            dve.wait_ge(ya_done, 1 + PAIRS)
            v.tensor_copy(selm, rowsel[0:MH, 0, :]).then_inc(selm_rdy, 1)
            tt(tS[:, :, :], qkvS[:, 0], qkvS[:, 1], ALU.mult).then_inc(sel_dve, 1)
            for s in (5, 6, 7):
                key_step(s, PAIRS - 1)
            for slot in range(KV_SLOTS):
                dve.wait_ge(page_free[slot], 1 + 2 * PAIRS)
            dve.wait_ge(sel_dve, 1)
            dve.sem_inc(sel_dve, 1)
            dve.wait_ge(st_k, 16 * (1 + PAIRS))
            dve.wait_ge(st_v, 16 * (1 + PAIRS))
            dve.wait_ge(v_one, 2)
            convolve(0, 0)
            dve.wait_ge(sel_pe, 1)
            chain(v.tensor_copy(selfp[:, :, :].rearrange("p b (t e) -> p e t b", e=2),
                                ps[:, 4, 0:64].rearrange("p (e t b) -> p e t b", e=2, t=PAIRS)))
            dve.wait_ge(sel_pe, 3)
            chain(v.tensor_reduce(bsum[:, :, :], ps[0:B, 7, 0:P].rearrange("p (n w h) -> p h n w", n=NBLK, w=2),
                                  AX, ALU.add))
            sm = bsum[:, :, :].unsqueeze(2).broadcast_to([B, AH, NBLK, NBLK])
            sn = bsum[:, :, :].unsqueeze(3).broadcast_to([B, AH, NBLK, NBLK])
            tt(cmpA, sm, sn, ALU.is_gt)
            chain(tt(cmpB, sm, sn, ALU.is_equal))
            chain(tt(cmpB, cmpB, earlier[:, :, :].unsqueeze(1).broadcast_to([B, AH, NBLK, NBLK]), ALU.mult))
            chain(tt(cmpA, cmpA, cmpB, ALU.add))
            chain(v.tensor_reduce(pen[:, :].rearrange("p (h n) -> p h n", n=NBLK), cmpA, AX, ALU.add))
            chain(v.tensor_scalar(pen[:, :], pen[:, :], float(TOPK), NEG, ALU.is_ge, ALU.mult))
            tt(pend, pen[:, :].unsqueeze(1).broadcast_to([B, B, AH * NBLK]), over(ident[0:B, 0:B], AH * NBLK),
               ALU.mult).then_inc(sel_dve, 1)
            convolve(1, 0)
            dve.wait_ge(sel_pe, 4)
            sc = score.rearrange("p (b n w h) -> p b n w h", b=B, n=NBLK, w=2)
            for w in range(2):
                last = tt(sc[:, :, :, w, :], sc[:, :, :, w, :],
                          ps[:, 7, :].rearrange("p (b h n) -> p b n h", b=B, h=AH), ALU.add)
            chain(last)
            by_bh = score.rearrange("p (b g h) -> p b h g", b=B, g=PAGES)
            mx3 = mxA[:, :].rearrange("p (b h) -> p b h", b=B)
            v.tensor_reduce(mx3, by_bh, AX, ALU.max).then_inc(sel_dve, 1)
            dve.wait_ge(sel_pe, 5)
            chain(v.tensor_reduce(mx64[:, :], ps[0:B * AH, 4, 0:P], AX, ALU.max))
            v.tensor_scalar(dg64[:, :], ident[0:B * AH, 0:B * AH], mx64[:, 0:1], None, ALU.mult).then_inc(sel_dve, 1)
            dve.wait_ge(sel_pe, 6)
            chain(tt(mx3, ps[:, 4, 128:192].rearrange("p (b h) -> p b h", b=B), selfp[:, :, :], ALU.max))
            tt(by_bh, by_bh, over(mx3, PAGES), ALU.subtract)
            tt(selfp[:, :, :], selfp[:, :, :], mx3, ALU.subtract).then_inc(sel_dve, 1)
            dve.wait_ge(sel_act, 2)
            v.tensor_reduce(mx3, by_bh, AX, ALU.add).then_inc(sel_dve, 1)
            dve.wait_ge(sel_pe, 7)
            chain(tt(mx3, ps[:, 4, 256:320].rearrange("p (b h) -> p b h", b=B), selfp[:, :, :], ALU.add))
            chain(v.reciprocal(mx3, mx3))
            tt(by_bh, by_bh, over(mx3, PAGES), ALU.mult)
            tt(selfp[:, :, :], selfp[:, :, :], mx3, ALU.mult).then_inc(sel_dve, 1)
            dve.wait_ge(sel_dve, 8)

            def value_step(s, h, first):
                prod = page[:, s % 4, :]
                if s % 2 == 0:
                    dve.wait_ge(ld_page[s % 4], 64 * (8 + 2 * h + s // 4 + 1))
                    heads = prod.rearrange("p (g n) -> p g n", n=DH)
                    chain(tt(heads, heads, over(score[:, bass.ds((8 * h + s) * 32, 32)], DH), ALU.mult))
                else:
                    dve.wait_ge(pool_mult, 3 * PAIRS + 4 * h + s // 2 + 1)
                chain(tt(prod[:, 0:1024], prod[:, 0:1024], prod[:, 1024:2048], ALU.add))
                acc = vacc[:, s // 4, :]
                if s % 4 == 0:
                    if not first:
                        dve.wait_ge(ys_mm, h)
                    tt(acc, prod[:, 0:512], prod[:, 512:1024], ALU.add).then_inc(page_free[0], 1)
                    return
                chain(tt(prod[:, 0:512], prod[:, 0:512], prod[:, 512:1024], ALU.add))
                dve.wait_ge(page_free[s % 4 - 1], 8 + 2 * h + s // 4 + 2)
                tt(acc, acc, prod[:, 0:512], ALU.add).then_inc(page_free[s % 4], 1)
                if s == 7:
                    dve.wait_ge(page_free[3], 8 + 2 * h + 3)
                    dve.sem_inc(vsum_rdy, 1)

            def mlstm(h, first):
                n = T_ML + 8 * h
                if not first:
                    convolve(0, h)
                    convolve(1, h)
                dve.wait_ge(mb_mm, h + 1)
                v.tensor_copy(selm, rowsel[0:MH, bass.ds(h + 1, 1), :].rearrange("p o n -> p (o n)"))\
                    .then_inc(selm_rdy, 1)
                dve.wait_ge(w_exp, h + 1)
                v.tensor_scalar(dl[:, 0, :], ec[:, :, bass.ds(h, 1)].rearrange("p j o -> p (j o)"),
                                ps[:, 7, T - 1:T], None, ALU.subtract).then_inc(mlast_rdy, 1)
                value_step(0, h, first)
                dve.wait_ge(sg_rdy, 2 * h + 2)
                v.tensor_scalar(qkc[:, 1, :], qkc[:, 1, :], KSCALE, None, ALU.mult).then_inc(qk_rdy, 1)
                value_step(1, h, first)
                dve.wait_ge(st_mm, h + 1)
                dve.wait_ge(w_rdy, h + 1)
                for k, b, c in ((0, 4, 0), (1, 5, 0), (3, 5, 384), (2, 6, 0)):
                    last = tt(wt[:, k, 0:T - k * P], wt[:, k, 0:T - k * P], ps[:, b, c:c + T - k * P], ALU.mult)
                last.then_inc(mpt_rdy, 1)
                dve.wait_ge(z_free, n + 6)
                v.tensor_copy(vS[:, bass.ds(2 * h, 2), :], mvT[:, :, T:NT])
                value_step(2, h, first)
                dve.wait_ge(kt_mm, h + 1)
                dve.wait_ge(wsc_rdy, h + 1)
                tt(kw, ps[:, 6, :].rearrange("p (j n) -> p j n", j=TT), over(wsc[:, :], P), ALU.mult)\
                    .then_inc(kw_rdy, 1)
                value_step(3, h, first)
                dve.wait_ge(hn_ev, 4 * h + 5)
                den = hn[:, :, MV]
                chain(v.tensor_scalar(dl[:, 1, :], den, -1.0, None, ALU.mult))
                chain(tt(dl[:, 1, :], dl[:, 1, :], den, ALU.max))
                chain(tt(dl[:, 1, :], dl[:, 1, :], em[:, :, bass.ds(h, 1)].rearrange("p j o -> p (j o)"), ALU.max))
                chain(v.reciprocal(dl[:, 2, :], dl[:, 1, :]))
                chain(tt(dl[:, 3, :], dl[:, 2, :], dl[:, 2, :], ALU.mult))
                chain(tt(dl[:, 3, :], dl[:, 3, :], ssm[:, :], ALU.mult))
                v.tensor_scalar(dl[:, 3, :], dl[:, 3, :], 1.0 / MV, EPS, ALU.mult, ALU.add).then_inc(rs1_rdy, 1)
                dve.wait_ge(rs2_rdy, h + 1)
                chain(v.reciprocal(dl[:, 3, :], dl[:, 1, :]))
                chain(tt(dl[:, 3, :], dl[:, 3, :], dl[:, 2, :], ALU.mult))
                tt(hn[:, :, 0:MV], hn[:, :, 0:MV], over(dl[:, 3, :], MV), ALU.mult).then_inc(hn_rdy, 1)
                value_step(4, h, first)
                value_step(5, h, first)
                for u in range(2):
                    dve.wait_ge(z_free, n + 9 + u)
                    chain(v.scalar_tensor_tensor(go[:, u, :], go[:, u, :], vcol[:, bass.ds(2 * h + (V_MG + u), 1)],
                                                 gz[:, u, :], ALU.mult, ALU.mult))
                v.tensor_copy(ymT[:, bass.ds(2 * h, 2), T:NT], go[:, :, T:NT])
                dve.wait_ge(ht_mm, h + 1)
                tt(ymT[:, bass.ds(2 * h, 2), 0:T], ps[:, 4:6, :], go[:, :, 0:T], ALU.mult).then_inc(ym_done, 1)
                value_step(6, h, first)
                value_step(7, h, first)

            mlstm(0, True)
            with dve.Fori(0, MH - 1) as h:
                chain.loop(h, 2 * 3 + 4 * 1 + 8 * 1 + 6 * 1 + 6 + 2 + 2)
                mlstm(h + 1, False)
            chain.end(MH - 1)

            dve.wait_ge(ym_done, 1 + MH)
            awf = aw[:, :, :].rearrange("p a h -> p (a h)")
            dve.wait_ge(g_act, 3)
            tt(dgS[:, :, :], awf.unsqueeze(1).broadcast_to([B, B, 2 * MH]), over(ident[0:B, 0:B], 2 * MH), ALU.mult)\
                .then_inc(sam_dve, 1)
            st3 = stT[:, :, :].rearrange("p k (b j) -> p k b j", j=3)
            chain(tt(cvS[:, :, :], preS[:, :, 3:11], over(vcol[:, V_WC + 3 * KT:V_WC + 4 * KT], B), ALU.mult))
            for j in range(3):
                chain(tt(cvT[:, :, :], st3[:, :, :, j], over(vcol[:, V_WC + j * KT:V_WC + (j + 1) * KT], B), ALU.mult))
                chain(tt(cvS[:, :, :], cvS[:, :, :], cvT[:, :, :], ALU.add))
            tt(cvS[:, :, :], cvS[:, :, :], over(vcol[:, V_BC:V_BC + KT], B), ALU.add).then_inc(sam_dve, 1)
            dve.wait_ge(sam_act, 1)
            v.tensor_scalar(cvS[:, MH:KT, :], cvS[:, MH:KT, :], KSCALE, None, ALU.mult).then_inc(sam_dve, 1)
            dve.wait_ge(sam_pe, 1)
            chain(v.tensor_copy(abc[:, :, :].rearrange("p b n -> p (b n)"), ps[:, 7, 0:64]))
            v4 = vS[:, :, :].rearrange("p (h u) b -> p h u b", u=2)
            chain(tt(v4, v4, abc[:, :, MH:2 * MH].rearrange("p b h -> p h b").unsqueeze(2).broadcast_to([P, MH, 2, B]),
                     ALU.mult))
            dve.wait_ge(sam_act, 3)
            dve.wait_ge(ld_n, 16)
            kS = kqN[:, 0:AW].rearrange("p (h n) -> p h n", h=MH)
            qS = kqN[:, AW:2 * AW].rearrange("p (h n) -> p h n", h=MH)
            tt(nT, kS, over(aw[:, 1, :], MQ), ALU.mult)
            chain(tt(nN, nN, over(aw[:, 0, :], MQ), ALU.mult))
            chain(tt(nN, nN, nT, ALU.add))
            chain(tt(nT, nN, qS, ALU.mult))
            chain(v.tensor_reduce(dS[:, 0, :], nT, AX, ALU.add))
            chain(v.tensor_scalar(dS[:, 1, :], dS[:, 0, :], -1.0, None, ALU.mult))
            chain(tt(dS[:, 1, :], dS[:, 1, :], dS[:, 0, :], ALU.max))
            chain(tt(dS[:, 1, :], dS[:, 1, :], gs[:, 2, :], ALU.max))
            chain(v.reciprocal(dS[:, 2, :], dS[:, 1, :]))
            tt(dgS[:, :, 0:MH], dS[:, 2, :].unsqueeze(1).broadcast_to([B, B, MH]), over(ident[0:B, 0:B], MH), ALU.mult)\
                .then_inc(sam_dve, 1)
            dve.wait_ge(sam_pe, 4)
            v.tensor_copy(rbc[:, :, :].rearrange("p b n -> p (b n)"), ps[:, 7, 64:96]).then_inc(sam_dve, 1)
            dve.wait_ge(ys_ev, MH)
            sp_t = selfp[:, :, :].rearrange("p b (t e) -> p e t b", e=2)
            for e in range(2):
                r = slice(DH * e, DH * e + DH)
                last = tt(tS[r], qkvS[r, 2], sp_t[r, e], ALU.mult)
            chain(last)
            chain(tt(tS[:, :, :], tS[:, :, :], yaS[:, :, :], ALU.add))
            chain(tt(yaT[:, :, T:NT], yaT[:, :, T:NT], tS[:, :, :], ALU.mult))

            for e in range(2):
                v.tensor_copy(selg[0:B, e, :], rowsel[:, e, :]).then_inc(selg_rdy, 1)
            dve.sem_inc(ya_rdy, 1)

            def new_state(e, t):
                dve.wait_ge(kq_mm, 2 * t + e + 1)
                v.tensor_copy(selg[0:B, e, :], rowsel[:, bass.ds(2 * t + e + 2, 1), :]
                              .rearrange("p o n -> p (o n)")).then_inc(selg_rdy, 1)
                dve.wait_ge(cw_rdy, 2 * t + e + 1)
                four = cS[:, e].rearrange("p (h u n) -> p h u n", h=MH, u=2)
                key = ps[:, 4 + 2 * e, :].rearrange("p (h n) -> p h n", h=MH).unsqueeze(2)
                query = ps[:, 5 + 2 * e, :].rearrange("p (h n) -> p h n", h=MH).unsqueeze(2)
                val = vS[:, :, bass.ds(2 * t + e, 1)].rearrange("p (h u) o -> p h (u o)", u=2)
                chain(tt(four, key.broadcast_to([P, MH, 2, MQ]), over(val, MQ), ALU.mult))
                tt(cW, cW, cS[:, e], ALU.add).then_inc(cnew_rdy, 1)
                dve.wait_ge(cnew_rdy, 2 * t + e + 1)
                tt(four, cW.rearrange("p (h u n) -> p h u n", h=MH, u=2), query.broadcast_to([P, MH, 2, MQ]),
                   ALU.mult).then_inc(kq_used, 1)
                dve.wait_ge(kq_used, 2 * t + e + 3)
                v.tensor_reduce(Cq[:, :, bass.ds(2 * t + e, 1)].rearrange("p k o -> p (k o)"),
                                cS[:, e].rearrange("p (k n) -> p k n", k=KT), AX, ALU.add).then_inc(c_used, 1)

            def halved(ap, c):
                return ap[:, bass.ds(c, 1), :].rearrange("p o (a n) -> p (o a) n", a=2)

            def attention_leaves(c):
                dve.wait_ge(z_done, T_WA + c + 3)
                tt(halved(sga, c), zps(c % 2), halved(sga, c), ALU.mult).then_inc(z_free, 1)

            with dve.Fori(0, 3) as t:
                chain.loop(t, 2 * 1)
                new_state(0, t)
                new_state(1, t)
            chain.end(3)
            dve.wait_ge(z_free, 2 + T_WA)
            new_state(0, 3)
            attention_leaves(0)
            attention_leaves(1)
            new_state(1, 3)
            for c in range(2, 5):
                attention_leaves(c)
            dve.wait_ge(c_used, 2 + B)
            C4 = Cq[:, :, :].rearrange("p (h u) b -> p h u b", u=2)
            chain(tt(C4, C4, rbc[:, :, :].rearrange("p b h -> p h b").unsqueeze(2).broadcast_to([P, MH, 2, B]), ALU.mult))
            tt(sqS[:, :, :], Cq[:, :, :], Cq[:, :, :], ALU.mult).then_inc(fin_dve, 1)
            attention_leaves(5)
            dve.wait_ge(ym_hi, 1)
            tt(hL[:, 4:KT, 0:T], ymT[:, 4:KT, 0:T], hH[:, 4:KT, 0:T].bitcast(F32), ALU.subtract).then_inc(ym_lo, 1)
            dve.wait_ge(fin_pe, 1)
            chain(v.tensor_reduce(rmsS[:, :, :], ps[:, 4, 0:64].rearrange("p (h u b) -> p h b u", u=2, b=B), AX, ALU.add))
            v.tensor_scalar(rmsS[:, :, :], rmsS[:, :, :], 1.0 / MV, EPS, ALU.mult, ALU.add).then_inc(fin_dve, 1)
            attention_leaves(6)
            dve.wait_ge(fin_act, 1)
            chain(v.reciprocal(rmsS[:, :, :], rmsS[:, :, :]))
            chain(tt(C4, C4, rmsS[:, :, :].unsqueeze(2).broadcast_to([P, MH, 2, B]), ALU.mult))
            tt(ymT[:, :, T:NT], ymT[:, :, T:NT], Cq[:, :, :], ALU.mult).then_inc(fin_dve, 1)
            attention_leaves(7)
            dve.wait_ge(ym_hi, 2)
            tt(hL[:, :, T:NT], ymT[:, :, T:NT], hH[:, :, T:NT].bitcast(F32), ALU.subtract).then_inc(ym_lo, 1)

            with dve.Fori(0, 2) as t:
                for j in range(4):
                    c = 4 * t + j
                    dve.wait_ge(z_done, c + (T_WM + 3))
                    tt(halved(sgm, c), zps(j % 2), halved(sgm, c), ALU.mult).then_inc(z_free, 1)
                    dve.wait_ge(z_free, c + (T_WM + 3))
                    tt(sgm[:, bass.ds(c, 1), :], sgm[:, bass.ds(c, 1), :], sga[:, bass.ds(c, 1), :], ALU.add)\
                        .then_inc(uu_rdy, 1)

            def gated_sample(j):
                dve.wait_ge(ot_act, j + 1)
                tt(oT[:, j % 2, T:NT], oS[:, j % 2, :], modT[:, 16 + j, 0:B], ALU.mult).then_inc(ot_rdy, 1)

            dve.wait_ge(ld_xo, 48)
            for j in range(8):
                gated_sample(j)
                s = j % 2
                col = slice(j * P, (j + 1) * P)
                dve.wait_ge(ot_mm, j + 1)
                tt(xN[:, :, col], xN[:, :, col], ps[:, 4 + 2 * s, :].rearrange("p (i n) -> p i n", i=TT), ALU.add)
                tt(xs2[:, col], xs2[:, col], ps[0:B, 5 + 2 * s, 0:P], ALU.add).then_inc(y_acc, 1)
            dve.wait_ge(y_sq, 1)
            v.tensor_scalar(rstd[:, :], ss[:, :], 1.0 / D, EPS, ALU.mult, ALU.add).then_inc(y_var, 1)
            dve.wait_ge(y_std, 1)
            chain(v.reciprocal(rstd[:, :], ss[:, :]))
            for j in range(TT):
                v.scalar_tensor_tensor(xN[:, j, :], xN[:, j, :], rstd[:, j:j + 1], fg, ALU.mult, ALU.mult)\
                    .then_inc(y_rdy, 1)
            v.scalar_tensor_tensor(xs2, xs2, rstd[0:B, 4:5], fg[0:B, :], ALU.mult, ALU.mult).then_inc(y_rdy, 1)

_INS = ["x_prompt", "x_sample", "cache_k", "cache_v", "state_C", "state_n", "state_m", "state_conv",
        "page_table", "c_prompt", "c_sample", "w_ada", "b_ada", "norm_g", "w_in", "b_if", "w_conv",
        "b_conv", "m_norm_g", "w_att", "w_mlstm", "w_out", "final_g"]
_OUTS = [("y_p", (1, T, D)), ("y_s", (B, 1, D)),
         ("k_p", (1, 1, T, AH, DH)), ("v_p", (1, 1, T, AH, DH)),
         ("C_p", (1, 1, MH, MV, MQ)), ("n_p", (1, 1, MH, MQ)), ("m_p", (1, 1, MH)),
         ("conv_p", (1, 1, 3, D)),
         ("k_s", (1, B, 1, AH, DH)), ("v_s", (1, B, 1, AH, DH)),
         ("C_s", (1, B, MH, MV, MQ)), ("n_s", (1, B, MH, MQ)), ("m_s", (1, B, MH)),
         ("conv_s", (1, B, 3, D))]


def kernel(**inputs):
    import numpy as np
    import concourse.bacc as bacc
    from concourse.bass_utils import run_bass_kernel_spmd

    nc = bacc.Bacc("TRN2", target_bir_lowering=False, num_devices=1)
    arrays, ins, outs = {}, {}, {}
    for name in _INS:
        a = np.ascontiguousarray(inputs[name])
        arrays["in_" + name] = a
        ins[name] = nc.dram_tensor("in_" + name, a.shape, mybir.dt.from_np(a.dtype), kind="ExternalInput").ap()
    for name, shape in _OUTS:
        outs[name] = nc.dram_tensor("out_" + name, shape, F32, kind="ExternalOutput").ap()
    decoder_step(nc, ins, outs)
    r = run_bass_kernel_spmd(nc, [arrays], core_ids=[0])
    return tuple(r.results[0]["out_" + name] for name, _ in _OUTS)
```

```python
from contextlib import ExitStack

import concourse.bass as bass
from concourse import mybir

ALU = mybir.AluOpType
ACT = mybir.ActivationFunctionType
F32 = mybir.dt.float32
F32R = mybir.dt.float32r
I32 = mybir.dt.int32
AX = mybir.AxisListType.X

P = 128
D = 1024
KT = D // P
T = 512
TT = T // P
B = 8
NT = T + B
HALF = NT // 2
AH, DH = 8, 64
AW = AH * DH
PAIRS = AW // P
MH, MQ, MV = 4, 128, 256
PAGE, PAGES = 128, 16
NBLK = 8
TOPK = 3
EPS = 1e-6
NEG = -1e30
SCALE = DH ** -0.5
KSCALE = MQ ** -0.5

CQ, CK, CV, CZ = 0, 512, 1024, 1536
CMQK, CMV, CMO, CMZ = 2048, 3072, 4096, 5120
CIF, CGA, CGM = 6144, 6152, 7176

T_ATT, T_ML = 0, 16
T_GATE = T_ML + 32
T_WA = T_GATE + 16
T_WM = T_WA + 8
T_OUT = T_WM + 8
T_ALL = T_OUT + 8

STEP_PAGES = 4
KV_SLOTS = 4
V_G, V_MG, V_BC, V_WC, V_BA = 0, 8, 16, 24, 56
V_ROWS = V_BA + 24


class Chain:

    def __init__(self, eng, sem):
        self.eng, self.sem, self.base, self.k = eng, sem, 0, 0

    def __call__(self, ins):
        ins.then_inc(self.sem, 1)
        self.k += 1
        self.eng.wait_ge(self.sem, self.base + self.k)

    def loop(self, i, per):
        self.start = self.base + self.k
        self.base, self.k, self.per = self.start + i * per, 0, per

    def end(self, trips):
        assert self.k == self.per, (self.k, self.per)
        self.base, self.k = self.start + trips * self.per, 0


def decoder_step(nc, I, O):
    x_p = I["x_prompt"].rearrange("b s d -> (b s) d")
    x_s = I["x_sample"].rearrange("b s d -> (b s) d")
    w_in = I["w_in"][0].rearrange("(k p) n -> p k n", p=P)
    w_ada = I["w_ada"][0].rearrange("(k p) n -> p k n", p=P)
    w_att = I["w_att"][0].rearrange("(k p) n -> p k n", p=P)
    w_ml = I["w_mlstm"][0].rearrange("(k p) n -> p k n", p=P)
    w_out = I["w_out"][0].rearrange("(k p) n -> p k n", p=P)
    pages_k = I["cache_k"][0].rearrange("n t h d -> t n (h d)")
    pages_v = I["cache_v"][0].rearrange("n t h d -> t n (h d)")
    state_c = I["state_C"][0].rearrange("b h (u v) d -> v b (h u) d", v=P)
    new_c = O["C_s"][0].rearrange("b h (u v) d -> v b (h u) d", v=P)
    n_phys = I["cache_k"].shape[1]
    y_rows = O["y_p"].rearrange("o (j p) d -> p (o j) d", p=P)

    with ExitStack() as ctx:
        names = set()

        def sb(name, shape, dt=F32):
            return ctx.enter_context(nc.sbuf_tensor("sb_" + name, shape, dt))

        def sem(name):
            assert name not in names
            names.add(name)
            return ctx.enter_context(nc.semaphore(name))

        ps = ctx.enter_context(nc.psum_tensor("ps", [P, 8, 512], F32))

        def zps(slot):
            return ps[:, 2 * slot:2 * slot + 2, 0:HALF]

        def halves(ap):
            return ap.rearrange("p (a n) -> p a n", a=2)

        ident = sb("ident", [P, P])
        ones = sb("ones", [P, P])
        cmask = sb("cmask", [P, P])
        upper = sb("upper", [P, P])
        rowsel = sb("rowsel", [B, B + 2, P])
        colsel = sb("colsel", [P, B, B])
        earlier = sb("earlier", [B, NBLK, NBLK])
        headsel = sb("headsel", [P, 2, P])
        vcol = sb("vcol", [P, V_ROWS])
        modT = sb("modT", [P, 24, 9])
        hscale = sb("hscale", [P, KT, 9])
        ptab = sb("ptab", [1, B * PAGES], I32)
        bif = sb("bif", [P, 2 * MH])
        hH = sb("hH", [P, KT, NT], F32R)
        hL = sb("hL", [P, KT, NT], F32R)
        hS = sb("hS", [P, KT, B])
        wraw = sb("wraw", [P, 4, KT, P])
        wH = sb("wH", [P, 2, KT, P], F32R)
        wL = sb("wL", [P, 2, KT, P], F32R)
        with nc.sbuf_tensor("sb_gated", [P, 6240], F32) as gated:
            pass
        ymT = gated[:, 0:4160].rearrange("p (k n) -> p k n", k=KT)
        yaT = gated[:, 4160:6240].rearrange("p (k n) -> p k n", k=PAIRS)
        uH = sb("uH", [P, KT, NT], F32R)
        sb("uH_rest", [P, 2080])
        mod = gated[0:9, 0:3072]
        cN = gated[0:9, 3072:4096]
        stC = gated[0:3 * B, 5184:6208]
        with nc.sbuf_tensor("sb_arenaA", [P, 10240], F32) as arenaA:
            pass
        page = arenaA[:, 0:8192].rearrange("p (s n) -> p s n", s=KV_SLOTS)
        qbc = arenaA[:, 8192:9216].rearrange("p (s n) -> p s n", s=2)
        vacc = qbc
        score = arenaA[:, 9216:10240]
        ada = arenaA[:, 0:8192].rearrange("p (s k n) -> p s k n", s=2, k=KT)
        yaH = sb("yaH", [P, PAIRS, NT], F32R)
        yaL = sb("yaL", [P, PAIRS, NT], F32R)
        with nc.sbuf_tensor("sb_kqr", [B, 2304], F32R) as kqr:
            pass
        selg = kqr[:, 2048:2304].rearrange("p (s n) -> p s n", s=2)
        uL = sb("uL", [P, KT, NT], F32R)
        sb("arenaA_rest", [P, 10240 - 8320])
        with nc.sbuf_tensor("sb_arenaB", [P, 11900], F32) as arenaB:
            pass
        sb("arenaB_rest", [P, 10620])
        qsr = sb("qsr", [B, 1280], F32R)
        selc = qsr[:, 1024:1280].rearrange("p (s n) -> p s n", s=2)
        used = [0]

        def work(n, shape=None, **kw):
            ap = arenaB[:, used[0]:used[0] + n]
            used[0] += n
            assert used[0] <= 11900, used
            return ap.rearrange(shape, **kw) if shape else ap

        cT = work(KT * 9, "p (k n) -> p k n", k=KT)
        vrow = work(P)[0:V_ROWS, :]
        xt = work(TT * D, "p (s n) -> p s n", s=TT)
        htmp = work(2 * D, "p (s k n) -> p s k n", s=2, k=KT)
        xsN = work(D)[0:B, :]
        sqj = work(D)
        used[0] = 0
        qT = work(NT)
        kT = work(NT)
        vT = work(NT)
        vN = work(TT * P, "p (j n) -> p j n", j=TT)
        kN = work(TT * P, "p (j n) -> p j n", j=TT)
        prA = work(2 * TT * T, "p (e j n) -> p e j n", e=2, j=TT)
        pT = work(TT * T, "p (j n) -> p j n", j=TT)
        used[0] = 0
        pre = work(2 * (NT + 4), "p (e n) -> p e n", e=2)
        cacc = work(2 * T, "p (e n) -> p e n", e=2)
        qkc = work(2 * T, "p (e n) -> p e n", e=2)
        mvT = work(2 * NT, "p (u n) -> p u n", u=2)
        v1 = work(TT * 257, "p (j n) -> p j n", j=TT)
        go = work(2 * NT, "p (u n) -> p u n", u=2)
        gz = work(2 * NT, "p (u n) -> p u n", u=2)
        wtF = work(4 * 640)
        sqh = cacc[:, :, :].rearrange("p e n -> p (e n)").rearrange("p (q n) -> p q n", q=TT)
        wt = wtF.rearrange("p (j n) -> p j n", n=640)
        hn = wtF[:, 0:TT * 257].rearrange("p (j n) -> p j n", j=TT)
        kw = work(TT * P, "p (j n) -> p j n", j=TT)
        cout = work(3 * P)
        selm = work(P)[0:MH, :]
        used[0] = 0
        sga = work(KT * NT, "p (k n) -> p k n", k=KT)
        sgm = work(KT * NT, "p (k n) -> p k n", k=KT)
        cS = work(2 * D, "p (s n) -> p s n", s=2)
        cW = (work(D), score)
        used[0] = 0
        oT = work(2 * NT, "p (s n) -> p s n", s=2)
        oS = work(2 * B, "p (s n) -> p s n", s=2)
        xN = arenaA[:, 0:TT * D].rearrange("p (j n) -> p j n", j=TT)
        yN = work(TT * D, "p (j n) -> p j n", j=TT)
        ysN = work(D)[0:B, :]
        used[0] = 2 * KT * NT
        xs2 = work(D)[0:B, :]
        fg = work(D)
        osq = work(D)
        ssq = work(5 * KT, "p (c j) -> p c j", c=KT)

        qsN = sb("qsN", [B, AW])
        wif = sb("wif", [P, KT, 2 * MH])
        wif2 = sb("wif2", [P, KT, 4 * MH], F32R)
        pairsum = sb("pairsum", [4 * MH, 2 * MH])
        ss = sb("ss", [P, 5])
        rstd = sb("rstd", [P, 5])
        G = sb("G", [P, 5, 2 * MH])
        gf = sb("gf", [P, 5, MH])
        lf = sb("lf", [P, 5, MH])
        bc = sb("bc", [P, TT, MH])
        ec = sb("ec", [P, TT, MH])
        Mc = sb("Mc", [P, TT, MH])
        mt = sb("mt", [P, TT, MH])
        em = sb("em", [P, TT, MH])
        scr = sb("scr", [P, 1536])
        eR = scr[0:MH, 0:T]
        gT = scr[0:4 * MH, 0:NT]
        MR = sb("MR", [MH, T])
        m0 = sb("m0", [B, MH])
        gs = sb("gs", [B, 4, MH])
        aw = sb("aw", [B, 2, MH])
        mx = sb("mx", [P, 2, TT])
        nmx = sb("nmx", [P, 2, TT])
        rsum = sb("rsum", [P, 2, TT])
        rinv = sb("rinv", [P, 2, TT])
        qkvS = sb("qkvS", [P, 3, PAIRS, B])
        selfp = sb("selfp", [P, B, AH])
        yaS = sb("yaS", [P, PAIRS, B])
        tS = sb("tS", [P, PAIRS, B])
        bsum = sb("bsum", [B, AH, NBLK])
        cmpA = scr[0:B, 0:512].rearrange("p (h n m) -> p h n m", h=AH, n=NBLK)
        cmpB = scr[0:B, 512:1024].rearrange("p (h n m) -> p h n m", h=AH, n=NBLK)
        pen = sb("pen", [B, AH * NBLK])
        pend = scr[0:B, 1024:1536].rearrange("p (b n) -> p b n", b=B)
        mxA = sb("mxA", [P, B * AH])
        mx64 = sb("mx64", [B * AH, 1])
        dg64 = sb("dg64", [B * AH, B * AH])
        preS = sb("preS", [P, KT, 11])
        preN = scr[0:11, 512:1536]
        stT = sb("stT", [P, KT, 3 * B])
        cvS = sb("cvS", [P, KT, B])
        cvT = sb("cvT", [P, KT, B])
        vS = sb("vS", [P, KT, B])
        wsc = sb("wsc", [P, TT])
        dl = sb("dl", [P, 4, TT])
        ssm = sb("ssm", [P, TT])
        kqN = sb("kqN", [B, 2 * AW])
        ksN = kqN[:, :].rearrange("p (a n) -> p a n", a=2)
        nN = qsN[:, :].rearrange("p (h n) -> p h n", h=MH)
        nT = scr[0:B, 0:512].rearrange("p (h n) -> p h n", h=MH)
        dS = sb("dS", [B, 3, MH])
        abc = sb("abc", [P, B, 2 * MH])
        rbc = sb("rbc", [P, B, MH])
        dgS = sb("dgS", [B, B, 2 * MH])
        Cq = sb("Cq", [P, KT, B])
        sqS = sb("sqS", [P, KT, B])
        rmsS = sb("rmsS", [P, MH, B])

        ld_c, ld_vec, ld_small, ld_x, ld_xs = (sem(n) for n in ("ld_c", "ld_vec", "ld_small", "ld_x", "ld_xs"))
        ld_st, ld_n, ld_xo = (sem(n) for n in ("ld_st", "ld_n", "ld_xo"))
        ld_ada = [sem(f"ld_ada{i}") for i in range(2)]
        ld_w = [sem(f"ld_w{i}") for i in range(4)]
        ld_page = [sem(f"ld_page{i}") for i in range(KV_SLOTS)]
        ld_C = [sem(f"ld_C{i}") for i in range(2)]
        hi_done = sem("hi_done")
        lo_done = sem("lo_done")
        z_done = sem("z_done")
        z_free = sem("z_free")
        page_free = [sem(f"page_free{i}") for i in range(KV_SLOTS)]
        pool_mult = sem("pool_mult")
        consts, id_rdy, ss_set, c_silu, t_c, c_T, t_vec, v_col = (
            sem(n) for n in ("consts", "id_rdy", "ss_set", "c_silu", "t_c", "c_T", "t_vec", "v_col"))
        ada_used, ada_ev, t_mod, mod_rdy, x_sq, x_var, x_std, x_nrm = (
            sem(n) for n in ("ada_used", "ada_ev", "t_mod", "mod_rdy", "x_sq", "x_var", "x_std", "x_nrm"))
        t_x, h_rdy, h_hi, h_lo, q_ev, if_hi, if_lo = (
            sem(n) for n in ("t_x", "h_rdy", "h_hi", "h_lo", "q_ev", "if_hi", "if_lo"))
        gt_mm, gt_ev, g_mm, g_dve, g_act, g_pe, t_st, st_ev = (
            sem(n) for n in ("gt_mm", "gt_ev", "g_mm", "g_dve", "g_act", "g_pe", "t_st", "st_ev"))
        selc_rdy, qbc_mm, qbc_rdy, qk_done, smx, sexp, pnorm, pt_mm, pt_ev, pt4_ev = (
            sem(n) for n in ("selc_rdy", "qbc_mm", "qbc_rdy", "qk_done", "smx", "sexp", "pnorm", "pt_mm", "pt_ev",
                           "pt4_ev"))
        kn_mm, kn_ev, vn_mm, vn_ev, pv_done, ya_done = (
            sem(n) for n in ("kn_mm", "kn_ev", "vn_mm", "vn_ev", "pv_done", "ya_done"))
        sel_pe, sel_dve, sel_act, mx_read = sem("sel_pe"), sem("sel_dve"), sem("sel_act"), sem("mx_read")
        vsum_rdy, ys_mm, ys_ev, selm_rdy, mb_mm, w_exp, w_rdy, mlast_rdy, wsc_rdy = (
            sem(n) for n in ("vsum_rdy", "ys_mm", "ys_ev", "selm_rdy", "mb_mm", "w_exp", "w_rdy", "mlast_rdy", "wsc_rdy"))
        cv_rdy, sg_rdy, qk_rdy, st_mm, vt_mm, vt_ev, mpt_rdy, kt_mm, kw_rdy = (
            sem(n) for n in ("cv_rdy", "sg_rdy", "qk_rdy", "st_mm", "vt_mm", "vt_ev", "mpt_rdy", "kt_mm", "kw_rdy"))
        pv_mm, hn_ev, rs1_rdy, rs2_rdy, hn_rdy, cc_mm, c_ev, ht_mm, ym_done, v_one = (
            sem(n) for n in ("pv_mm", "hn_ev", "rs1_rdy", "rs2_rdy", "hn_rdy", "cc_mm", "c_ev", "ht_mm", "ym_done", "v_one"))
        sam_pe, sam_dve, sam_act, abc_rdy = sem("sam_pe"), sem("sam_dve"), sem("sam_act"), sem("abc_rdy")
        selg_rdy, kq_mm, cw_rdy, c_used, kq_used, cnew_rdy = (
            sem(n) for n in ("selg_rdy", "kq_mm", "cw_rdy", "c_used", "kq_used", "cnew_rdy"))
        fin_pe, fin_dve, fin_act, ya_rdy, ya_hi, ym_hi, ya_lo, ym_lo = (
            sem(n) for n in ("fin_pe", "fin_dve", "fin_act", "ya_rdy", "ya_hi", "ym_hi", "ya_lo", "ym_lo"))
        uu_rdy, u_hi, u_lo, ot_act, ot_rdy, ot_mm, y_acc, y_sq, y_var, y_std, y_rdy, y_gain, y_act, q_lo, kq_lo, st_y2 = (
            sem(n) for n in ("uu_rdy", "u_hi", "u_lo", "ot_act", "ot_rdy", "ot_mm", "y_acc", "y_sq", "y_var", "y_std", "y_rdy", "y_gain", "y_act",
                               "q_lo", "kq_lo", "st_y2"))
        st_k, st_v, st_misc, st_pre, st_c, st_y = (
            sem(n) for n in ("st_k", "st_v", "st_misc", "st_pre", "st_c", "st_y"))
        st_C = [sem(f"st_C{i}") for i in range(2)]
        dve_chain, act_chain, pool_chain = sem("dve_chain"), sem("act_chain"), sem("pool_chain")

        ADA_COLS = (1024, 1536, 0, 512, 2048, 2560)
        block = ctx.enter_context(nc.Block())

        @block.sync
        def _(sp):
            def tile(j, n, src):
                sp.wait_ge(lo_done, n + 1)
                sp.dma_start(wraw[:, j % 4, 0:src.shape[1], :], src).then_inc(ld_w[j % 4], 16)

            def step(pages, s, count, first):
                sp.wait_ge(page_free[s % 4], count)
                for i in range(STEP_PAGES):
                    number = sp.value_load(ptab[0:1, bass.ds(first + i, 1)], min_val=0, max_val=n_phys - 1)
                    sp.dma_start(page[:, s % 4, i * AW:(i + 1) * AW],
                                 pages[:, bass.ds(number, 1), :].rearrange("t o n -> t (o n)")
                                 ).then_inc(ld_page[s % 4], 16)

            sp.dma_start(cN[0:B, :], I["c_sample"]).then_inc(ld_c, 16)
            sp.dma_start(cN[B:B + 1, :], I["c_prompt"]).then_inc(ld_c, 16)
            for i in range(2):
                sp.dma_start(ada[:, i], w_ada[:, :, ADA_COLS[i]:ADA_COLS[i] + 512]).then_inc(ld_ada[i], 16)
            sp.dma_start(xt, x_p.rearrange("(j p) d -> p j d", p=P)).then_inc(ld_x, 16)
            sp.dma_start(xsN, x_s).then_inc(ld_xs, 16)
            sp.dma_start(ptab[:, :], I["page_table"].rearrange("b n -> (b n)").rearrange("(o n) -> o n", o=1)
                         ).then_inc(ld_small, 16)
            sp.dma_start(bif[:, :], I["b_if"][0:1].broadcast_to([P, 2 * MH])).then_inc(ld_small, 16)
            sp.dma_start(wif[:, :, :], w_in[:, :, CIF:CIF + 2 * MH]).then_inc(ld_small, 16)
            sp.dma_start(m0[:, :], I["state_m"][0]).then_inc(ld_small, 16)
            sp.dma_start(stC, I["state_conv"][0].rearrange("b j d -> (b j) d")).then_inc(ld_st, 16)
            for i in range(2, 7):
                if i == 4:
                    for j in range(4):
                        tile(j, T_ATT + j, w_in[:, :, (CQ, CK, CV, CZ)[j]:(CQ, CK, CV, CZ)[j] + P])
                sp.wait_ge(ada_used, i - 1)
                src = w_ada[:, :, ADA_COLS[i]:ADA_COLS[i] + 512] if i < 6 else w_in[:, :, CQ:CQ + AW]
                sp.dma_start(ada[:, i % 2], src).then_inc(ld_ada[i % 2], 16)
            sp.wait_ge(ld_small, 64)

            def att_tile(j, t):
                return w_in[:, :, bass.ds(t * P + (CQ, CK, CV, CZ)[j], P)]

            def ml_tile(j, h):
                col, by = ((CMQK, MQ), (CMQK + MH * MQ, MQ), (CMV, MV), (CMV + P, MV), (CMO, MV), (CMO + P, MV),
                           (CMZ, MV), (CMZ + P, MV))[j]
                return w_in[:, :, bass.ds(h * by + col, P)]

            def gate_tile(j, t):
                return w_in[:, :, bass.ds(t * 2 * P + (j // 2) * P + (CGA, CGM)[j % 2], P)]

            def four(w):
                return lambda j, t: w[:, :, bass.ds(t * 4 * P + j * P, P)]

            sp.wait_ge(ada_used, 7)

            def attention(t, following, tt_):
                n = T_ATT + 4 * t + 4
                tile(0, n, following(0, tt_))
                tile(1, n + 1, following(1, tt_))
                for s in range(8):
                    if s in (2, 4):
                        tile(1 + s // 2, n + 1 + s // 2, following(1 + s // 2, tt_))
                    step(pages_k, s, 2 * t + s // 4 + 1, 32 * t + 4 * s)

            with sp.Fori(0, PAIRS - 1) as t:
                attention(t, att_tile, t + 1)
            attention(PAIRS - 1, ml_tile, 0)
            sp.wait_ge(qbc_mm, 2 * PAIRS)
            sp.dma_start(qsN[:, :], I["state_n"][0].rearrange("b h d -> b (h d)")).then_inc(ld_n, 16)

            def mlstm(h, following, hh):
                n = T_ML + 8 * h + 4
                for j in range(8):
                    tile(j, n + j, ml_tile(j + 4, h) if j < 4 else following(j - 4, hh))
                    step(pages_v, j, 8 + 2 * h + j // 4 + 1, 32 * h + 4 * j)

            for j in (0, 1, 2, 3, "v0", "v1", 4, "v2", 5, "v3", 6, "v4", "v5", 7, "v6", "v7"):
                if isinstance(j, int):
                    tile(j, T_ML + 4 + j, ml_tile(j + 4, 0) if j < 4 else ml_tile(j - 4, 1))
                else:
                    s = int(j[1])
                    step(pages_v, s, 8 + s // 4 + 1, 4 * s)
            with sp.Fori(0, MH - 2) as h:
                mlstm(h + 1, ml_tile, h + 2)
            mlstm(MH - 1, gate_tile, 0)

            def states(e, t):
                sp.wait_ge(c_used, 2 * t + e + 1)
                sp.dma_start(cS[:, e].rearrange("p (u d) -> p u d", u=KT),
                             state_c[:, bass.ds(2 * t + e, 1)].rearrange("v o u d -> v (o u) d")).then_inc(ld_C[e], 16)

            for j in range(4):
                tile(j, T_GATE + 4 + j, gate_tile(j, 1))
                if j == 1:
                    sp.wait_ge(ym_done, 1 + MH)
                    sp.wait_ge(st_c, 16 * (2 * MH + 2))
                    states(0, 0)
            states(1, 0)
            with sp.Fori(0, 2) as t:
                for j in range(4):
                    tile(j, T_GATE + 4 * t + 8 + j, gate_tile(j, t + 2))
                    if j % 2 == 1:
                        states(j // 2, t + 1)
            for j in range(4):
                tile(j, T_WA + j, four(w_att)(j, 0))
            for e in range(2):
                states(e, 3)
            for n, w in ((T_WA + 4, w_att), (T_WM, w_ml), (T_WM + 4, w_ml), (T_OUT, w_out), (T_OUT + 4, w_out)):
                for j in range(4):
                    tile(j, n + j, four(w)(j, 1 if n in (T_WA + 4, T_WM + 4, T_OUT + 4) else 0))
                if n == T_WM:
                    sp.wait_ge(z_done, 2 + T_WM)
                    for e in range(2):
                        sp.wait_ge(st_C[e], 16 + 16 * B // 2)
                    sp.wait_ge(c_used, 2 + B)
                    sp.dma_start(xN, x_p.rearrange("(j p) d -> p j d", p=P)).then_inc(ld_xo, 16)
                    sp.dma_start(xs2, x_s).then_inc(ld_xo, 16)
                    sp.dma_start(fg, I["final_g"].rearrange("(o n) -> o n", o=1).broadcast_to([P, D])).then_inc(ld_xo, 16)
            for i, j in enumerate((0, 2)):
                sp.wait_ge(y_rdy, i + 1)
                sp.dma_start(y_rows[:, j, :], yN[:, j, :]).then_inc(st_y, 16)
            sp.wait_ge(y_rdy, 3)
            sp.dma_start(O["y_s"].rearrange("b o d -> (b o) d"), ysN).then_inc(st_y, 16)
            sp.wait_ge(st_y, 48)

        @block.tensor
        def _(pe):
            mm = nc.tensor.matmul
            tr = nc.tensor.transpose

            def ztile(j, n, xH, xL, ks=KT, part_ready=None):
                pe.wait_ge(lo_done, n + 5)
                pe.wait_ge(z_free, n + 1)
                s = j % 2
                for k in range(ks):
                    if part_ready:
                        pe.wait_ge(part_ready, 2 + k + 1)
                    for w, xs_ in ((wH, (xH, xL)), (wL, (xH,))):
                        for x in xs_:
                            for a in range(2):
                                last = mm(ps[:, 2 * s + a, 0:HALF], w[:, s, k, :], x[:, k, a * HALF:(a + 1) * HALF],
                                          start=(k == 0 and w is wH and x is xH), stop=(k == ks - 1 and w is wL))
                last.then_inc(z_done, 1)

            pe.sem_inc(z_done, 2)
            pe.wait_ge(id_rdy, 1)
            pe.wait_ge(c_silu, 1)
            for k in range(KT):
                last = tr(ps[:, 4, 9 * k:9 * k + 9], cN[:, k * P:(k + 1) * P], ident[0:9, 0:9])
            last.then_inc(t_c, 1)
            pe.wait_ge(c_T, 1)

            def modulation(i):
                pe.wait_ge(ld_ada[i % 2], 16 * (i // 2 + 1))
                if i >= 2:
                    pe.wait_ge(ada_ev, i - 1)
                for k in range(KT):
                    last = mm(ps[0:9, i % 2, :], cT[:, k, :], ada[:, i % 2, k, :], start=(k == 0), stop=(k == KT - 1))
                last.then_inc(ada_used, 1)

            def mod_turn(lo, hi):
                for j in range(lo, hi):
                    last = tr(ps[:, 5, 9 * (j - lo):9 * (j - lo) + 9], mod[:, j * P:(j + 1) * P], ident[0:9, 0:9])
                last.then_inc(t_mod, 1)

            def token_turn(j):
                b = 2 if j % 2 == 0 else 6
                for k in range(KT):
                    last = tr(ps[:, b + k // 4, (k % 4) * P:(k % 4 + 1) * P], xt[:, j, k * P:(k + 1) * P], ident[:, :])
                last.then_inc(t_x, 1)

            modulation(0)
            modulation(1)
            pe.wait_ge(ld_vec, 80)
            tr(ps[:, 5, 0:V_ROWS], vrow, ident[0:V_ROWS, 0:V_ROWS]).then_inc(t_vec, 1)
            modulation(2)
            pe.wait_ge(x_nrm, 1)
            token_turn(0)
            token_turn(1)
            for k in range(KT):
                last = tr(ps[:, 4, B * k:B * k + B], xsN[:, k * P:(k + 1) * P], ident[0:B, 0:B])
            last.then_inc(t_x, 1)
            modulation(3)
            pe.wait_ge(ada_ev, 4)
            pe.wait_ge(v_col, 1)
            mod_turn(0, 16)
            modulation(4)
            pe.wait_ge(h_rdy, 1)
            token_turn(2)
            pe.wait_ge(h_rdy, 2)
            token_turn(3)
            modulation(5)
            pe.wait_ge(ld_ada[0], 64)
            pe.wait_ge(h_rdy, 3)
            pe.wait_ge(consts, 1)
            pe.wait_ge(ada_ev, 5)
            for k in range(KT):
                last = mm(ps[0:B, 0, :], hS[:, k, :], ada[:, 0, k, :], start=(k == 0), stop=(k == KT - 1))
            last.then_inc(ada_used, 1)
            pe.wait_ge(ada_ev, 6)
            pe.wait_ge(mod_rdy, 1)
            mod_turn(16, 24)
            pe.wait_ge(ld_st, 16)
            pe.wait_ge(h_rdy, 4)
            for k in range(KT):
                last = tr(ps[:, 2, 24 * k:24 * k + 24], stC[:, k * P:(k + 1) * P], ident[0:24, 0:24])
            last.then_inc(t_st, 1)
            pe.wait_ge(h_lo, TT + 1)
            pe.wait_ge(if_lo, 1)
            pe.wait_ge(mod_rdy, 2)
            for k in range(KT):
                for x in (hH, hL):
                    for a in range(2):
                        last = mm(ps[0:4 * MH, 4 + a, 0:HALF], wif2[:, k, :], x[:, k, a * HALF:(a + 1) * HALF],
                                  start=(k == 0 and x is hH), stop=(k == KT - 1 and x is hL))
            last.then_inc(gt_mm, 1)
            pe.wait_ge(q_ev, 1)
            pe.wait_ge(st_ev, 1)

            def qk(e, t):
                r = slice(DH * e, DH * e + DH)
                if e == 1:
                    pe.wait_ge(pt4_ev, 2 * t + 2)
                for q, b, c in (((2, 5, 0), (0, 5, 384), (1, 6, 0), (3, 4, 0)),
                                ((3, 4, 0), (2, 5, 0), (0, 5, 384), (1, 6, 0)))[e]:
                    if e == 0 and b == 4:
                        pe.wait_ge(qbc_rdy, 2 * t + 1)
                    if e == 1 and q == 2:
                        pe.wait_ge(pt_ev, 2 * t + 2)
                    last = mm(ps[:, b, c:c + (q + 1) * P], qT[r, q * P:(q + 1) * P], kT[r, 0:(q + 1) * P],
                              start=True, stop=True)
                last.then_inc(qk_done, 1)

            def ptrans(e):
                for k, b, c in ((0, 4, 0), (1, 5, 0), (3, 5, 384), (2, 6, 0)):
                    for q in range(k, TT):
                        last = tr(ps[:, b, c + (q - k) * P:c + (q - k + 1) * P], prA[:, e, q, k * P:(k + 1) * P],
                                  ident[:, :])
                last.then_inc(pt_mm, 1)

            def pv(e):
                for k in range(TT):
                    last = mm(ps[DH * e:DH * e + DH, 7, k * P:T], vN[:, k, DH * e:DH * e + DH], pT[:, k, k * P:T],
                              start=(k == 0), stop=(k == TT - 1))
                return last

            def query_copy(e, t, bank):
                pe.wait_ge(selc_rdy, 2 * t + e + 1)
                mm(ps[:, bank, :], selc[:, e, :], qsr[:, 0:AW], start=True, stop=False)
                mm(ps[:, bank, :], selc[:, e, :], qsr[:, AW:2 * AW], start=False, stop=True).then_inc(qbc_mm, 1)

            def attention(t, before):
                n = T_ATT + 4 * t
                ztile(0, n, hH, hL)
                if before:
                    pe.wait_ge(pnorm, 2 * t)
                    ptrans(1)
                else:
                    pe.wait_ge(gt_ev, 1)
                    pe.wait_ge(h_rdy, TT + 1)
                    for j in range(TT + 1):
                        tok = slice(j * P, min((j + 1) * P, NT))
                        last = mm(ps[0:tok.stop - tok.start, 6, 8 * j:8 * j + 8], gT[:, tok], pairsum[:, :],
                                  start=True, stop=True)
                    last.then_inc(g_mm, 1)
                ztile(1, n + 1, hH, hL)
                if not before:
                    pe.wait_ge(g_dve, 3)
                    for j in range(TT):
                        last = mm(ps[:, 7, MH * j:MH * j + MH], upper[:, :], lf[:, j, :], start=True, stop=(j == 0))
                        for i in range(j):
                            last = mm(ps[:, 7, MH * j:MH * j + MH], ones[:, :], lf[:, i, :], start=False,
                                      stop=(i == j - 1))
                    last.then_inc(g_pe, 1)
                pe.wait_ge(pt_ev, 2 * t + 1)
                query_copy(0, t, 4)
                if before:
                    pv(1).then_inc(pv_done, 1)
                pe.wait_ge(z_free, n + 4)
                qk(0, t)
                if not before:
                    pe.wait_ge(g_dve, 4)
                    for j in range(TT):
                        last = tr(ps[0:MH, 7, j * P:(j + 1) * P], ec[:, j, :], ident[:, :])
                    last.then_inc(g_pe, 1)
                ztile(2, n + 2, hH, hL)
                if not before:
                    pe.wait_ge(g_dve, 5)
                    for j in range(TT):
                        last = tr(ps[:, 7, MH * j:MH * j + MH], MR[:, j * P:(j + 1) * P], ident[0:MH, 0:MH])
                    last.then_inc(g_pe, 1)
                    pe.wait_ge(g_dve, 6)
                pe.wait_ge(ya_done, t + 1)
                for j in range(TT):
                    last = tr(ps[:, 7, j * P:(j + 1) * P], kT[:, j * P:(j + 1) * P], ident[:, :])
                last.then_inc(kn_mm, 1)
                ztile(3, n + 3, hH, hL)
                pe.wait_ge(kn_ev, t + 1)
                pe.wait_ge(z_free, n + 5)
                for j in range(TT):
                    last = tr(ps[:, 7, j * P:(j + 1) * P], vT[:, j * P:(j + 1) * P], ident[:, :])
                last.then_inc(vn_mm, 1)
                pe.wait_ge(pnorm, 2 * t + 1)
                ptrans(0)
                pe.wait_ge(vn_ev, t + 1)
                query_copy(1, t, 7)
                qk(1, t)
                pe.wait_ge(qbc_rdy, 2 * t + 2)
                pv(0)

            pe.wait_ge(q_lo, 1)
            attention(0, False)
            with pe.Fori(0, PAIRS - 1) as t:
                attention(t + 1, True)
            def page_sums(h, bank):
                pe.wait_ge(vsum_rdy, h)
                for e in range(2):
                    for c in range(PAIRS):
                        last = mm(ps[:, bank, PAIRS * e + c:PAIRS * e + c + 1], vacc[:, e, c * P:(c + 1) * P], ones[:, 0:1],
                                  start=True, stop=True)
                last.then_inc(ys_mm, 1)

            def spread_max(h):
                pe.wait_ge(selm_rdy, h + 1)
                pe.wait_ge(c_ev, h + 1)
                mm(ps[:, 7, :], selm, MR[:, :], start=True, stop=True).then_inc(mb_mm, 1)

            def mlstm(h, first):
                n = T_ML + 8 * h
                if not first:
                    ztile(0, n, hH, hL)
                    ztile(1, n + 1, hH, hL)
                    spread_max(h)
                    ztile(2, n + 2, hH, hL)
                    ztile(3, n + 3, hH, hL)
                    pe.wait_ge(hn_ev, 4 * h + 1)
                pe.wait_ge(sg_rdy, 2 * h + 2)
                pe.wait_ge(qk_rdy, h + 1)
                pe.wait_ge(ym_done, h + 1)
                for k, b, c in ((0, 4, 0), (1, 5, 0), (3, 5, 384), (2, 6, 0)):
                    last = mm(ps[:, b, c:c + T - k * P], qkc[:, 1, k * P:(k + 1) * P], qkc[:, 0, k * P:T],
                              start=True, stop=True)
                last.then_inc(st_mm, 1)
                if first:
                    pe.wait_ge(sel_dve, 4)
                    tr(ps[0:B * AH, 7, 0:P], mxA[:, :], ident[:, :]).then_inc(sel_pe, 1)
                    pe.wait_ge(sel_dve, 5)
                    mm(ps[:, 7, 128:192], ones[0:B * AH, :], dg64[:, :], start=True, stop=True).then_inc(sel_pe, 1)
                    pe.wait_ge(mx_read, 1)
                    spread_max(0)
                    ztile(2, n + 6, hH, hL)
                pe.wait_ge(w_exp, h + 1)
                pe.wait_ge(mlast_rdy, h + 1)
                pe.wait_ge(z_free, n + 6)
                for u in range(2):
                    if u == 1:
                        pe.wait_ge(vt_ev, 2 * h + 1)
                    for j in range(TT):
                        last = tr(ps[:, 7, j * P:(j + 1) * P], mvT[:, u, j * P:(j + 1) * P], ident[:, :])
                    last.then_inc(vt_mm, 1)
                    if not first:
                        ztile(u, n + 4 + u, hH, hL)
                if first:
                    pe.wait_ge(vt_ev, 2)
                    pe.wait_ge(sel_dve, 7)
                    mm(ps[:, 7, 256:320], ones[:, :], mxA[:, :], start=True, stop=True).then_inc(sel_pe, 1)
                else:
                    pe.wait_ge(vt_ev, 2 * h + 2)
                    page_sums(h, 7)
                pe.wait_ge(mpt_rdy, h + 1)
                for j in range(TT):
                    last = tr(ps[:, 6, j * P:(j + 1) * P], qkc[:, 1, j * P:(j + 1) * P], ident[:, :])
                last.then_inc(kt_mm, 1)
                pe.wait_ge(vt_ev, 2 * h + 2)
                pe.wait_ge(v_one, 1)
                if first:
                    pe.wait_ge(mx_read, 2)
                else:
                    pe.wait_ge(ys_ev, h)
                for q, b in ((0, 4), (1, 5), (2, 7), (3, 6)):
                    if q == 3:
                        pe.wait_ge(kw_rdy, h + 1)
                    for k in range(q + 1):
                        last = mm(ps[:, b, 0:MV + 1], wt[:, k, (q - k) * P:(q - k + 1) * P], v1[:, k, :],
                                  start=(k == 0), stop=(k == q))
                last.then_inc(pv_mm, 1)
                if not first:
                    ztile(2, n + 6, hH, hL)
                ztile(3, n + 7, hH, hL)
                pe.wait_ge(hn_ev, 4 * h + 5)
                for u in range(3):
                    for j in range(TT):
                        if u < 2:
                            last = mm(ps[:, 7, u * P:(u + 1) * P], v1[:, j, u * P:(u + 1) * P], kw[:, j, :],
                                      start=(j == 0), stop=(j == TT - 1))
                        else:
                            last = mm(ps[0:1, 7, 2 * P:3 * P], ones[:, 0:1], kw[:, j, :],
                                      start=(j == 0), stop=(j == TT - 1))
                last.then_inc(cc_mm, 1)
                pe.wait_ge(hn_rdy, h + 1)
                for u in range(2):
                    for j in range(TT):
                        last = tr(ps[:, 4 + u, j * P:(j + 1) * P], hn[:, j, u * P:(u + 1) * P], ident[:, :])
                last.then_inc(ht_mm, 1)

            ztile(0, T_ML, hH, hL)
            pe.wait_ge(pnorm, 2 * PAIRS)
            ptrans(1)
            ztile(1, T_ML + 1, hH, hL)
            pe.wait_ge(pt_ev, 2 * PAIRS + 1)
            pv(1).then_inc(pv_done, 1)
            ztile(2, T_ML + 2, hH, hL)
            pe.wait_ge(sel_dve, 1)
            for e in range(2):
                last = mm(ps[:, 4, 32 * e:32 * e + 32], headsel[:, e, :], tS[:, :, :].rearrange("p a b -> p (a b)"),
                          start=True, stop=True)
            last.then_inc(sel_pe, 1)
            for a in range(2):
                for t in range(PAIRS):
                    last = tr(ps[0:B, 5 + a, t * P:(t + 1) * P], qkvS[:, 1 + a, t, :], ident[:, :])
            last.then_inc(sel_pe, 1)
            ztile(3, T_ML + 3, hH, hL)
            pe.wait_ge(ya_done, 1 + PAIRS)
            pe.wait_ge(sel_dve, 2)
            for b in range(B):
                last = mm(ps[0:B, 7, 0:P], colsel[:, b, :], score[:, b * P:(b + 1) * P], start=(b == 0), stop=(b == B - 1))
            last.then_inc(sel_pe, 1)
            ztile(4, T_ML + 4, hH, hL)
            pe.wait_ge(sel_dve, 3)
            mm(ps[:, 7, :], ones[0:B, :], pend.rearrange("p b n -> p (b n)"), start=True, stop=True).then_inc(sel_pe, 1)
            ztile(5, T_ML + 5, hH, hL)
            pe.wait_ge(sel_act, 1)
            mlstm(0, True)
            with pe.Fori(0, MH - 1) as h:
                mlstm(h + 1, False)
            ztile(0, T_GATE, hH, hL)
            ztile(1, T_GATE + 1, hH, hL)
            pe.wait_ge(c_ev, 1 + MH)
            pe.wait_ge(ym_done, 1 + MH)
            pe.wait_ge(sam_dve, 1)
            mm(ps[:, 7, 0:64], ones[0:B, :], dgS[:, :, :].rearrange("p b n -> p (b n)"), start=True, stop=True)\
                .then_inc(sam_pe, 1)
            for k in range(KT):
                last = tr(ps[0:11, 4 + k // 4, (k % 4) * P:(k % 4 + 1) * P], preS[:, k, :], ident[:, :])
            last.then_inc(sam_pe, 1)
            ztile(2, T_GATE + 2, hH, hL)
            pe.wait_ge(sam_dve, 3)
            pe.wait_ge(sam_act, 2)
            for k in range(KT):
                last = tr(ps[0:B, 4 + k // 4, (k % 4) * P:(k % 4 + 1) * P], cvS[:, (k + 4) % KT, :], ident[:, :])
            last.then_inc(sam_pe, 1)
            ztile(3, T_GATE + 3, hH, hL)
            page_sums(MH, 6)
            pe.wait_ge(abc_rdy, 1)
            pe.wait_ge(sam_act, 3)
            pe.wait_ge(ys_ev, MH)
            pe.wait_ge(kq_lo, 1)

            def key_query(e, t):
                pe.wait_ge(selg_rdy, 2 * t + e + 1)
                pe.wait_ge(kq_used, 2 * t + e + 1)
                for a in range(2):
                    for part in range(2):
                        first = (2 * part + a) * AW
                        last = mm(ps[:, 4 + 2 * e + a, :], selg[:, e, :], kqr[:, first:first + AW],
                                  start=(part == 0), stop=(part == 1))
                last.then_inc(kq_mm, 1)

            with pe.Fori(0, 3) as t:
                n = T_GATE + 4 * t + 4
                for e in range(2):
                    key_query(e, t)
                    ztile(0, n + 2 * e, hH, hL)
                    ztile(1, n + 2 * e + 1, hH, hL)
            pe.wait_ge(sam_dve, 4)
            pe.wait_ge(kq_used, 2 + 6)
            mm(ps[:, 7, 64:96], ones[0:B, :], dgS[:, :, 0:MH], start=True, stop=True).then_inc(sam_pe, 1)
            pe.wait_ge(ya_lo, 1)
            for j in range(8):
                if j == 1:
                    pe.wait_ge(sam_dve, 5)
                if j < 2:
                    key_query(j, 3)
                ztile(j, T_WA + j, yaH, yaL, PAIRS)
                if j == 4:
                    pe.wait_ge(fin_dve, 1)
                    mm(ps[:, 4, 0:64], ones[:, :], sqS[:, :, :].rearrange("p k b -> p (k b)"), start=True, stop=True)\
                        .then_inc(fin_pe, 1)
            pe.wait_ge(ym_lo, 3)
            with pe.Fori(0, 2) as t:
                for j in range(4):
                    ztile(j, T_WM + 4 * t + j, hH, hL)

            def out_turn(s, j):
                pe.wait_ge(ot_rdy, j + 1)
                pe.wait_ge(y_acc, j + 1)
                for i in range(TT):
                    tr(ps[:, 4 + 2 * s, i * P:(i + 1) * P], oT[:, s, i * P:(i + 1) * P], ident[:, :])
                tr(ps[0:B, 5 + 2 * s, 0:P], oT[:, s, T:NT], ident[:, :]).then_inc(ot_mm, 1)

            ztile(0, T_OUT, uH, uL, part_ready=u_lo)
            ztile(1, T_OUT + 1, uH, uL)
            with pe.Fori(0, 3) as t:
                for s in range(2):
                    out_turn(s, 2 * t + s)
                    ztile(s, T_OUT + 2 * t + 2 + s, uH, uL)
            out_turn(0, 6)
            out_turn(1, 7)

        @block.scalar
        def _(act):
            chain = Chain(act, act_chain)
            f = nc.scalar.activation

            def high(j, n, quad, ks=KT):
                act.wait_ge(ld_w[j % 4], 16 * (quad + 1))
                act.wait_ge(z_done, n + 1)
                f(wH[:, j % 2, 0:ks], wraw[:, j % 4, 0:ks], ACT.Copy).then_inc(hi_done, 1)

            def leave(j, n, *dests):
                act.wait_ge(z_done, n + 3)
                for dst, func in dests:
                    ins = f(halves(dst), zps(j % 2), func)
                ins.then_inc(z_free, 1)

            act.sem_inc(z_free, 2)
            act.sem_inc(pt_ev, 1)
            act.sem_inc(pt4_ev, 1)
            act.sem_inc(hn_ev, 1)
            act.sem_inc(c_ev, 1)
            act.sem_inc(st_k, 16)
            act.sem_inc(st_v, 16)
            for e in range(2):
                act.sem_inc(st_C[e], 16)
            act.sem_inc(st_c, 32)
            for row, name in ((V_G, "norm_g"), (V_MG, "m_norm_g"), (V_BC, "b_conv"), (V_WC, "w_conv"),
                              (V_BA, "b_ada")):
                src = I[name][0:1] if name != "w_conv" else I[name][0]
                n = (src.shape[0] * src.shape[1]) // P
                act.dma_start(vrow[row:row + n, :], src.rearrange("a (r n) -> (a r) n", n=P)).then_inc(ld_vec, 16)
            act.wait_ge(ld_c, 32)
            f(cN, cN, ACT.Silu).then_inc(c_silu, 1)

            def ada_leave(i):
                act.wait_ge(ada_used, i + 1)
                f(mod[:, ADA_COLS[i]:ADA_COLS[i] + 512], ps[0:9, i % 2, :], ACT.Copy).then_inc(ada_ev, 1)

            ada_leave(0)
            act.wait_ge(ld_x, 16)
            act.wait_ge(ld_xs, 16)
            act.wait_ge(ss_set, 1)
            for j in range(TT):
                chain(f(sqj, xt[:, j, :], ACT.Square, accum_out=ss[:, j:j + 1]))
            f(sqj[0:B, :], xsN, ACT.Square, accum_out=ss[0:B, 4:5]).then_inc(x_sq, 1)
            act.wait_ge(x_var, 1)
            f(ss[:, :], rstd[:, :], ACT.Sqrt).then_inc(x_std, 1)
            for i in range(1, 4):
                ada_leave(i)
            act.wait_ge(ld_small, 64)
            f(wif2[:, :, 0:2 * MH], wif[:, :, :], ACT.Copy).then_inc(if_hi, 1)

            def h_high(i, j):
                act.wait_ge(h_rdy, i)
                f(hH[:, :, j * P:(j + 1) * P], htmp[:, j % 2], ACT.Copy).then_inc(h_hi, 1)

            h_high(1, 0)
            h_high(2, 1)
            act.wait_ge(h_rdy, 3)
            f(hH[:, :, T:NT], hS[:, :, :], ACT.Copy).then_inc(h_hi, 1)
            ada_leave(4)
            h_high(4, 2)
            h_high(5, 3)
            high(0, 0, 0)
            ada_leave(5)
            high(1, 1, 0)
            act.wait_ge(ada_used, 7)
            f(qsr[:, 0:AW], ps[0:B, 0, :], ACT.Copy)
            f(qsN[:, :], ps[0:B, 0, :], ACT.Copy).then_inc(q_ev, 1)
            act.wait_ge(t_st, 1)
            f(stT[:, :, :].rearrange("p k n -> p (k n)"), ps[:, 2, 0:192], ACT.Copy).then_inc(st_ev, 1)
            act.wait_ge(gt_mm, 1)
            f(halves(gT), ps[0:4 * MH, 4:6, 0:HALF], ACT.Copy).then_inc(gt_ev, 1)

            def gate_logs():
                act.wait_ge(g_dve, 2)
                chain(f(gf[:, :, :], gf[:, :, :], ACT.Exp))
                f(gf[:, :, :], gf[:, :, :], ACT.Ln, bias=1.0).then_inc(g_act, 1)

            def gate_exps():
                act.wait_ge(g_dve, 6)
                f(em[:, :, :], mt[:, :, :], ACT.Exp, scale=-1.0).then_inc(g_act, 1)
                act.wait_ge(g_dve, 7)
                f(aw[:, :, :], aw[:, :, :], ACT.Exp)
                f(gs[:, 2, :], gs[:, 1, :], ACT.Exp, scale=-1.0).then_inc(g_act, 1)
                act.dma_start(O["m_s"][0], gs[:, 1, :]).then_inc(st_misc, 16)
                act.dma_start(O["m_p"][0], mt[P - 1:P, TT - 1, :]).then_inc(st_misc, 16)

            def rows_out(dst, t):
                return dst.rearrange("o b (j p) h d -> p (o b j) (h d)", p=P)[:, :, bass.ds(t * P, P)]

            def weights(e, t):
                act.wait_ge(smx, 2 * t + e + 1)
                for q, b, c in ((3, 4, 0), (2, 5, 0), (0, 5, 384), (1, 6, 0)):
                    last = f(prA[:, e, q, 0:(q + 1) * P], ps[:, b, c:c + (q + 1) * P], ACT.Exp,
                             bias=nmx[:, e, q:q + 1], scale=SCALE, accum_out=rsum[:, e, q:q + 1])
                last.then_inc(sexp, 1)

            def turned(e, t):
                act.wait_ge(pt_mm, 2 * t + e + 1)
                for k, b, c in ((0, 4, 0), (1, 5, 0), (3, 5, 384), (2, 6, 0)):
                    last = f(pT[:, k, k * P:T], ps[:, b, c:c + T - k * P], ACT.Copy)
                    if b == 4:
                        last.then_inc(pt4_ev, 1)
                last.then_inc(pt_ev, 1)

            def copy_out(e, t, before):
                if before:
                    for slot in range(KV_SLOTS):
                        act.wait_ge(page_free[slot], 2 * t + e)
                act.wait_ge(qbc_mm, 2 * t + e + 1)
                f(qbc[:, e, :], ps[:, 4 + 3 * e, :], ACT.Copy).then_inc(qbc_rdy, 1)

            def attention(t, before):
                n, quad = T_ATT + 4 * t, t
                high(2, n + 2, quad)
                leave(0, n, (qT, ACT.Copy))
                if before:
                    turned(1, t - 1)
                else:
                    gate_logs()
                leave(1, n + 1, (kT, ACT.Copy))
                copy_out(0, t, before)
                high(3, n + 3, quad)
                weights(0, t)
                leave(0, n + 2, (vT, ACT.Copy))
                act.wait_ge(kn_mm, t + 1)
                act.wait_ge(st_k, 16 * t + 16)
                f(kN, ps[:, 7, :].rearrange("p (j n) -> p j n", j=TT), ACT.Copy).then_inc(kn_ev, 1)
                act.wait_ge(kn_ev, t + 1)
                act.dma_start(rows_out(O["k_p"], t), kN).then_inc(st_k, 16)
                high(0, n + 4, quad + 1)
                if not before:
                    gate_exps()
                act.wait_ge(vn_mm, t + 1)
                act.wait_ge(st_v, 16 * t + 16)
                f(vN, ps[:, 7, :].rearrange("p (j n) -> p j n", j=TT), ACT.Copy).then_inc(vn_ev, 1)
                act.wait_ge(vn_ev, t + 1)
                act.dma_start(rows_out(O["v_p"], t), vN).then_inc(st_v, 16)
                turned(0, t)
                copy_out(1, t, before)
                leave(1, n + 3, (yaT[:, bass.ds(t, 1), :].rearrange("p o n -> p (o n)"), ACT.Silu))
                high(1, n + 5, quad + 1)
                weights(1, t)

            attention(0, False)
            with act.Fori(0, PAIRS - 1) as t:
                attention(t + 1, True)
            high(2, T_ML + 2, T_ML // 4)
            leave(0, T_ML, (pre[:, 0, 3:3 + NT], ACT.Copy))
            turned(1, PAIRS - 1)
            high(3, T_ML + 3, T_ML // 4)
            leave(1, T_ML + 1, (pre[:, 1, 3:3 + NT], ACT.Copy))
            high(0, T_ML + 4, T_ML // 4 + 1)
            leave(0, T_ML + 2, (mvT[:, 0, :], ACT.Copy))
            act.wait_ge(sel_pe, 2)
            for a in range(2):
                last = f(ksN[:, a, :], ps[0:B, 5 + a, :], ACT.Copy)
            last.then_inc(sel_act, 1)
            act.wait_ge(sel_act, 1)
            act.dma_start(O["k_s"].rearrange("o b q h d -> (o b q) (h d)"), ksN[:, 0, :]).then_inc(st_misc, 16)
            act.dma_start(O["v_s"].rearrange("o b q h d -> (o b q) (h d)"), ksN[:, 1, :]).then_inc(st_misc, 16)
            high(1, T_ML + 5, T_ML // 4 + 1)
            leave(1, T_ML + 3, (mvT[:, 1, :], ACT.Copy))
            act.wait_ge(ya_done, 1 + PAIRS)
            act.wait_ge(st_k, 16 * (1 + PAIRS))
            act.wait_ge(st_v, 16 * (1 + PAIRS))
            for e in range(2):
                act.wait_ge(cv_rdy, e + 1)
                f(qkc[:, e, :], cacc[:, e, :], ACT.Silu).then_inc(sg_rdy, 1)
            high(2, T_ML + 6, T_ML // 4 + 1)
            leave(0, T_ML + 4, (go[:, 0, :], ACT.Sigmoid))
            high(3, T_ML + 7, T_ML // 4 + 1)
            leave(1, T_ML + 5, (go[:, 1, :], ACT.Sigmoid))

            def choice_weights():
                act.wait_ge(sel_dve, 6)
                f(score, score, ACT.Exp, scale=SCALE)
                f(selfp[:, :, :], selfp[:, :, :], ACT.Exp, scale=SCALE).then_inc(sel_act, 1)

            def sums_leave(h, bank):
                act.wait_ge(ys_mm, h)
                f(yaS[:, :, bass.ds(2 * h - 2, 2)].rearrange("p c e -> p e c"),
                  ps[:, bank, 0:2 * PAIRS].rearrange("p (e c) -> p e c", e=2), ACT.Copy).then_inc(ys_ev, 1)

            def decays(h, first):
                act.wait_ge(mb_mm, h + 1)
                for k in range(TT):
                    last = f(wt[:, k, 0:T - k * P], ps[:, 7, k * P:T], ACT.Exp, bias=ec[:, k, bass.ds(h, 1)], scale=-1.0)
                last.then_inc(w_exp, 1)
                if first:
                    choice_weights()
                act.wait_ge(mlast_rdy, h + 1)
                f(wsc[:, :], dl[:, 0, :], ACT.Exp).then_inc(wsc_rdy, 1)

            def mlstm(h, first):
                n, quad = T_ML + 8 * h, T_ML // 4 + 2 * h
                if first:
                    decays(h, True)
                else:
                    high(2, n + 2, quad)
                    leave(0, n, (pre[:, 0, 3:3 + NT], ACT.Copy))
                    high(3, n + 3, quad)
                    leave(1, n + 1, (pre[:, 1, 3:3 + NT], ACT.Copy))
                    decays(h, False)
                    for e in range(2):
                        act.wait_ge(cv_rdy, 2 * h + e + 1)
                        f(qkc[:, e, :], cacc[:, e, :], ACT.Silu).then_inc(sg_rdy, 1)
                    high(0, n + 4, quad + 1)
                    leave(0, n + 2, (mvT[:, 0, :], ACT.Copy))
                    high(1, n + 5, quad + 1)
                    leave(1, n + 3, (mvT[:, 1, :], ACT.Copy))
                for u in range(2):
                    act.wait_ge(vt_mm, 2 * h + u + 1)
                    f(v1[:, :, u * P:(u + 1) * P], ps[:, 7, :].rearrange("p (j n) -> p j n", j=TT), ACT.Copy)\
                        .then_inc(vt_ev, 1)
                    if first:
                        if u == 1:
                            high(0, n + 8, quad + 2)
                            leave(0, n + 6, (gz[:, 0, :], ACT.Silu))
                    else:
                        high(2 + u, n + 6 + u, quad + 1)
                        leave(u, n + 4 + u, (go[:, u, :], ACT.Sigmoid))
                if not first:
                    sums_leave(h, 7)
                act.wait_ge(pv_mm, h + 1)
                for q, b in ((0, 4), (1, 5), (2, 7), (3, 6)):
                    f(sqh[:, q, :], ps[:, b, 0:MV], ACT.Square, accum_out=ssm[:, q:q + 1])
                    f(hn[:, q, :], ps[:, b, 0:MV + 1], ACT.Copy).then_inc(hn_ev, 1)
                act.wait_ge(rs1_rdy, h + 1)
                f(dl[:, 1, :], dl[:, 3, :], ACT.Sqrt).then_inc(rs2_rdy, 1)
                if not first:
                    high(0, n + 8, quad + 2)
                    leave(0, n + 6, (gz[:, 0, :], ACT.Silu))
                high(1, n + 9, quad + 2)
                leave(1, n + 7, (gz[:, 1, :], ACT.Silu))
                act.wait_ge(cc_mm, h + 1)
                act.wait_ge(st_c, 32 * h + 32)
                f(cout[:, 0:2 * P], ps[:, 7, 0:2 * P], ACT.Copy)
                f(cout[0:1, 2 * P:3 * P], ps[0:1, 7, 2 * P:3 * P], ACT.Copy).then_inc(c_ev, 1)
                act.wait_ge(c_ev, h + 2)
                act.dma_start(O["C_p"][0, 0].rearrange("h (u v) d -> v (h u) d", v=P)[:, bass.ds(2 * h, 2), :],
                              cout[:, 0:2 * P].rearrange("p (u d) -> p u d", u=2)).then_inc(st_c, 16)
                act.dma_start(O["n_p"][0, 0][bass.ds(h, 1), :], cout[0:1, 2 * P:3 * P]).then_inc(st_c, 16)

            mlstm(0, True)
            with act.Fori(0, MH - 1) as h:
                mlstm(h + 1, False)
            act.dma_start(O["conv_s"][0, :, 0:2, :], I["state_conv"][0, :, 1:3, :]).then_inc(st_misc, 16)

            def gate_leave(j, t):
                leave(j, T_GATE + 4 * t + j, ((sga, sgm)[j % 2][:, bass.ds(2 * t + j // 2, 1), :]
                                              .rearrange("p o n -> p (o n)"), ACT.Sigmoid))

            act.wait_ge(ym_done, 1 + MH)
            act.wait_ge(st_c, 32 * MH + 32)
            high(2, T_GATE + 2, T_GATE // 4)
            gate_leave(0, 0)
            high(3, T_GATE + 3, T_GATE // 4)
            gate_leave(1, 0)
            act.wait_ge(sam_dve, 2)
            f(cvS[:, :, :], cvS[:, :, :], ACT.Silu).then_inc(sam_act, 1)
            act.wait_ge(sam_pe, 2)
            f(preN.rearrange("p (a n) -> p a n", a=2), ps[0:11, 4:6, :], ACT.Copy).then_inc(sam_act, 1)
            act.wait_ge(sam_act, 2)
            act.dma_start(O["conv_p"][0, 0], preN[0:3, :]).then_inc(st_pre, 16)
            act.dma_start(O["conv_s"][0, :, 2, :], preN[3:11, :]).then_inc(st_pre, 16)
            act.wait_ge(sam_pe, 3)
            act.wait_ge(st_misc, 16 * 5)
            act.wait_ge(vsum_rdy, MH)
            f(kqr[:, 0:2 * AW].rearrange("p (a n) -> p a n", a=2), ps[0:B, 4:6, :], ACT.Copy)
            f(kqN[:, :].rearrange("p (a n) -> p a n", a=2), ps[0:B, 4:6, :], ACT.Copy).then_inc(sam_act, 1)
            high(0, T_GATE + 4, T_GATE // 4 + 1)
            gate_leave(2, 0)
            sums_leave(MH, 6)
            high(1, T_GATE + 5, T_GATE // 4 + 1)
            gate_leave(3, 0)
            act.wait_ge(sam_dve, 4)
            act.dma_start(O["n_s"][0], nN).then_inc(st_misc, 16)
            act.wait_ge(ya_rdy, 1)
            f(yaH[:, :, :], yaT, ACT.Copy).then_inc(ya_hi, 1)

            def states_out(e, t):
                act.wait_ge(cnew_rdy, 2 * t + e + 1)
                act.dma_start(new_c[:, bass.ds(2 * t + e, 1)].rearrange("v o u d -> v (o u) d"),
                              cW[e].rearrange("p (u d) -> p u d", u=KT)).then_inc(st_C[e], 16)

            with act.Fori(0, 3) as i:
                n, quad = T_GATE + 4 * i + 4, T_GATE // 4 + i + 1
                for j in range(4):
                    high((j + 2) % 4, n + j + 2, quad + (j + 2) // 4)
                    gate_leave(j, i + 1)
                    if j % 2 == 1:
                        states_out(j // 2, i)
            for j in range(8):
                if j == 2:
                    act.wait_ge(z_done, 2 + T_WA)
                    f(hH[:, :, 0:T], ymT[:, :, 0:T], ACT.Copy).then_inc(ym_hi, 1)
                if j in (1, 3):
                    states_out(j // 2, 3)
                if j == 5:
                    act.wait_ge(fin_dve, 2)
                    f(rmsS[:, :, :], rmsS[:, :, :], ACT.Sqrt).then_inc(fin_act, 1)
                if j == 6:
                    act.wait_ge(fin_dve, 3)
                    f(hH[:, :, T:NT], ymT[:, :, T:NT], ACT.Copy).then_inc(ym_hi, 1)
                high(j + 2, T_WA + j + 2, (T_WA + j + 2) // 4, PAIRS if j < 6 else KT)
            with act.Fori(0, 2) as t:
                n, quad = T_WM + 4 * t, T_WM // 4 + t
                for j in range(4):
                    high((j + 2) % 4, n + j + 2, quad + (j + 2) // 4)
                    act.wait_ge(uu_rdy, 4 * t + j + 1)
                    act.wait_ge(ym_lo, 3)
                    c = bass.ds(4 * t + j, 1)
                    f(uH[:, c, :], sgm[:, c, :], ACT.Copy).then_inc(u_hi, 1)
            act.wait_ge(uu_rdy, KT)

            def squares(j):
                act.wait_ge(y_acc, 2 + j + 1)
                col = slice(j * P, (j + 1) * P)
                for i in range(TT):
                    chain(f(osq[:, 0:P], xN[:, i, col], ACT.Square, accum_out=ssq[:, j, i:i + 1]))
                chain(f(osq[0:B, 0:P], xs2[:, col], ACT.Square, accum_out=ssq[0:B, j, 4:5]))
                act.sem_inc(y_sq, 1)

            for j in range(8):
                n = T_OUT + j
                if j < 6:
                    high(j + 2, n + 2, (n + 2) // 4)
                if j >= 2:
                    act.wait_ge(ot_mm, j - 1)
                else:
                    act.wait_ge(u_lo, 2 + KT)
                act.wait_ge(z_done, n + 3)
                f(halves(oT[:, j % 2, :]), zps(j % 2), ACT.Copy, scale=modT[:, 16 + j, B:B + 1])
                f(oS[:, j % 2, :], ps[:, 2 * (j % 2) + 1, HALF - B:HALF], ACT.Copy).then_inc(ot_act, 1)
                act.wait_ge(ot_act, j + 1)
                act.sem_inc(z_free, 1)
                if j >= 1:
                    squares(j - 1)
            squares(KT - 1)
            act.wait_ge(y_var, 1)
            f(rstd[:, :], ss[:, :], ACT.Sqrt).then_inc(y_std, 1)
            act.wait_ge(y_gain, KT + 1)
            for i, j in enumerate((1, 3)):
                f(yN[:, j, :], yN[:, j, :], ACT.Copy, scale=ss[:, j:j + 1]).then_inc(y_act, 1)
                act.wait_ge(y_act, i + 1)
                act.dma_start(y_rows[:, j, :], yN[:, j, :]).then_inc(st_y2, 16)
            act.wait_ge(st_y2, 32)
            act.wait_ge(st_misc, 16 * 6)
            act.wait_ge(st_pre, 32)
            for e in range(2):
                act.wait_ge(st_C[e], 16 + 16 * B // 2)

        @block.gpsimd
        def _(pool):
            chain = Chain(pool, pool_chain)
            tt = nc.gpsimd.tensor_tensor

            def fill(ap, value, pattern, mult, op, other, base=0):
                chain(nc.gpsimd.memset(ap, value))
                return nc.gpsimd.affine_select(out=ap, in_=ap, compare_op=op, fill=other, base=base, pattern=pattern,
                                               channel_multiplier=mult)

            def low(j, n, ks=KT):
                pool.wait_ge(hi_done, n + 1)
                tt(wL[:, j % 2, 0:ks], wraw[:, j % 4, 0:ks], wH[:, j % 2, 0:ks].bitcast(F32), ALU.subtract)\
                    .then_inc(lo_done, 1)

            pool.sem_inc(lo_done, 4)
            for slot in range(KV_SLOTS):
                pool.sem_inc(page_free[slot], 1)
            pool.sem_inc(u_lo, 2)
            fill(ident[:, :], 0.0, [[-1, P]], 1, ALU.not_equal, 1.0).then_inc(id_rdy, 1)
            nc.gpsimd.memset(ones[:, :], 1.0)
            chain(fill(cmask[:, :], 0.0, [[-1, P]], 1, ALU.is_ge, NEG))
            chain(fill(upper[:, :], 1.0, [[1, P]], -1, ALU.is_ge, 0.0))
            chain(fill(rowsel[:, :, :], 0.0, [[-1, B + 2], [0, P]], 1, ALU.not_equal, 1.0))
            chain(fill(colsel[:, :, :], 0.0, [[1, B], [-1, B]], 0, ALU.not_equal, 1.0))
            chain(fill(earlier[:, :, :], 1.0, [[1, NBLK], [-1, NBLK]], 0, ALU.is_gt, 0.0))
            chain(nc.gpsimd.memset(headsel[:, :, :], 0.0))
            nc.gpsimd.memset(headsel[0:DH, 0, :], 1.0)
            chain(nc.gpsimd.memset(headsel[DH:P, 1, :], 1.0))
            chain(nc.gpsimd.memset(G[:, :, :], 0.0))
            chain(fill(pairsum[:, :], 0.0, [[-1, 2 * MH]], 1, ALU.not_equal, 1.0))
            nc.gpsimd.affine_select(out=pairsum[:, :], in_=pairsum[:, :], compare_op=ALU.not_equal, fill=1.0,
                                    base=-2 * MH, pattern=[[-1, 2 * MH]], channel_multiplier=1).then_inc(consts, 1)
            pool.wait_ge(if_hi, 1)
            tt(wif2[:, :, 2 * MH:4 * MH], wif[:, :, :], wif2[:, :, 0:2 * MH].bitcast(F32), ALU.subtract).then_inc(if_lo, 1)
            for i, j in enumerate((0, 1, None, 2, 3)):
                pool.wait_ge(h_hi, i + 1)
                if j is None:
                    tt(hL[:, :, T:NT], hS[:, :, :], hH[:, :, T:NT].bitcast(F32), ALU.subtract).then_inc(h_lo, 1)
                else:
                    tok = slice(j * P, (j + 1) * P)
                    tt(hL[:, :, tok], htmp[:, j % 2], hH[:, :, tok].bitcast(F32), ALU.subtract).then_inc(h_lo, 1)
            for n in range(2):
                low(n, n)
            pool.wait_ge(q_ev, 1)
            tt(qsr[:, AW:2 * AW], qsN[:, :], qsr[:, 0:AW].bitcast(F32), ALU.subtract).then_inc(q_lo, 1)

            def key_step(s, t):
                pool.wait_ge(ld_page[s % 4], 64 * (2 * t + s // 4 + 1))
                pool.wait_ge(qbc_rdy, 2 * t + s // 4 + 1)
                four = page[:, s % 4, :].rearrange("p (g n) -> p g n", g=STEP_PAGES)
                tt(four, four, qbc[:, s // 4:s // 4 + 1, :].broadcast_to([P, STEP_PAGES, AW]), ALU.mult)\
                    .then_inc(pool_mult, 1)

            def attention(t, before):
                n = T_ATT + 4 * t
                if before:
                    key_step(3, t - 1)
                low(2, n + 2)
                if before:
                    key_step(5, t - 1)
                low(3, n + 3)
                if before:
                    key_step(7, t - 1)
                low(0, n + 4)
                low(1, n + 5)

            attention(0, False)
            with pool.Fori(0, PAIRS - 1) as t:
                attention(t + 1, True)

            def causal_weights(h):
                diag = wt[:, :, 0:P]
                nc.gpsimd.affine_select(out=diag, in_=diag, compare_op=ALU.is_ge, fill=0.0, base=0,
                                        pattern=[[0, TT], [1, P]], channel_multiplier=-1).then_inc(w_rdy, 1)

            def value_step(s, h):
                pool.wait_ge(ld_page[s % 4], 64 * (8 + 2 * h + s // 4 + 1))
                heads = page[:, s % 4, :].rearrange("p (g n) -> p g n", n=DH)
                tt(heads, heads, score[:, bass.ds((8 * h + s) * 32, 32)].unsqueeze(2).broadcast_to([P, 32, DH]),
                   ALU.mult).then_inc(pool_mult, 1)

            key_step(3, PAIRS - 1)
            low(2, T_ML + 2)
            key_step(5, PAIRS - 1)
            low(3, T_ML + 3)
            key_step(7, PAIRS - 1)
            pool.wait_ge(ya_done, 1 + PAIRS)
            nc.gpsimd.memset(v1[:, :, MV:MV + 1], 1.0).then_inc(v_one, 1)
            nc.gpsimd.memset(pre[:, :, 0:3], 0.0).then_inc(v_one, 1)
            for j in range(3):
                low(j, T_ML + 4 + j)
            pool.wait_ge(w_exp, 1)
            low(3, T_ML + 7)
            causal_weights(0)
            low(0, T_ML + 8)
            pool.wait_ge(sel_dve, 8)
            value_step(1, 0)
            value_step(3, 0)
            low(1, T_ML + 9)
            value_step(5, 0)
            with pool.Fori(0, MH - 1) as i:
                h = i + 1
                n = T_ML + 8 * h
                low(2, n + 2)
                low(3, n + 3)
                value_step(7, h - 1)
                pool.wait_ge(w_exp, h + 1)
                low(0, n + 4)
                causal_weights(h)
                low(1, n + 5)
                value_step(1, h)
                low(2, n + 6)
                value_step(3, h)
                for j in range(3):
                    low((3 + j) % 4, n + 7 + j)
                value_step(5, h)
            low(2, T_GATE + 2)
            value_step(7, MH - 1)
            for j in range(1, 4):
                low((j + 2) % 4, T_GATE + j + 2)
            pool.wait_ge(ya_hi, 1)
            tt(yaL[:, :, :], yaT, yaH[:, :, :].bitcast(F32), ALU.subtract).then_inc(ya_lo, 1)
            pool.wait_ge(abc_rdy, 1)

            def decayed_state(e, t):
                pool.wait_ge(ld_C[e], 16 * t + 16)
                pool.wait_ge(st_C[e], 16 * t + 16)
                pool.wait_ge(c_used, 2 * t + e + 1)
                tt(cW[e].rearrange("p (h n) -> p h n", h=MH), cS[:, e].rearrange("p (h n) -> p h n", h=MH),
                   abc[:, bass.ds(2 * t + e, 1), 0:MH].rearrange("p o h -> p (o h)").unsqueeze(2)
                   .broadcast_to([P, MH, 2 * MQ]), ALU.mult).then_inc(cw_rdy, 1)

            decayed_state(0, 0)
            with pool.Fori(0, 3) as t:
                n = T_GATE + 4 * t + 4
                low(2, n + 2)
                decayed_state(1, t)
                low(3, n + 3)
                low(4, n + 4)
                decayed_state(0, t + 1)
                low(5, n + 5)
            decayed_state(1, 3)
            for j in range(8):
                low(j + 2, T_WA + j + 2, PAIRS if j < 6 else KT)
                if j in (3, 4):
                    pool.wait_ge(ym_hi, 1)
                    quarter = slice(2 * j - 6, 2 * j - 4)
                    last = tt(hL[:, quarter, 0:T], ymT[:, quarter, 0:T], hH[:, quarter, 0:T].bitcast(F32), ALU.subtract)
                    if j == 4:
                        last.then_inc(ym_lo, 1)
            def gained(j):
                pool.wait_ge(y_acc, 2 + j + 1)
                col = slice(j * P, (j + 1) * P)
                tt(ysN[:, col], xs2[:, col], fg[0:B, col], ALU.mult)
                tt(yN[:, :, col], xN[:, :, col], fg[:, col].unsqueeze(1).broadcast_to([P, TT, P]), ALU.mult)\
                    .then_inc(y_gain, 1)

            with pool.Fori(0, 2) as t:
                n = T_WM + 4 * t
                for j in range(4):
                    low((j + 2) % 4, n + j + 2)
                    pool.wait_ge(u_hi, 4 * t + j + 1)
                    c = bass.ds(4 * t + j, 1)
                    tt(uL[:, c, :], sgm[:, c, :], uH[:, c, :].bitcast(F32), ALU.subtract).then_inc(u_lo, 1)
            pool.wait_ge(ld_xo, 48)
            for j in range(8):
                if j < 6:
                    low(j + 2, T_OUT + j + 2)
                if j >= 1:
                    gained(j - 1)
            gained(KT - 1)

        @block.vector
        def _(dve):
            chain = Chain(dve, dve_chain)
            v = nc.vector
            tt = v.tensor_tensor

            def over(ap, n):
                return ap.unsqueeze(len(ap.shape)).broadcast_to(list(ap.shape) + [n])

            dve.sem_inc(ya_done, 1)
            dve.sem_inc(ym_done, 1)
            dve.sem_inc(c_used, 2)
            dve.sem_inc(kq_used, 2)
            dve.sem_inc(y_acc, 2)
            v.memset(ss[:, :], 1.0).then_inc(ss_set, 1)
            dve.wait_ge(t_c, 1)
            v.tensor_copy(cT.rearrange("p k n -> p (k n)"), ps[:, 4, 0:9 * KT]).then_inc(c_T, 1)
            dve.wait_ge(t_vec, 1)
            v.tensor_copy(vcol[:, :], ps[:, 5, 0:V_ROWS]).then_inc(v_col, 1)
            dve.wait_ge(x_sq, 1)
            v.tensor_scalar(rstd[:, :], ss[:, :], 1.0 / D, EPS, ALU.mult, ALU.add).then_inc(x_var, 1)
            dve.wait_ge(x_std, 1)
            chain(v.reciprocal(rstd[:, :], ss[:, :]))
            for j in range(TT):
                v.tensor_scalar(xt[:, j, :], xt[:, j, :], rstd[:, j:j + 1], None, ALU.mult)
            v.tensor_scalar(xsN, xsN, rstd[0:B, 4:5], None, ALU.mult).then_inc(x_nrm, 1)
            dve.wait_ge(t_mod, 1)
            chain(tt(modT[:, 0:16, :], ps[:, 5, 0:144].rearrange("p (k n) -> p k n", n=9),
                     over(vcol[:, V_BA:V_BA + 16], 9), ALU.add))
            v.scalar_tensor_tensor(hscale[:, :, :], modT[:, 8:16, :], 1.0, over(vcol[:, V_G:V_G + KT], 9),
                                   ALU.add, ALU.mult).then_inc(mod_rdy, 1)

            def tokens(j, count):
                b = 2 if j % 2 == 0 else 6
                dve.wait_ge(t_x, count)
                if j >= 2:
                    dve.wait_ge(h_lo, j - 1)
                chain(tt(htmp[:, j % 2], ps[:, b:b + 2, :].rearrange("p a (k n) -> p (a k) n", n=P),
                         over(hscale[:, :, B], P), ALU.mult))
                tt(htmp[:, j % 2], htmp[:, j % 2], over(modT[:, 0:KT, B], P), ALU.add).then_inc(h_rdy, 1)

            dve.wait_ge(mod_rdy, 1)
            tokens(0, 1)
            tokens(1, 2)
            dve.wait_ge(t_x, 3)
            chain(tt(hS[:, :, :], ps[:, 4, 0:B * KT].rearrange("p (k n) -> p k n", n=B), hscale[:, :, 0:B], ALU.mult))
            tt(hS[:, :, :], hS[:, :, :], modT[:, 0:KT, 0:B], ALU.add).then_inc(h_rdy, 1)
            tokens(2, 4)
            tokens(3, 5)
            dve.wait_ge(t_mod, 2)
            tt(modT[:, 16:24, :], ps[:, 5, 0:72].rearrange("p (k n) -> p k n", n=9),
               over(vcol[:, V_BA + 16:V_BA + 24], 9), ALU.add).then_inc(mod_rdy, 1)

            def gates_in():
                dve.wait_ge(g_mm, 1)
                dve.wait_ge(ld_small, 64)
                tt(G[:, 0:TT, :], ps[:, 6, 0:32].rearrange("p (j n) -> p j n", n=8),
                   bif[:, :].unsqueeze(1).broadcast_to([P, TT, 8]), ALU.add)
                tt(G[0:B, TT, :], ps[0:B, 6, 32:40], bif[0:B, :], ALU.add).then_inc(g_dve, 1)
                dve.wait_ge(g_dve, 1)
                fg_ = G[:, :, MH:2 * MH]
                chain(v.tensor_scalar(gf[:, :, :], fg_, -1.0, None, ALU.mult))
                tt(gf[:, :, :], gf[:, :, :], fg_, ALU.min).then_inc(g_dve, 1)
                dve.wait_ge(g_act, 1)
                v.scalar_tensor_tensor(lf[:, :, :], fg_, 0.0, gf[:, :, :], ALU.min, ALU.subtract).then_inc(g_dve, 1)
                dve.wait_ge(g_dve, 3)

            def gate_sums():
                dve.wait_ge(g_pe, 1)
                chain(v.tensor_copy(bc[:, :, :].rearrange("p j h -> p (j h)"), ps[:, 7, 0:16]))
                tt(ec[:, :, :], G[:, 0:TT, 0:MH], bc[:, :, :], ALU.subtract).then_inc(g_dve, 1)

            def gate_max():
                dve.wait_ge(g_pe, 2)
                chain(v.tensor_copy(eR, ps[0:MH, 7, :]))
                v.tensor_tensor_scan(MR[:, :], eR, eR, 0.0, ALU.max, ALU.max).then_inc(g_dve, 1)

            def gate_stabilisers():
                dve.wait_ge(g_pe, 3)
                tt(mt[:, :, :].rearrange("p j h -> p (j h)"), ps[:, 7, 0:16], bc[:, :, :].rearrange("p j h -> p (j h)"),
                   ALU.add).then_inc(g_dve, 1)
                chain(tt(gs[:, 0, :], lf[0:B, TT, :], m0[:, :], ALU.add))
                chain(tt(gs[:, 1, :], gs[:, 0, :], G[0:B, TT, 0:MH], ALU.max))
                tt(aw[:, 0, :], gs[:, 0, :], gs[:, 1, :], ALU.subtract)
                tt(aw[:, 1, :], G[0:B, TT, 0:MH], gs[:, 1, :], ALU.subtract).then_inc(g_dve, 1)

            def causal_max(e, t):
                dve.wait_ge(qk_done, 2 * t + e + 1)
                for q, b, c in ((3, 4, 0), (2, 5, 0), (0, 5, 384), (1, 6, 0)):
                    own = ps[:, b, c + q * P:c + (q + 1) * P]
                    last = tt(own, own, cmask[:, :], ALU.add)
                chain(last)
                for q, b, c in ((3, 4, 0), (2, 5, 0), (0, 5, 384), (1, 6, 0)):
                    last = v.tensor_reduce(mx[:, e, q:q + 1], ps[:, b, c:c + (q + 1) * P], AX, ALU.max)
                chain(last)
                v.tensor_scalar(nmx[:, e, :], mx[:, e, :], -SCALE, None, ALU.mult).then_inc(smx, 1)

            def normalise(e, t):
                dve.wait_ge(sexp, 2 * t + e + 1)
                chain(v.reciprocal(rinv[:, e, :], rsum[:, e, :]))
                for q in range(TT):
                    last = v.tensor_scalar(prA[:, e, q, 0:(q + 1) * P], prA[:, e, q, 0:(q + 1) * P],
                                           rinv[:, e, q:q + 1], None, ALU.mult)
                last.then_inc(pnorm, 1)

            def key_products(s, t):
                if s in (3, 5, 7):
                    dve.wait_ge(pool_mult, 3 * t + (s - 3) // 2 + 1)
                else:
                    dve.wait_ge(ld_page[s % 4], 64 * (2 * t + s // 4 + 1))
                    dve.wait_ge(qbc_rdy, 2 * t + s // 4 + 1)
                    four = page[:, s % 4, :].rearrange("p (g n) -> p g n", g=STEP_PAGES)
                    chain(tt(four, four, qbc[:, s // 4:s // 4 + 1, :].broadcast_to([P, STEP_PAGES, AW]), ALU.mult))

            def key_sums(s, t):
                v.tensor_reduce(score[:, bass.ds((8 * t + s) * 32, 32)],
                                page[:, s % 4, :].rearrange("p (g n) -> p g n", n=DH), AX, ALU.add)\
                    .then_inc(page_free[s % 4], 1)

            def key_step(s, t):
                key_products(s, t)
                key_sums(s, t)

            def next_selector(e, t):
                dve.wait_ge(qbc_mm, 2 * t + e + 1)
                v.tensor_copy(selc[:, e, :], rowsel[:, bass.ds(2 * t + e + 2, 1), :].rearrange("p o n -> p (o n)"))\
                    .then_inc(selc_rdy, 1)

            def finish(t):
                normalise(1, t)
                key_sums(1, t)
                for s in (2, 3, 4):
                    key_step(s, t)
                dve.wait_ge(z_free, T_ATT + 4 * t + 6)
                dve.wait_ge(pv_done, t + 1)
                ya = yaT[:, bass.ds(t, 1), 0:T].rearrange("p o n -> p (o n)")
                tt(ya, ya, ps[:, 7, :], ALU.mult).then_inc(ya_done, 1)

            def attention(t, before):
                n = T_ATT + 4 * t
                if before:
                    finish(t - 1)
                else:
                    gates_in()
                    gate_sums()
                next_selector(0, t)
                causal_max(0, t)
                if not before:
                    gate_max()
                if before:
                    key_step(6, t - 1)
                normalise(0, t)
                if before:
                    key_step(5, t - 1)
                    key_step(7, t - 1)
                if not before:
                    gate_stabilisers()
                key_step(0, t)
                for i, src, at in ((0, qT, 3), (1, kT, 4), (2, vT, 5)):
                    dve.wait_ge(z_free, n + at)
                    v.tensor_copy(qkvS[:, i, bass.ds(t, 1), :].rearrange("p o n -> p (o n)"), src[:, T:NT])
                causal_max(1, t)
                next_selector(1, t)
                key_products(1, t)

            for e in range(2):
                v.tensor_copy(selc[:, e, :], rowsel[:, e, :]).then_inc(selc_rdy, 1)
            attention(0, False)
            with dve.Fori(0, PAIRS - 1) as t:
                chain.loop(t, 2 * 1 + 2 * 2 + 5 * 1)
                attention(t + 1, True)
            chain.end(PAIRS - 1)
            finish(PAIRS - 1)

            def convolve(e, h):
                dve.wait_ge(z_free, T_ML + 8 * h + 3 + e)
                acc = cacc[:, e, :]

                def tap(j):
                    return vcol[:, bass.ds(h + (V_WC + KT * j + MH * e), 1)]

                chain(v.tensor_scalar(acc, pre[:, e, 0:T], tap(0), vcol[:, bass.ds(h + (V_BC + MH * e), 1)],
                                      ALU.mult, ALU.add))
                for j in range(1, 4):
                    last = v.scalar_tensor_tensor(acc, pre[:, e, j:j + T], tap(j), acc, ALU.mult, ALU.add)
                    if j < 3:
                        chain(last)
                last.then_inc(cv_rdy, 1)
                v.tensor_copy(preS[:, bass.ds(h + MH * e, 1), :].rearrange("p o n -> p (o n)"), pre[:, e, T:T + 11])

            dve.wait_ge(ya_done, 1 + PAIRS)
            v.tensor_copy(selm, rowsel[0:MH, 0, :]).then_inc(selm_rdy, 1)
            tt(tS[:, :, :], qkvS[:, 0], qkvS[:, 1], ALU.mult).then_inc(sel_dve, 1)
            for s in (5, 6, 7):
                key_step(s, PAIRS - 1)
            for slot in range(KV_SLOTS):
                dve.wait_ge(page_free[slot], 1 + 2 * PAIRS)
            dve.wait_ge(sel_dve, 1)
            dve.sem_inc(sel_dve, 1)
            dve.wait_ge(st_k, 16 * (1 + PAIRS))
            dve.wait_ge(st_v, 16 * (1 + PAIRS))
            dve.wait_ge(v_one, 2)
            convolve(0, 0)
            dve.wait_ge(sel_pe, 1)
            chain(v.tensor_copy(selfp[:, :, :].rearrange("p b (t e) -> p e t b", e=2),
                                ps[:, 4, 0:64].rearrange("p (e t b) -> p e t b", e=2, t=PAIRS)))
            dve.wait_ge(sel_pe, 3)
            chain(v.tensor_reduce(bsum[:, :, :], ps[0:B, 7, 0:P].rearrange("p (n w h) -> p h n w", n=NBLK, w=2),
                                  AX, ALU.add))
            sm = bsum[:, :, :].unsqueeze(2).broadcast_to([B, AH, NBLK, NBLK])
            sn = bsum[:, :, :].unsqueeze(3).broadcast_to([B, AH, NBLK, NBLK])
            tt(cmpA, sm, sn, ALU.is_gt)
            chain(tt(cmpB, sm, sn, ALU.is_equal))
            chain(tt(cmpB, cmpB, earlier[:, :, :].unsqueeze(1).broadcast_to([B, AH, NBLK, NBLK]), ALU.mult))
            chain(tt(cmpA, cmpA, cmpB, ALU.add))
            chain(v.tensor_reduce(pen[:, :].rearrange("p (h n) -> p h n", n=NBLK), cmpA, AX, ALU.add))
            chain(v.tensor_scalar(pen[:, :], pen[:, :], float(TOPK), NEG, ALU.is_ge, ALU.mult))
            tt(pend, pen[:, :].unsqueeze(1).broadcast_to([B, B, AH * NBLK]), over(ident[0:B, 0:B], AH * NBLK),
               ALU.mult).then_inc(sel_dve, 1)
            convolve(1, 0)
            dve.wait_ge(sel_pe, 4)
            sc = score.rearrange("p (b n w h) -> p b n w h", b=B, n=NBLK, w=2)
            for w in range(2):
                last = tt(sc[:, :, :, w, :], sc[:, :, :, w, :],
                          ps[:, 7, :].rearrange("p (b h n) -> p b n h", b=B, h=AH), ALU.add)
            chain(last)
            by_bh = score.rearrange("p (b g h) -> p b h g", b=B, g=PAGES)
            mx3 = mxA[:, :].rearrange("p (b h) -> p b h", b=B)
            v.tensor_reduce(mx3, by_bh, AX, ALU.max).then_inc(sel_dve, 1)
            dve.wait_ge(sg_rdy, 2)
            v.tensor_scalar(qkc[:, 1, :], qkc[:, 1, :], KSCALE, None, ALU.mult).then_inc(qk_rdy, 1)
            dve.wait_ge(sel_pe, 5)
            chain(v.tensor_reduce(mx64[:, :], ps[0:B * AH, 7, 0:P], AX, ALU.max))
            v.tensor_scalar(dg64[:, :], ident[0:B * AH, 0:B * AH], mx64[:, 0:1], None, ALU.mult).then_inc(sel_dve, 1)
            dve.wait_ge(sel_pe, 6)
            chain(tt(mx3, ps[:, 7, 128:192].rearrange("p (b h) -> p b h", b=B), selfp[:, :, :], ALU.max))
            dve.sem_inc(mx_read, 1)
            tt(by_bh, by_bh, over(mx3, PAGES), ALU.subtract)
            tt(selfp[:, :, :], selfp[:, :, :], mx3, ALU.subtract).then_inc(sel_dve, 1)
            def choice_sums():
                dve.wait_ge(sel_act, 2)
                v.tensor_reduce(mx3, by_bh, AX, ALU.add).then_inc(sel_dve, 1)

            def choice_normalise():
                dve.wait_ge(sel_pe, 7)
                chain(tt(mx3, ps[:, 7, 256:320].rearrange("p (b h) -> p b h", b=B), selfp[:, :, :], ALU.add))
                dve.sem_inc(mx_read, 1)
                chain(v.reciprocal(mx3, mx3))
                tt(by_bh, by_bh, over(mx3, PAGES), ALU.mult)
                tt(selfp[:, :, :], selfp[:, :, :], mx3, ALU.mult).then_inc(sel_dve, 1)
                dve.wait_ge(sel_dve, 8)

            def value_step(s, h, first):
                prod = page[:, s % 4, :]
                if s % 2 == 0:
                    dve.wait_ge(ld_page[s % 4], 64 * (8 + 2 * h + s // 4 + 1))
                    heads = prod.rearrange("p (g n) -> p g n", n=DH)
                    chain(tt(heads, heads, over(score[:, bass.ds((8 * h + s) * 32, 32)], DH), ALU.mult))
                else:
                    dve.wait_ge(pool_mult, 3 * PAIRS + 4 * h + s // 2 + 1)
                chain(tt(prod[:, 0:1024], prod[:, 0:1024], prod[:, 1024:2048], ALU.add))
                acc = vacc[:, s // 4, :]
                if s % 4 == 0:
                    if not first:
                        dve.wait_ge(ys_mm, h)
                    tt(acc, prod[:, 0:512], prod[:, 512:1024], ALU.add).then_inc(page_free[0], 1)
                    return
                chain(tt(prod[:, 0:512], prod[:, 0:512], prod[:, 512:1024], ALU.add))
                dve.wait_ge(page_free[s % 4 - 1], 8 + 2 * h + s // 4 + 2)
                tt(acc, acc, prod[:, 0:512], ALU.add).then_inc(page_free[s % 4], 1)
                if s == 7:
                    dve.wait_ge(page_free[3], 8 + 2 * h + 3)
                    dve.sem_inc(vsum_rdy, 1)

            def mlstm(h, first):
                n = T_ML + 8 * h
                if not first:
                    convolve(0, h)
                dve.wait_ge(mb_mm, h + 1)
                v.tensor_copy(selm, rowsel[0:MH, bass.ds(h + 1, 1), :].rearrange("p o n -> p (o n)"))\
                    .then_inc(selm_rdy, 1)
                dve.wait_ge(w_exp, h + 1)
                v.tensor_scalar(dl[:, 0, :], ec[:, :, bass.ds(h, 1)].rearrange("p j o -> p (j o)"),
                                ps[:, 7, T - 1:T], None, ALU.subtract).then_inc(mlast_rdy, 1)
                if not first:
                    convolve(1, h)
                if first:
                    choice_sums()
                else:
                    dve.wait_ge(sg_rdy, 2 * h + 2)
                    v.tensor_scalar(qkc[:, 1, :], qkc[:, 1, :], KSCALE, None, ALU.mult).then_inc(qk_rdy, 1)
                    value_step(6, h - 1, False)
                    value_step(7, h - 1, False)
                dve.wait_ge(st_mm, h + 1)
                dve.wait_ge(w_rdy, h + 1)
                for k, b, c in ((0, 4, 0), (1, 5, 0), (3, 5, 384), (2, 6, 0)):
                    last = tt(wt[:, k, 0:T - k * P], wt[:, k, 0:T - k * P], ps[:, b, c:c + T - k * P], ALU.mult)
                last.then_inc(mpt_rdy, 1)
                dve.wait_ge(z_free, n + 6)
                v.tensor_copy(vS[:, bass.ds(2 * h, 2), :], mvT[:, :, T:NT])
                if first:
                    choice_normalise()
                dve.wait_ge(kt_mm, h + 1)
                dve.wait_ge(wsc_rdy, h + 1)
                tt(kw, ps[:, 6, :].rearrange("p (j n) -> p j n", j=TT), over(wsc[:, :], P), ALU.mult)\
                    .then_inc(kw_rdy, 1)
                value_step(0, h, first)
                if not first:
                    value_step(1, h, first)
                dve.wait_ge(hn_ev, 4 * h + 5)
                den = hn[:, :, MV]
                chain(v.tensor_scalar(dl[:, 1, :], den, -1.0, None, ALU.mult))
                chain(tt(dl[:, 1, :], dl[:, 1, :], den, ALU.max))
                chain(tt(dl[:, 1, :], dl[:, 1, :], em[:, :, bass.ds(h, 1)].rearrange("p j o -> p (j o)"), ALU.max))
                chain(v.reciprocal(dl[:, 2, :], dl[:, 1, :]))
                chain(tt(dl[:, 3, :], dl[:, 2, :], dl[:, 2, :], ALU.mult))
                chain(tt(dl[:, 3, :], dl[:, 3, :], ssm[:, :], ALU.mult))
                v.tensor_scalar(dl[:, 3, :], dl[:, 3, :], 1.0 / MV, EPS, ALU.mult, ALU.add).then_inc(rs1_rdy, 1)
                dve.wait_ge(rs2_rdy, h + 1)
                chain(v.reciprocal(dl[:, 3, :], dl[:, 1, :]))
                chain(tt(dl[:, 3, :], dl[:, 3, :], dl[:, 2, :], ALU.mult))
                tt(hn[:, :, 0:MV], hn[:, :, 0:MV], over(dl[:, 3, :], MV), ALU.mult).then_inc(hn_rdy, 1)
                if first:
                    value_step(1, h, first)
                value_step(2, h, first)
                value_step(3, h, first)
                for u in range(2):
                    dve.wait_ge(z_free, n + 9 + u)
                    chain(v.scalar_tensor_tensor(go[:, u, :], go[:, u, :], vcol[:, bass.ds(2 * h + (V_MG + u), 1)],
                                                 gz[:, u, :], ALU.mult, ALU.mult))
                v.tensor_copy(ymT[:, bass.ds(2 * h, 2), T:NT], go[:, :, T:NT])
                dve.wait_ge(ht_mm, h + 1)
                tt(ymT[:, bass.ds(2 * h, 2), 0:T], ps[:, 4:6, :], go[:, :, 0:T], ALU.mult).then_inc(ym_done, 1)
                value_step(4, h, first)
                value_step(5, h, first)

            mlstm(0, True)
            with dve.Fori(0, MH - 1) as h:
                chain.loop(h, 2 * 3 + 4 * 1 + 8 * 1 + 6 * 1 + 6 + 2 + 2)
                mlstm(h + 1, False)
            chain.end(MH - 1)

            dve.wait_ge(ym_done, 1 + MH)
            awf = aw[:, :, :].rearrange("p a h -> p (a h)")
            dve.wait_ge(g_act, 3)
            tt(dgS[:, :, :], awf.unsqueeze(1).broadcast_to([B, B, 2 * MH]), over(ident[0:B, 0:B], 2 * MH), ALU.mult)\
                .then_inc(sam_dve, 1)
            st3 = stT[:, :, :].rearrange("p k (b j) -> p k b j", j=3)
            chain(tt(cvS[:, :, :], preS[:, :, 3:11], over(vcol[:, V_WC + 3 * KT:V_WC + 4 * KT], B), ALU.mult))
            for j in range(3):
                chain(tt(cvT[:, :, :], st3[:, :, :, j], over(vcol[:, V_WC + j * KT:V_WC + (j + 1) * KT], B), ALU.mult))
                chain(tt(cvS[:, :, :], cvS[:, :, :], cvT[:, :, :], ALU.add))
            tt(cvS[:, :, :], cvS[:, :, :], over(vcol[:, V_BC:V_BC + KT], B), ALU.add).then_inc(sam_dve, 1)
            value_step(6, MH - 1, False)
            dve.wait_ge(sam_act, 1)
            v.tensor_scalar(cvS[:, MH:KT, :], cvS[:, MH:KT, :], KSCALE, None, ALU.mult).then_inc(sam_dve, 1)
            dve.wait_ge(sam_pe, 1)
            v.tensor_copy(abc[:, :, :].rearrange("p b n -> p (b n)"), ps[:, 7, 0:64]).then_inc(abc_rdy, 1)
            dve.wait_ge(abc_rdy, 1)
            v4 = vS[:, :, :].rearrange("p (h u) b -> p h u b", u=2)
            chain(tt(v4, v4, abc[:, :, MH:2 * MH].rearrange("p b h -> p h b").unsqueeze(2).broadcast_to([P, MH, 2, B]),
                     ALU.mult))
            value_step(7, MH - 1, False)
            for e in range(2):
                v.tensor_copy(selg[:, e, :], rowsel[:, e, :]).then_inc(selg_rdy, 1)
            dve.wait_ge(sam_act, 3)
            tt(kqr[:, 2 * AW:4 * AW], kqN[:, :], kqr[:, 0:2 * AW].bitcast(F32), ALU.subtract).then_inc(kq_lo, 1)
            dve.wait_ge(ld_n, 16)
            kS = kqN[:, 0:AW].rearrange("p (h n) -> p h n", h=MH)
            qS = kqN[:, AW:2 * AW].rearrange("p (h n) -> p h n", h=MH)
            tt(nT, kS, over(aw[:, 1, :], MQ), ALU.mult)
            chain(tt(nN, nN, over(aw[:, 0, :], MQ), ALU.mult))
            chain(tt(nN, nN, nT, ALU.add))
            chain(tt(nT, nN, qS, ALU.mult))
            chain(v.tensor_reduce(dS[:, 0, :], nT, AX, ALU.add))
            chain(v.tensor_scalar(dS[:, 1, :], dS[:, 0, :], -1.0, None, ALU.mult))
            chain(tt(dS[:, 1, :], dS[:, 1, :], dS[:, 0, :], ALU.max))
            chain(tt(dS[:, 1, :], dS[:, 1, :], gs[:, 2, :], ALU.max))
            chain(v.reciprocal(dS[:, 2, :], dS[:, 1, :]))
            tt(dgS[:, :, 0:MH], dS[:, 2, :].unsqueeze(1).broadcast_to([B, B, MH]), over(ident[0:B, 0:B], MH), ALU.mult)\
                .then_inc(sam_dve, 1)
            dve.wait_ge(ys_ev, MH)
            sp_t = selfp[:, :, :].rearrange("p b (t e) -> p e t b", e=2)
            for e in range(2):
                r = slice(DH * e, DH * e + DH)
                last = tt(tS[r], qkvS[r, 2], sp_t[r, e], ALU.mult)
            chain(last)
            chain(tt(tS[:, :, :], tS[:, :, :], yaS[:, :, :], ALU.add))
            chain(tt(yaT[:, :, T:NT], yaT[:, :, T:NT], tS[:, :, :], ALU.mult))

            dve.sem_inc(ya_rdy, 1)

            def new_state(e, t, leaving=None):
                dve.wait_ge(kq_mm, 2 * t + e + 1)
                v.tensor_copy(selg[:, e, :], rowsel[:, bass.ds(2 * t + e + 2, 1), :]
                              .rearrange("p o n -> p (o n)")).then_inc(selg_rdy, 1)
                dve.wait_ge(cw_rdy, 2 * t + e + 1)
                four = cS[:, e].rearrange("p (h u n) -> p h u n", h=MH, u=2)
                key = ps[:, 4 + 2 * e, :].rearrange("p (h n) -> p h n", h=MH).unsqueeze(2)
                query = ps[:, 5 + 2 * e, :].rearrange("p (h n) -> p h n", h=MH).unsqueeze(2)
                val = vS[:, :, bass.ds(2 * t + e, 1)].rearrange("p (h u) o -> p h (u o)", u=2)
                chain(tt(four, key.broadcast_to([P, MH, 2, MQ]), over(val, MQ), ALU.mult))
                tt(cW[e], cW[e], cS[:, e], ALU.add).then_inc(cnew_rdy, 1)
                if leaving is not None:
                    attention_leaves(leaving)
                dve.wait_ge(cnew_rdy, 2 * t + e + 1)
                tt(four, cW[e].rearrange("p (h u n) -> p h u n", h=MH, u=2), query.broadcast_to([P, MH, 2, MQ]),
                   ALU.mult).then_inc(kq_used, 1)
                dve.wait_ge(kq_used, 2 * t + e + 3)
                v.tensor_reduce(Cq[:, :, bass.ds(2 * t + e, 1)].rearrange("p k o -> p (k o)"),
                                cS[:, e].rearrange("p (k n) -> p k n", k=KT), AX, ALU.add).then_inc(c_used, 1)

            def halved(ap, c):
                return ap[:, bass.ds(c, 1), :].rearrange("p o (a n) -> p (o a) n", a=2)

            def attention_leaves(c):
                dve.wait_ge(z_done, T_WA + c + 3)
                tt(halved(sga, c), zps(c % 2), halved(sga, c), ALU.mult).then_inc(z_free, 1)

            with dve.Fori(0, 3) as t:
                chain.loop(t, 2 * 1)
                new_state(0, t)
                new_state(1, t)
            chain.end(3)
            dve.wait_ge(sam_pe, 4)
            v.tensor_copy(rbc[:, :, :].rearrange("p b n -> p (b n)"), ps[:, 7, 64:96]).then_inc(sam_dve, 1)
            new_state(0, 3)
            dve.wait_ge(z_free, 2 + T_WA)
            attention_leaves(0)
            attention_leaves(1)
            new_state(1, 3, 2)
            attention_leaves(3)
            dve.wait_ge(c_used, 2 + B)
            C4 = Cq[:, :, :].rearrange("p (h u) b -> p h u b", u=2)
            chain(tt(C4, C4, rbc[:, :, :].rearrange("p b h -> p h b").unsqueeze(2).broadcast_to([P, MH, 2, B]), ALU.mult))
            tt(sqS[:, :, :], Cq[:, :, :], Cq[:, :, :], ALU.mult).then_inc(fin_dve, 1)
            attention_leaves(4)
            dve.wait_ge(fin_pe, 1)
            chain(v.tensor_reduce(rmsS[:, :, :], ps[:, 4, 0:64].rearrange("p (h u b) -> p h b u", u=2, b=B), AX, ALU.add))
            v.tensor_scalar(rmsS[:, :, :], rmsS[:, :, :], 1.0 / MV, EPS, ALU.mult, ALU.add).then_inc(fin_dve, 1)
            attention_leaves(5)
            dve.wait_ge(fin_act, 1)
            chain(v.reciprocal(rmsS[:, :, :], rmsS[:, :, :]))
            chain(tt(C4, C4, rmsS[:, :, :].unsqueeze(2).broadcast_to([P, MH, 2, B]), ALU.mult))
            tt(ymT[:, :, T:NT], ymT[:, :, T:NT], Cq[:, :, :], ALU.mult).then_inc(fin_dve, 1)
            dve.wait_ge(ym_hi, 1)
            tt(hL[:, 4:KT, 0:T], ymT[:, 4:KT, 0:T], hH[:, 4:KT, 0:T].bitcast(F32), ALU.subtract).then_inc(ym_lo, 1)
            attention_leaves(6)
            dve.wait_ge(ym_hi, 2)
            tt(hL[:, :, T:NT], ymT[:, :, T:NT], hH[:, :, T:NT].bitcast(F32), ALU.subtract).then_inc(ym_lo, 1)
            attention_leaves(7)

            with dve.Fori(0, 2) as t:
                for j in range(4):
                    c = 4 * t + j
                    dve.wait_ge(z_done, c + (T_WM + 3))
                    tt(halved(sgm, c), zps(j % 2), halved(sgm, c), ALU.mult).then_inc(z_free, 1)
                    dve.wait_ge(z_free, c + (T_WM + 3))
                    tt(sgm[:, bass.ds(c, 1), :], sgm[:, bass.ds(c, 1), :], sga[:, bass.ds(c, 1), :], ALU.add)\
                        .then_inc(uu_rdy, 1)

            def gated_sample(j):
                dve.wait_ge(ot_act, j + 1)
                tt(oT[:, j % 2, T:NT], oS[:, j % 2, :], modT[:, 16 + j, 0:B], ALU.mult).then_inc(ot_rdy, 1)

            chain(v.memset(ssq, 0.0))
            dve.wait_ge(ld_xo, 48)
            for j in range(8):
                gated_sample(j)
                s = j % 2
                col = slice(j * P, (j + 1) * P)
                dve.wait_ge(ot_mm, j + 1)
                tt(xN[:, :, col], xN[:, :, col], ps[:, 4 + 2 * s, :].rearrange("p (i n) -> p i n", i=TT), ALU.add)
                tt(xs2[:, col], xs2[:, col], ps[0:B, 5 + 2 * s, 0:P], ALU.add).then_inc(y_acc, 1)
            dve.wait_ge(y_sq, KT)
            chain(v.tensor_reduce(rstd[:, :], ssq.rearrange("p c j -> p j c"), AX, ALU.add))
            v.tensor_scalar(ss[:, :], rstd[:, :], 1.0 / D, EPS, ALU.mult, ALU.add).then_inc(y_var, 1)
            dve.wait_ge(y_std, 1)
            v.reciprocal(ss[:, :], rstd[:, :]).then_inc(y_gain, 1)
            dve.wait_ge(y_gain, KT + 1)
            for j in (0, 2):
                v.tensor_scalar(yN[:, j, :], yN[:, j, :], ss[:, j:j + 1], None, ALU.mult).then_inc(y_rdy, 1)
            v.tensor_scalar(ysN, ysN, ss[0:B, 4:5], None, ALU.mult).then_inc(y_rdy, 1)

_INS = ["x_prompt", "x_sample", "cache_k", "cache_v", "state_C", "state_n", "state_m", "state_conv",
        "page_table", "c_prompt", "c_sample", "w_ada", "b_ada", "norm_g", "w_in", "b_if", "w_conv",
        "b_conv", "m_norm_g", "w_att", "w_mlstm", "w_out", "final_g"]
_OUTS = [("y_p", (1, T, D)), ("y_s", (B, 1, D)),
         ("k_p", (1, 1, T, AH, DH)), ("v_p", (1, 1, T, AH, DH)),
         ("C_p", (1, 1, MH, MV, MQ)), ("n_p", (1, 1, MH, MQ)), ("m_p", (1, 1, MH)),
         ("conv_p", (1, 1, 3, D)),
         ("k_s", (1, B, 1, AH, DH)), ("v_s", (1, B, 1, AH, DH)),
         ("C_s", (1, B, MH, MV, MQ)), ("n_s", (1, B, MH, MQ)), ("m_s", (1, B, MH)),
         ("conv_s", (1, B, 3, D))]


def kernel(**inputs):
    import numpy as np
    import concourse.bacc as bacc
    from concourse.bass_utils import run_bass_kernel_spmd

    nc = bacc.Bacc("TRN2", target_bir_lowering=False, num_devices=1)
    arrays, ins, outs = {}, {}, {}
    for name in _INS:
        a = np.ascontiguousarray(inputs[name])
        arrays["in_" + name] = a
        ins[name] = nc.dram_tensor("in_" + name, a.shape, mybir.dt.from_np(a.dtype), kind="ExternalInput").ap()
    for name, shape in _OUTS:
        outs[name] = nc.dram_tensor("out_" + name, shape, F32, kind="ExternalOutput").ap()
    decoder_step(nc, ins, outs)
    r = run_bass_kernel_spmd(nc, [arrays], core_ids=[0])
    return tuple(r.results[0]["out_" + name] for name, _ in _OUTS)
```
